# Optimizing a Trainium2 kernel written in Bass

```python
import jax, jax.numpy as jnp
from jax import lax
import numpy as np

D_MODEL = 1024
BATCH = 1
SEQ = 512
DEPTH = 1

CHUNK = 64
N_LEFT_CHUNKS = 8
BAND = (N_LEFT_CHUNKS + 1) * CHUNK
A_HEADS = 8
A_HEAD_DIM = 64
A_WIDTH = A_HEADS * A_HEAD_DIM
REL_CLIP = 256
B_HEADS = 8
B_HEAD_DIM = 64
B_WIDTH = B_HEADS * B_HEAD_DIM
IDX_HEADS = 8
IDX_DIM = 32
TOPK_MAX = 256
Q_BLOCK = 128
ROPE_THETA = 500000.0
ROT_DIM_B = B_HEAD_DIM // 4
ROT_DIM_IDX = IDX_DIM // 4
EPS = 1e-6
NEG = -1e30

SPLIT_SIZES = (
    A_WIDTH, A_WIDTH, A_WIDTH, A_WIDTH,
    B_WIDTH, B_HEAD_DIM, B_HEAD_DIM, B_WIDTH,
    IDX_HEADS * IDX_DIM, IDX_DIM, IDX_HEADS,
    D_MODEL, D_MODEL,
)
IN_WIDTH = sum(SPLIT_SIZES)


def rms_norm(x, g):
    xf = x.astype(jnp.float32)
    y = xf * lax.rsqrt(jnp.mean(xf * xf, axis=-1, keepdims=True) + EPS)
    return (y * g.astype(jnp.float32)).astype(x.dtype)

def partial_rope(x, rot_dim):
    S = x.shape[1]
    half = rot_dim // 2
    inv = ROPE_THETA ** (-jnp.arange(half, dtype=jnp.float32) / half)
    ang = jnp.arange(S, dtype=jnp.float32)[:, None] * inv[None, :]
    cos = jnp.cos(ang)[None, :, None, :].astype(x.dtype)
    sin = jnp.sin(ang)[None, :, None, :].astype(x.dtype)
    x1, x2, xp = x[..., :half], x[..., half:rot_dim], x[..., rot_dim:]
    return jnp.concatenate([x1 * cos - x2 * sin, x2 * cos + x1 * sin, xp], axis=-1)

def chunked_relpos_attention(q, k, v, rel_bias):
    B, S, H, d = q.shape
    n_chunks = S // CHUNK
    pad = N_LEFT_CHUNKS * CHUNK
    k_pad = jnp.pad(k, ((0, 0), (pad, 0), (0, 0), (0, 0)))
    v_pad = jnp.pad(v, ((0, 0), (pad, 0), (0, 0), (0, 0)))
    i = jnp.arange(CHUNK)[:, None]
    j = jnp.arange(BAND)[None, :]
    dist = pad + i - j
    bias = rel_bias.astype(jnp.float32)[:, jnp.clip(dist, -REL_CLIP, REL_CLIP) + REL_CLIP]
    scale = d ** -0.5

    def one_chunk(c):
        start = c * CHUNK
        qc = lax.dynamic_slice_in_dim(q, start, CHUNK, axis=1)
        kc = lax.dynamic_slice_in_dim(k_pad, start, BAND, axis=1)
        vc = lax.dynamic_slice_in_dim(v_pad, start, BAND, axis=1)
        s = jnp.einsum('bqhd,bkhd->bhqk', qc, kc).astype(jnp.float32) * scale + bias[None]
        valid = (start - pad + j) >= 0
        s = jnp.where(valid[None, None], s, NEG)
        p = jax.nn.softmax(s, axis=-1).astype(v.dtype)
        return jnp.einsum('bhqk,bkhd->bqhd', p, vc)

    out = lax.map(one_chunk, jnp.arange(n_chunks))
    return out.transpose(1, 0, 2, 3, 4).reshape(B, S, H * d)

def dsa_sparse_attention(q, k, v, iq, ik, iw):
    B, S, H, d = q.shape
    top_k = min(TOPK_MAX, S // 4)
    n_blocks = S // Q_BLOCK
    key_chunk = jnp.arange(S) // CHUNK
    scale = d ** -0.5
    gather = jax.vmap(lambda a, idx: a[idx])

    def one_block(blk):
        start = blk * Q_BLOCK
        qb = lax.dynamic_slice_in_dim(q, start, Q_BLOCK, axis=1)
        iqb = lax.dynamic_slice_in_dim(iq, start, Q_BLOCK, axis=1)
        iwb = lax.dynamic_slice_in_dim(iw, start, Q_BLOCK, axis=1)
        q_chunk = (start + jnp.arange(Q_BLOCK)) // CHUNK
        logits = jax.nn.relu(jnp.einsum('bqhd,bsd->bqhs', iqb, ik))
        score = jnp.einsum('bqhs,bqh->bqs', logits, iwb).astype(jnp.float32)
        adm = key_chunk[None, :] <= q_chunk[:, None]
        score = jnp.where(adm[None], score, -jnp.inf)
        _, idx = lax.top_k(score, top_k)
        sel_valid = (idx // CHUNK) <= q_chunk[None, :, None]
        ks = gather(k, idx)
        vs = gather(v, idx)
        s = jnp.einsum('bqhd,bqkd->bqhk', qb, ks).astype(jnp.float32) * scale
        s = jnp.where(sel_valid[:, :, None, :], s, NEG)
        p = jax.nn.softmax(s, axis=-1).astype(v.dtype)
        return jnp.einsum('bqhk,bqkd->bqhd', p, vs)

    out = lax.map(one_block, jnp.arange(n_blocks))
    return out.transpose(1, 0, 2, 3, 4).reshape(B, S, H * d)

def first_inputs(seed: int = 0) -> dict:
    key = jax.random.key(seed)
    ks = jax.random.split(key, 10)
    nrm = jax.random.normal
    return {
        "x": nrm(ks[0], (BATCH, SEQ, D_MODEL), jnp.float32),
        "norm_gain": 1.0 + 0.05 * nrm(ks[1], (DEPTH, D_MODEL), jnp.float32),
        "w_in": nrm(ks[2], (DEPTH, D_MODEL, IN_WIDTH), jnp.float32) * D_MODEL ** -0.5,
        "b_merge": 0.05 * nrm(ks[3], (DEPTH, 2, D_MODEL), jnp.float32),
        "rel_bias": 0.2 * nrm(ks[4], (DEPTH, A_HEADS, 2 * REL_CLIP + 1), jnp.float32),
        "w_branch_a": nrm(ks[5], (DEPTH, A_WIDTH, D_MODEL), jnp.float32) * A_WIDTH ** -0.5,
        "w_branch_b": nrm(ks[6], (DEPTH, B_WIDTH, D_MODEL), jnp.float32) * B_WIDTH ** -0.5,
        "w_out": nrm(ks[7], (DEPTH, D_MODEL, D_MODEL), jnp.float32) * D_MODEL ** -0.5,
        "final_norm_gain": 1.0 + 0.05 * nrm(ks[8], (D_MODEL,), jnp.float32),
    }

def first_block(x, norm_gain, w_in, b_merge, rel_bias, w_branch_a, w_branch_b, w_out, final_norm_gain):
    B, S, _ = x.shape
    offsets = [int(o) for o in np.cumsum(SPLIT_SIZES)[:-1]]
    h = x
    for layer in range(DEPTH):
        xn = rms_norm(h, norm_gain[layer])
        proj = xn @ w_in[layer]
        qa, ka, va, ga, qb, kb, vb, gb, iq, ik, iw, za, zb = jnp.split(proj, offsets, axis=-1)
        qa = qa.reshape(B, S, A_HEADS, A_HEAD_DIM)
        ka = ka.reshape(B, S, A_HEADS, A_HEAD_DIM)
        va = va.reshape(B, S, A_HEADS, A_HEAD_DIM)
        ya = chunked_relpos_attention(qa, ka, va, rel_bias[layer]) * jax.nn.silu(ga)
        qb = partial_rope(qb.reshape(B, S, B_HEADS, B_HEAD_DIM), ROT_DIM_B)
        kb = partial_rope(kb[:, :, None, :], ROT_DIM_B)[:, :, 0]
        iq = partial_rope(iq.reshape(B, S, IDX_HEADS, IDX_DIM), ROT_DIM_IDX)
        ik = partial_rope(ik[:, :, None, :], ROT_DIM_IDX)[:, :, 0]
        iw = iw * (IDX_HEADS ** -0.5 * IDX_DIM ** -0.5)
        yb = dsa_sparse_attention(qb, kb, vb, iq, ik, iw) * jax.nn.silu(gb)
        gate_a = jax.nn.sigmoid(za + b_merge[layer, 0])
        gate_b = jax.nn.sigmoid(zb + b_merge[layer, 1])
        merged = gate_a * (ya @ w_branch_a[layer]) + gate_b * (yb @ w_branch_b[layer])
        h = h + merged @ w_out[layer]
    return rms_norm(h, final_norm_gain)


DEPTH_2 = 2

N_MIXERS = 2
N_A_LAYERS = (DEPTH_2 + 1) // 2
N_B_LAYERS = DEPTH_2 // 2

HG_HEADS = 6
HG_KDIM = 128
HG_VDIM = 128
HG_CHUNK = 64
HG_F = HG_HEADS * HG_KDIM
HG_V = HG_HEADS * HG_VDIM

MLA_HEADS = 6
MLA_Q_LORA = 384
MLA_KV_LORA = 256
MLA_NOPE = 128
MLA_ROPE = 64
MLA_QK = MLA_NOPE + MLA_ROPE
MLA_VDIM = 128
ROPE_THETA_2 = 10000.0

MEM_LEN = 256
MEM_HEADS = 4
MEM_HDIM = 64
MEM_W = MEM_HEADS * MEM_HDIM

MIX_W = 768
OUT_W = MIX_W + MEM_W
HG_IN_W = 2 * HG_F + 2 * HG_V + MEM_W
MLA_IN_W = MLA_Q_LORA + MLA_KV_LORA + MLA_ROPE + MEM_W

D_FF = 2816
CONV_W = 3


def rms_norm_2(x, g):
    xf = x.astype(jnp.float32)
    y = xf * lax.rsqrt(jnp.mean(xf * xf, axis=-1, keepdims=True) + EPS)
    return (y * g.astype(jnp.float32)).astype(x.dtype)

def rope_tables(positions):
    half = MLA_ROPE // 2
    inv = ROPE_THETA_2 ** (-jnp.arange(half, dtype=jnp.float32) / half)
    ang = positions.astype(jnp.float32)[..., None] * inv
    return jnp.cos(ang)[:, :, None, :], jnp.sin(ang)[:, :, None, :]

def apply_rope(x, cos, sin):
    half = MLA_ROPE // 2
    xf = x.astype(jnp.float32)
    x1, x2 = xf[..., :half], xf[..., half:]
    return jnp.concatenate([x1 * cos - x2 * sin, x1 * sin + x2 * cos], axis=-1).astype(x.dtype)

def hgrn2_mixer(z, lb, onorm_g):
    B, S, _ = z.shape
    C = HG_CHUNK
    N = S // C
    q, f, i, g = jnp.split(z, [HG_F, 2 * HG_F, 2 * HG_F + HG_V], axis=-1)
    q = jax.nn.silu(q.astype(jnp.float32)) * (HG_KDIM ** -0.5)
    fg = lb + (1.0 - lb) * jax.nn.sigmoid(f.astype(jnp.float32))
    k = 1.0 - fg
    logf = jnp.log(fg)
    v = i.astype(jnp.float32)

    def to_chunks(t, d):
        return t.reshape(B, N, C, HG_HEADS, d).transpose(1, 0, 3, 2, 4)

    qc, kc, lc = to_chunks(q, HG_KDIM), to_chunks(k, HG_KDIM), to_chunks(logf, HG_KDIM)
    vc = to_chunks(v, HG_VDIM)
    causal = jnp.tril(jnp.ones((C, C), dtype=bool))[:, :, None]

    def step(state, xs):
        q_, k_, v_, lf = xs
        b = jnp.cumsum(lf, axis=2)
        o_inter = jnp.einsum('bhtk,bhkv->bhtv', q_ * jnp.exp(b), state)
        diff = b[:, :, :, None, :] - b[:, :, None, :, :]
        decay = jnp.exp(jnp.where(causal, diff, -jnp.inf))
        attn = jnp.einsum('bhtk,bhtsk,bhsk->bhts', q_, decay, k_)
        o = o_inter + jnp.einsum('bhts,bhsv->bhtv', attn, v_)
        b_last = b[:, :, -1, :]
        state = state * jnp.exp(b_last)[..., None] + jnp.einsum(
            'bhsk,bhsv->bhkv', k_ * jnp.exp(b_last[:, :, None, :] - b), v_)
        return state, o

    s0 = jnp.zeros((B, HG_HEADS, HG_KDIM, HG_VDIM), jnp.float32)
    _, o = lax.scan(step, s0, (qc, kc, vc, lc))
    o = o.transpose(1, 0, 3, 2, 4).reshape(B, S, HG_HEADS, HG_VDIM)
    gate = g.astype(jnp.float32).reshape(B, S, HG_HEADS, HG_VDIM)
    o = rms_norm_2(o, onorm_g) * jax.nn.silu(gate)
    return o.reshape(B, S, HG_V).astype(z.dtype)

def causal_block_attention(q, k, v):
    B, S, H, Dq = q.shape
    nb = S // Q_BLOCK
    scale = Dq ** -0.5
    qb = q.reshape(B, nb, Q_BLOCK, H, Dq).transpose(1, 0, 2, 3, 4)
    kpos = jnp.arange(S)

    def one_block(args):
        qi, idx = args
        s = jnp.einsum('bqhd,bkhd->bhqk', qi, k).astype(jnp.float32) * scale
        qpos = idx * Q_BLOCK + jnp.arange(Q_BLOCK)
        s = jnp.where(kpos[None, :] <= qpos[:, None], s, -jnp.inf)
        p = jax.nn.softmax(s, axis=-1)
        return jnp.einsum('bhqk,bkhd->bqhd', p.astype(v.dtype), v)

    out = lax.map(one_block, (qb, jnp.arange(nb)))
    return out.transpose(1, 0, 2, 3, 4).reshape(B, S, H, v.shape[-1])

def mla_mixer(z, cos, sin, qa_g, kva_g, w_uq, w_ukv, qn_g, kn_g):
    B, S, _ = z.shape
    cq, ckv, kpe = jnp.split(z, [MLA_Q_LORA, MLA_Q_LORA + MLA_KV_LORA], axis=-1)
    q = (rms_norm_2(cq, qa_g) @ w_uq).reshape(B, S, MLA_HEADS, MLA_QK)
    kv = (rms_norm_2(ckv, kva_g) @ w_ukv).reshape(B, S, MLA_HEADS, MLA_NOPE + MLA_VDIM)
    k_nope, v = kv[..., :MLA_NOPE], kv[..., MLA_NOPE:]
    k_rope = jnp.broadcast_to(kpe[:, :, None, :], (B, S, MLA_HEADS, MLA_ROPE))
    k = jnp.concatenate([k_nope, k_rope], axis=-1)
    q = rms_norm_2(q, qn_g)
    k = rms_norm_2(k, kn_g)
    q = jnp.concatenate([q[..., :MLA_NOPE], apply_rope(q[..., MLA_NOPE:], cos, sin)], axis=-1)
    k = jnp.concatenate([k[..., :MLA_NOPE], apply_rope(k[..., MLA_NOPE:], cos, sin)], axis=-1)
    o = causal_block_attention(q, k, v)
    return o.reshape(B, S, MLA_HEADS * MLA_VDIM)

def memory_attention(qm, mem_n, w_mem_kv, qn_g, kn_g):
    B, S, _ = qm.shape
    M = mem_n.shape[1]
    kv = mem_n @ w_mem_kv
    q = rms_norm_2(qm.reshape(B, S, MEM_HEADS, MEM_HDIM), qn_g)
    k = rms_norm_2(kv[..., :MEM_W].reshape(B, M, MEM_HEADS, MEM_HDIM), kn_g)
    v = kv[..., MEM_W:].reshape(B, M, MEM_HEADS, MEM_HDIM)
    s = jnp.einsum('bshd,bmhd->bhsm', q, k).astype(jnp.float32) * (MEM_HDIM ** -0.5)
    p = jax.nn.softmax(s, axis=-1)
    o = jnp.einsum('bhsm,bmhd->bshd', p.astype(v.dtype), v)
    return o.reshape(B, S, MEM_W)

def conv_ffn(h, w_up, conv_w, conv_b, w_down):
    u = h @ w_up
    u = lax.conv_general_dilated(
        u, conv_w[:, None, :].astype(u.dtype), window_strides=(1,),
        padding=[(CONV_W - 1, 0)], dimension_numbers=('NWC', 'WIO', 'NWC'),
        feature_group_count=u.shape[-1]) + conv_b
    a, b = u[..., :D_FF], u[..., D_FF:]
    return (jax.nn.silu(a) * b) @ w_down

def second_inputs(seed: int = 0) -> dict:
    key = jax.random.key(seed)
    ks = jax.random.split(key, 32)
    nrm = lambda k, shape, scale: jax.random.normal(k, shape, jnp.float32) * scale
    gain = lambda k, shape: 1.0 + 0.02 * jax.random.normal(k, shape, jnp.float32)
    offs = jax.random.randint(ks[2], (BATCH, 1), 0, 1024, dtype=jnp.int32)
    positions = offs + jnp.arange(SEQ, dtype=jnp.int32)[None, :]
    return {
        "x": nrm(ks[0], (BATCH, SEQ, D_MODEL), 1.0),
        "mem": nrm(ks[1], (BATCH, MEM_LEN, D_MODEL), 1.0),
        "positions": positions,
        "mix_norm_g": gain(ks[3], (DEPTH_2, D_MODEL)),
        "ffn_norm_g": gain(ks[4], (DEPTH_2, D_MODEL)),
        "mem_norm_g": gain(ks[5], (DEPTH_2, D_MODEL)),
        "w_mem_kv": nrm(ks[6], (DEPTH_2, D_MODEL, 2 * MEM_W), D_MODEL ** -0.5),
        "mem_q_norm_g": gain(ks[7], (DEPTH_2, MEM_HDIM)),
        "mem_k_norm_g": gain(ks[8], (DEPTH_2, MEM_HDIM)),
        "w_out": nrm(ks[9], (DEPTH_2, OUT_W, D_MODEL), OUT_W ** -0.5),
        "w_up": nrm(ks[10], (DEPTH_2, D_MODEL, 2 * D_FF), D_MODEL ** -0.5),
        "conv_w": nrm(ks[11], (DEPTH_2, CONV_W, 2 * D_FF), CONV_W ** -0.5),
        "conv_b": nrm(ks[12], (DEPTH_2, 2 * D_FF), 0.02),
        "w_down": nrm(ks[13], (DEPTH_2, D_FF, D_MODEL), D_FF ** -0.5),
        "hg_w_in": nrm(ks[14], (N_A_LAYERS, D_MODEL, HG_IN_W), D_MODEL ** -0.5),
        "hg_lb_logits": nrm(ks[15], (DEPTH_2 + 1, HG_F), 0.5),
        "hg_out_norm_g": gain(ks[16], (N_A_LAYERS, HG_VDIM)),
        "mla_w_in": nrm(ks[17], (N_B_LAYERS, D_MODEL, MLA_IN_W), D_MODEL ** -0.5),
        "mla_qa_norm_g": gain(ks[18], (N_B_LAYERS, MLA_Q_LORA)),
        "mla_kva_norm_g": gain(ks[19], (N_B_LAYERS, MLA_KV_LORA)),
        "mla_w_uq": nrm(ks[20], (N_B_LAYERS, MLA_Q_LORA, MLA_HEADS * MLA_QK), MLA_Q_LORA ** -0.5),
        "mla_w_ukv": nrm(ks[21], (N_B_LAYERS, MLA_KV_LORA, MLA_HEADS * (MLA_NOPE + MLA_VDIM)), MLA_KV_LORA ** -0.5),
        "mla_q_norm_g": gain(ks[22], (N_B_LAYERS, MLA_QK)),
        "mla_k_norm_g": gain(ks[23], (N_B_LAYERS, MLA_QK)),
    }

def second_block(x, mem, positions, mix_norm_g, ffn_norm_g, mem_norm_g, w_mem_kv,
              mem_q_norm_g, mem_k_norm_g, w_out, w_up, conv_w, conv_b, w_down,
              hg_w_in, hg_lb_logits, hg_out_norm_g, mla_w_in, mla_qa_norm_g,
              mla_kva_norm_g, mla_w_uq, mla_w_ukv, mla_q_norm_g, mla_k_norm_g):
    cos, sin = rope_tables(positions)
    lower_bounds = jnp.cumsum(jax.nn.softmax(hg_lb_logits.astype(jnp.float32), axis=0), axis=0)
    for layer in range(DEPTH_2):
        h = rms_norm_2(x, mix_norm_g[layer])
        j = layer // N_MIXERS
        if layer % N_MIXERS == 0:
            z = h @ hg_w_in[j]
            y = hgrn2_mixer(z[..., :-MEM_W], lower_bounds[layer], hg_out_norm_g[j])
        else:
            z = h @ mla_w_in[j]
            y = mla_mixer(z[..., :-MEM_W], cos, sin, mla_qa_norm_g[j], mla_kva_norm_g[j],
                          mla_w_uq[j], mla_w_ukv[j], mla_q_norm_g[j], mla_k_norm_g[j])
        m = memory_attention(z[..., -MEM_W:], rms_norm_2(mem, mem_norm_g[layer]), w_mem_kv[layer],
                             mem_q_norm_g[layer], mem_k_norm_g[layer])
        x = x + jnp.concatenate([y, m], axis=-1) @ w_out[layer]
        x = x + conv_ffn(rms_norm_2(x, ffn_norm_g[layer]), w_up[layer], conv_w[layer],
                         conv_b[layer], w_down[layer])
    return x


def setup_inputs(seed=0):
    out = dict(first_inputs(seed))
    for name, value in second_inputs(seed + 1).items():
        if name != "x":
            out[name + "_2"] = value
    return out


def reference(
    x, norm_gain, w_in, b_merge, rel_bias, w_branch_a, w_branch_b, w_out, final_norm_gain,
    mem_2, positions_2, mix_norm_g_2, ffn_norm_g_2, mem_norm_g_2, w_mem_kv_2, mem_q_norm_g_2,
    mem_k_norm_g_2, w_out_2, w_up_2, conv_w_2, conv_b_2, w_down_2, hg_w_in_2, hg_lb_logits_2,
    hg_out_norm_g_2, mla_w_in_2, mla_qa_norm_g_2, mla_kva_norm_g_2, mla_w_uq_2, mla_w_ukv_2,
    mla_q_norm_g_2, mla_k_norm_g_2,
):
    x = first_block(
        x, norm_gain, w_in, b_merge, rel_bias, w_branch_a, w_branch_b, w_out, final_norm_gain,
    )
    return second_block(
        x, mem_2, positions_2, mix_norm_g_2, ffn_norm_g_2, mem_norm_g_2, w_mem_kv_2,
        mem_q_norm_g_2, mem_k_norm_g_2, w_out_2, w_up_2, conv_w_2, conv_b_2, w_down_2,
        hg_w_in_2, hg_lb_logits_2, hg_out_norm_g_2, mla_w_in_2, mla_qa_norm_g_2,
        mla_kva_norm_g_2, mla_w_uq_2, mla_w_ukv_2, mla_q_norm_g_2, mla_k_norm_g_2,
    )


_drawn_inputs = setup_inputs


def setup_inputs(seed=0):
    import zlib

    import numpy as np

    out = dict(_drawn_inputs(seed))
    spreads = {}
    factors = {'norm_gain': 3.452,
     'b_merge': 8.0,
     'rel_bias': 5.569,
     'mix_norm_g_2': 3.402,
     'ffn_norm_g_2': 2.84,
     'mem_norm_g_2': 8.0,
     'mem_q_norm_g_2': 8.0,
     'mem_k_norm_g_2': 8.0,
     'conv_b_2': 2.913,
     'hg_lb_logits_2': 2.902,
     'hg_out_norm_g_2': 4.622,
     'mla_qa_norm_g_2': 8.0,
     'mla_kva_norm_g_2': 8.0,
     'mla_q_norm_g_2': 8.0,
     'mla_k_norm_g_2': 8.0}
    for name, (base, spread) in spreads.items():
        noise = np.random.default_rng([zlib.crc32(name.encode()), seed]).standard_normal(out[name].shape)
        drawn = base * np.exp(spread * noise) if base else spread * noise
        out[name] = __import__('jax').numpy.asarray(drawn.astype(out[name].dtype))
    for name, factor in factors.items():
        out[name] = (out[name] * factor).astype(out[name].dtype)
    return out
```

```python
from contextlib import ExitStack

import numpy as np

import concourse.bass as bass
from concourse import mybir

F32 = mybir.dt.float32
F32R = mybir.dt.float32r
I32 = mybir.dt.int32
I8 = mybir.dt.int8
ALU = mybir.AluOpType
ACT = mybir.ActivationFunctionType

P = 128
TOK = 512
NT = TOK // P
D = 1024
KD = D // P
CHUNK = 64
EPS = 1e-6
NEG = -1e30
TAKEN = -3e38
BARRED = -1e38
TOPK = 128
DH = 64
NHEAD = 8
IDXH = 8
IDXD = 32
MEM = 256
HG = 6
LEVELS = [64, 32, 16, 8, 4, 2, 1]
MLH = 6
FF = 22
RING = 4
SPLIT = 2
SLAB = 1024

COLS = {}


def _col(name, n):
    COLS[name] = (sum(c for _, c in COLS.values()), n)


for _name, _n in (("norm_gain", KD), ("final_gain", KD), ("mix0", KD), ("mix1", KD), ("ffn0", KD),
                  ("ffn1", KD), ("mem0", KD), ("mem1", KD), ("bm0", KD), ("bm1", KD), ("mq0", 1),
                  ("mq1", 1), ("mk0", 1), ("mk1", 1), ("lb", 3 * HG), ("onorm", 1), ("qa", 3),
                  ("kva", 2), ("qn", 2), ("kn", 2), ("inv", 1), ("eps", 3)):
    _col(_name, _n)
NCOL = sum(c for _, c in COLS.values())


class Job:

    def __init__(self, slabs, banks, kts, empties):
        self.slabs, self.banks, self.kts, self.empties = slabs, banks, kts, empties
        self.done = slabs[-1] + 1


def plan_stream():
    jobs, emptied, n, u = {}, [], 0, 0
    count = {"act": 0, "dve": 0}

    def add(name, nslab, nbank, kts, who):
        nonlocal n, u
        jobs[name] = Job(list(range(n, n + nslab)), list(range(u, u + nbank)), kts, who)
        n += nslab
        u += nbank
        for _ in range(nbank):
            count[who] += 1
            emptied.append((who, count[who]))

    add("vbiw", 1, NT, KD, "act")
    for k in ("iq0", "iq1", "ik", "kb"):
        add(k, 1, 1, KD, "act")
    for k in range(4):
        add(f"qa{k}", 1, 1, KD, "act")
    for k in range(4):
        add(f"ka{k}", 1, 1, KD, "act")
    add("va", 4, NT, KD, "act")
    for g in ("qb", "ga", "gb"):
        for k in range(4):
            add(f"{g}{k}", 1, 1, KD, "act")
    for k in range(KD):
        add(f"za{k}", 1, 1, KD, "act")
    for k in range(KD):
        add(f"zb{k}", 1, 1, KD, "act")
        add(f"pab{k}", 1, 2, 4, "dve")
    for k in range(KD):
        add(f"o1_{k}", 1, 1, KD, "dve")
    for l in range(2):
        for k in range(2):
            add(f"mk{l}{k}", 1, 1, KD, "act")
        add(f"mv{l}", 2, 2, KD, "act")
    for k in range(HG):
        add(f"hf{k}", 1, 1, KD, "act")
    for k in range(HG):
        add(f"hq{k}", 1, 1, KD, "act")
    for k in range(2):
        add(f"hv{k}", 4, NT, KD, "act")
    for k in range(2):
        add(f"qm0{k}", 1, 1, KD, "act")
    for k in range(HG):
        add(f"hg{k}", 1, 1, KD, "act")

    def ffn(l):
        for k in range(KD):
            add(f"wo{l}{k}", 1, 1, KD, "dve")
        for k in range(FF):
            add(f"ua{l}_{k}", 1, 1, KD, "dve")
            add(f"ub{l}_{k}", 1, 1, KD, "dve")
        for k in range(KD):
            add(f"dn{l}{k}", 3, 1, FF, "dve")

    ffn(0)
    for k in range(3):
        add(f"cq{k}", 1, 1, KD, "act")
    for k in range(2):
        add(f"ckv{k}", 1, 1, KD, "act")
    add("kpe", 1, 1, KD, "act")
    for k in range(2):
        add(f"qm1{k}", 1, 1, KD, "act")
    for k in range(3):
        add(f"uqn{k}", 1, 2, 3, "act")
    add("uqr0", 1, 2, 3, "act")
    add("uqr1", 1, 1, 3, "act")
    add("ukn0", 1, 4, 2, "act")
    add("ukn1", 1, 2, 2, "act")
    for k in range(2):
        add(f"uv{k}", 1, NT, 2, "act")
    ffn(1)
    return jobs, emptied, n


JOBS, EMPTIED, NSLAB = plan_stream()
NSLAB = -(-(NSLAB + SPLIT) // RING) * RING

SUMS = {0: 0, 1: KD, 2: 2 * KD, 3: 2 * KD + 1, 4: 3 * KD + 1, 5: 3 * KD + 2, 6: 3 * KD + 3}
XLB = {0: 0, 1: KD, 3: 3 * KD, 4: 4 * KD, 5: 5 * KD, 6: 6 * KD}


def plan_heads():
    plan, idx = {}, 0
    for names, parts in (([f"mk{l}{k}" for l in range(2) for k in range(2)], 1),
                         (["qm00", "qm01"], 1), ([f"ho{h}" for h in range(HG)], 1), (["cq"], 3), (["ckv"], 2),
                         (["qm10", "qm11"], 1), ([f"qn{h}" for h in range(MLH)], 2),
                         ([f"kn{h}" for h in range(MLH)], 2)):
        for name in names:
            plan[name] = (len(plan), list(range(idx, idx + parts)))
            idx += parts
    return plan


HEADS = plan_heads()
XTB = XLB

_t1 = 6.28125
_t2 = float(np.round((2 * np.pi - _t1) * 2 ** 20) / 2 ** 20)
TURN = (_t1, _t2, float(2 * np.pi - _t1 - _t2))
HALFTURN = 3.1415925
ROUND = 12582912.0


def build(nc, stream, xt_in, memt_in, pars, convp, consts, rope_tabs, toep, masks8, resets, cz_in, pos_in, out):
    with ExitStack() as ctx:
        BASE = 16512
        KB = 1024

        def at(name, shape, kb, dt=F32):
            return nc.alloc_sbuf_tensor_at(name, shape, dt, offset=BASE + int(kb * KB))

        def bank(name):
            return ctx.enter_context(nc.psum_tensor(name, [P, TOK], F32))

        def sem(name):
            return ctx.enter_context(nc.semaphore(name))

        X = at("X", [P, KD, TOK], 0)
        XH = at("XH", [P, KD, TOK], 16, F32R)
        XL = at("XL", [P, KD, TOK], 32, F32R)
        RAW = at("RAW", [P, RING, SLAB], 48)
        WH = at("WH", [P, SPLIT, SLAB], 64, F32R)
        WL = at("WL", [P, SPLIT, SLAB], 72, F32R)
        CONST = at("CONST", [P, 7, P], 80)
        IDENT, ONES, BONES, ROTB, ROTI, ROTM, CHB = (CONST[:, i, :] for i in range(7))
        CZ = at("CZ", [P, TOK], 84)
        PAR = at("PAR", [P, NCOL], 86)
        LBC = at("LBC", [P, 6 * HG], 87)
        CW = at("CW", [P, 2, FF, 8], 88)
        SB = at("SB", [P, 2, TOK], 90)
        PB = at("PB", [P, 3, TOK], 94)
        PT = at("PT", [P, 2, TOK], 100)
        SQ = at("SQ", [P, 2, TOK], 104)
        RS = at("RS", [P, TOK], 108)
        TMP = at("TMP", [P, 2, TOK], 110)
        ST = at("ST", [P, 32], 114)
        MX8 = at("MX8", [P, 8], 114.75)
        A0 = 115
        QA = at("QA", [P, 4, TOK], A0 + 0)
        KA = at("KA", [P, 4, TOK], A0 + 8)
        VA = at("VA", [P, NT, 512], A0 + 16)
        QB = at("QB", [P, 4, TOK], A0 + 24)
        GA = at("GA", [P, 4, TOK], A0 + 32)
        GB = at("GB", [P, 4, TOK], A0 + 40)
        TP = at("TP", [P, 2, 2, TOK], A0 + 48)
        IQ = at("IQ", [P, 2, TOK], A0 + 48)
        IK = at("IK", [P, TOK], A0 + 52)
        COSI = at("COSI", [P, TOK], A0 + 54)
        SINI = at("SINI", [P, TOK], A0 + 56)
        KBT = at("KBT", [P, TOK], A0 + 58)
        COSB = at("COSB", [P, TOK], A0 + 60)
        SINB = at("SINB", [P, TOK], A0 + 62)
        VB = at("VB", [P, NT, DH], A0 + 64)
        IW = at("IW", [P, NT, IDXH], A0 + 65)
        MB = at("MB", [P, 1152], A0 + 66)
        ZA = at("ZA", [P, KD, TOK], A0 + 71)
        YAH = at("YAH", [P, 4, TOK], A0 + 0, F32R)
        YAL = at("YAL", [P, 4, TOK], A0 + 8, F32R)
        YBL = at("YBL", [P, 4, TOK], A0 + 16, F32R)
        YBH = at("YBH", [P, 4, TOK], A0 + 24, F32R)
        MH = at("MH", [P, KD, TOK], A0 + 32, F32R)
        ML = at("ML", [P, KD, TOK], A0 + 48, F32R)
        MRAW = at("MRAW", [P, KD, MEM], A0 + 0)
        MKT = [at(f"MKT{l}", [P, 2, MEM], A0 + 84 + 4 * l) for l in range(2)]
        MVT = [at(f"MVT{l}", [P, 2, MEM], A0 + 86 + 4 * l) for l in range(2)]
        YH = at("YH", [P, KD, TOK], A0 + 0, F32R)
        YL = at("YL", [P, KD, TOK], A0 + 16, F32R)
        HK = at("HK", [P, HG, TOK], A0 + 0)
        HB = at("HB", [P, HG, TOK], A0 + 16)
        HQ = at("HQ", [P, HG, TOK], A0 + 32)
        HV = at("HV", [P, NT, HG * P], A0 + 44)
        HGT = at("HGT", [P, HG, TOK], A0 + 56)
        QM = at("QM", [P, 2, TOK], A0 + 68)
        MSK = at("MSK", [P, 8, P], A0 + 72, I8)
        MSKI = at("MSKI", [P, 8, P], A0 + 76, I32)
        AX = at("AX", [P, 6, P], A0 + 73)
        QX = at("QX", [P, TOK], A0 + 76)
        KX = at("KX", [P, TOK], A0 + 78)
        KX2 = at("KX2", [P, 3, P], A0 + 80)
        RESET = at("RESET", [P, TOK], A0 + 82)
        GH = at("GH", [P, FF, TOK], A0 + 0, F32R)
        GL = at("GL", [P, FF, TOK], A0 + 44, F32R)
        YH1 = at("YH1", [P, KD, TOK], A0 + 0, F32R)
        YL1 = at("YL1", [P, KD, TOK], A0 + 16, F32R)
        QN = at("QN", [P, MLH, TOK], A0 + 0)
        KN = at("KN", [P, MLH, TOK], A0 + 16)
        QR = at("QR", [P, 3, TOK], A0 + 32)
        KR = at("KR", [P, 3, TOK], A0 + 38)
        MV = at("MV", [P, NT, MLH * P], A0 + 44)
        CQH = at("CQH", [P, 3, TOK], A0 + 44, F32R)
        CQL = at("CQL", [P, 3, TOK], A0 + 50, F32R)
        QM1 = at("QM1", [P, 2, TOK], A0 + 56)
        CQ = at("CQ", [P, 3, TOK], A0 + 60)
        CKV = at("CKV", [P, 2, TOK], A0 + 66)
        KPE = at("KPE", [P, TOK], A0 + 70)
        CKH = at("CKH", [P, 2, TOK], A0 + 72, F32R)
        CKL = at("CKL", [P, 2, TOK], A0 + 76, F32R)
        COSM = at("COSM", [P, TOK], A0 + 80)
        SINM = at("SINM", [P, TOK], A0 + 82)
        POSI = at("POSI", [P, TOK], A0 + 84, I32)

        KPR = at("KPR", [P, TOK], A0 + 60)
        HALF = [slice(0, DH), slice(DH, P)]
        RH = [RS[:, :], SB[:, 1, :]]

        DB = [bank(f"DB{i}") for i in range(4)]
        SC = [bank(f"SC{i}") for i in range(2)]
        TB = bank("TB")
        OB = bank("OB")
        RB = [TB, OB]

        def col(name, i=0):
            c = COLS[name][0] + i
            return PAR[:, c:c + 1]

        raw_in = [sem(f"raw_in{i}") for i in range(RING)]
        hi_done = sem("hi_done")
        lo_done = sem("lo_done")
        slab_used = sem("slab_used")
        act_emptied = sem("act_emptied")
        dve_emptied = sem("dve_emptied")
        consts_in = sem("consts_in")
        tabs_in = sem("tabs_in")
        x_in = sem("x_in")
        mem_in = sem("mem_in")
        toep_in = [sem(f"toep_in{i}") for i in range(2)]
        hg_in = sem("hg_in")
        pos_ready = sem("pos_ready")
        sq_done = sem("sq_done")
        ss_done = sem("ss_done")
        std_done = sem("std_done")
        rs_used = sem("rs_used")
        xt_done = sem("xt_done")
        xh_done = sem("xh_done")
        xl_done = sem("xl_done")
        x_new = sem("x_new")
        rot_done = sem("rot_done")
        roped = sem("roped")
        ilog_done = sem("ilog_done")
        irelu_done = sem("irelu_done")
        iacc_done = sem("iacc_done")
        qk_done = sem("qk_done")
        bm_done = sem("bm_done")
        exp_done = sem("exp_done")
        nrm_done = sem("nrm_done")
        tr_done = sem("tr_done")
        pt_done = sem("pt_done")
        pv_done = sem("pv_done")
        o_out = sem("o_out")
        zb_used = sem("zb_used")
        hs_sq = sem("hs_sq")
        hs_ss = sem("hs_ss")
        hs_std = sem("hs_std")
        hs_done = sem("hs_done")
        lb_e = sem("lb_e")
        lb_done = sem("lb_done")
        hf_ln = sem("hf_ln")
        lv_e = sem("lv_e")
        lv_x = sem("lv_x")
        lv_w = sem("lv_w")
        lv_mm = sem("lv_mm")
        lv_cp = sem("lv_cp")
        tb_copied = sem("tb_copied")
        decays_ready = sem("decays_ready")
        ho_mm = sem("ho_mm")
        ho_out = sem("ho_out")
        cv_i = sem("cv_i")
        cv_c = sem("cv_c")
        cv_s = sem("cv_s")
        g_done = sem("g_done")
        ang_done = sem("ang_done")
        sin_done = sem("sin_done")
        sin_neg = sem("sin_neg")
        dve_chain = sem("dve_chain")
        act_chain = sem("act_chain")
        arena_free = sem("arena_free")
        gain_done = sem("gain_done")
        cv_g = sem("cv_g")
        hg_silu = sem("hg_silu")
        reset_ready = sem("reset_ready")
        out_done = sem("out_done")

        def steps_a():
            for p in range(4):
                for i in range(NT):
                    for e in range(2):
                        r = slice(DH * e, DH * e + DH)
                        w = P * (i + 1)
                        h = 2 * p + e
                        yield dict(qk=[(QA[r, p, P * i:P * i + P], KA[r, p, 0:w])], w=w,
                                   bias=TP[:, p % 2, e, TOK - w:TOK],
                                   v=[VA[:, s, DH * h:DH * h + DH] for s in range(i + 1)],
                                   o=OB[r, P * i:P * i + P], first=(i == 0 and e == 0), last=(i == NT - 1 and e == 1),
                                   kind="a", grp=p)

        def steps_b():
            for p in range(4):
                for i in range(NT):
                    for e in range(2):
                        r = slice(DH * e, DH * e + DH)
                        w = P * (i + 1)
                        off = {1: 0, 2: 256, 3: 640}.get(i, 0)
                        yield dict(qk=[(QB[r, p, P * i:P * i + P], KBT[r, 0:w])], w=w,
                                   bias=CHB if i == 0 else MB[:, off:off + w],
                                   v=[VB[:, s, :] for s in range(i + 1)],
                                   o=OB[r, P * i:P * i + P], first=(i == 0 and e == 0), last=(i == NT - 1 and e == 1),
                                   kind="b", grp=p)

        def steps_m(l):
            q = QM if l == 0 else QM1
            for p in range(2):
                for i in range(NT):
                    for e in range(2):
                        r = slice(DH * e, DH * e + DH)
                        h = 2 * p + e
                        yield dict(qk=[(q[r, p, P * i:P * i + P], MKT[l][r, p, :])], w=MEM,
                                   bias=CZ[:, 0:MEM],
                                   v=[MVT[l][:, s, DH * h:DH * h + DH] for s in range(2)],
                                   o=OB[r, P * i:P * i + P], first=(i == 0 and e == 0), last=(i == NT - 1 and e == 1),
                                   kind=f"m{l}", grp=p)

        def steps_l():
            for h in range(MLH):
                r = slice(DH * (h % 2), DH * (h % 2) + DH)
                for i in range(NT):
                    w = P * (i + 1)
                    yield dict(qk=[(QN[:, h, P * i:P * i + P], KN[:, h, 0:w]),
                                   (QR[r, h // 2, P * i:P * i + P], KR[r, h // 2, 0:w])], w=w,
                               bias=CZ[:, TOK - w:TOK],
                               v=[MV[:, s, P * h:P * h + P] for s in range(i + 1)],
                               o=OB[:, P * i:P * i + P], first=(i == 0), last=(i == NT - 1),
                               kind="l", grp=h)

        segments, g, grp = {}, 0, 0
        for name, it in (("ab", list(steps_a()) + list(steps_b())), ("m0", list(steps_m(0))),
                         ("l", list(steps_l())), ("m1", list(steps_m(1)))):
            for s in it:
                s["g"], s["group"] = g, grp
                g += 1
                grp += s["last"]
            segments[name] = it

        block = ctx.enter_context(nc.Block())

        @block.sync
        def _(sp):
            for j in range(RING):
                sp.dma_start(RAW[:, j, :], stream[j]).then_inc(raw_in[j], 16)
            with sp.Fori(1, NSLAB // RING) as it:
                for j in range(RING):
                    sp.wait_ge(lo_done, it * RING + (j - RING + 1))
                    sp.dma_start(RAW[:, j, :], stream[bass.ds(it * RING + j, 1)].rearrange("o p n -> (o p) n")
                                 ).then_inc(raw_in[j], 16)
            for m in range(KD):
                sp.wait_ge(dve_emptied, EMPTIED[JOBS[f"dn1{m}"].banks[0]][1])
                sp.dma_start(out[m], X[:, m, :]).then_inc(out_done, 16)
            sp.wait_ge(out_done, 16 * KD)

        @block.gpsimd
        def _(pool):
            def low(j, n):
                s = j % SPLIT
                pool.wait_ge(hi_done, n + 1)
                nc.gpsimd.tensor_tensor(WL[:, s, :], RAW[:, j, :], WH[:, s, :].bitcast(F32),
                                        ALU.subtract).then_inc(lo_done, 1)

            def lows(first, end):
                a, b = -(-first // RING), end // RING
                for n in range(first, a * RING):
                    low(n % RING, n)
                with pool.Fori(a, b) as it:
                    for j in range(RING):
                        low(j, it * RING + j)
                for n in range(b * RING, end):
                    low(n % RING, n)

            s0 = JOBS["qm00"].slabs[0]
            lows(0, s0 + 2)
            slabs = [[], [2, 3], [4, 5], [6], [7], [8]]
            pool.wait_ge(decays_ready, 1)
            for h in range(HG):
                b = HB[:, h, :]
                for l in range(8):
                    e = SB[:, l % 2, :]
                    if l >= 2:
                        pool.wait_ge(lv_w, 10 * h + l - 1)
                    elif h:
                        pool.wait_ge(lv_w, 10 * h - 3 * (l == 0))
                    if l < 7:
                        m = LEVELS[l]
                        bv = b.rearrange("p (n s m) -> p n s m", s=2, m=m)
                        ev = e.rearrange("p (n s m) -> p n s m", s=2, m=m)
                        ref = bv[:, :, 0, m - 1:m].broadcast_to([P, TOK // (2 * m), m])
                        nc.gpsimd.tensor_tensor(ev[:, :, 1, :], bv[:, :, 1, :], ref, ALU.subtract)
                        nc.gpsimd.tensor_tensor(ev[:, :, 0, :], ref, bv[:, :, 0, :], ALU.subtract).then_inc(lv_e, 1)
                    else:
                        bv = b.rearrange("p (n m) -> p n m", m=P)
                        nc.gpsimd.tensor_tensor(e.rearrange("p (n m) -> p n m", m=P),
                                                bv[:, :, P - 1:P].broadcast_to([P, NT, P]), bv, ALU.subtract).then_inc(lv_e, 1)
                    if l == 1:
                        for n in slabs[h]:
                            low((s0 + n) % RING, s0 + n)
            lows(s0 + 9, NSLAB)

        @block.tensor
        def _(pe):
            mm = nc.tensor.matmul

            def wait_empty(u):
                if u >= 4:
                    who, c = EMPTIED[u - 4]
                    pe.wait_ge(act_emptied if who == "act" else dve_emptied, c)

            def feature_job(*args, **kw):
                for _ in feature_tiles(*args, **kw):
                    pass

            def feature_tiles(name, hi, lo, n=TOK, xready=None):
                job = JOBS[name]
                u = job.banks[0]
                wait_empty(u)
                o = DB[u % 4][:, 0:n]
                for k in range(job.kts):
                    sl = job.slabs[k // 8]
                    s, c = sl % SPLIT, slice(P * (k % 8), P * (k % 8) + P)
                    if k % 8 == 0:
                        pe.wait_ge(lo_done, sl + 1)
                    if xready is not None:
                        pe.wait_ge(xl_done, xready + k + 1)
                    mm(o, WH[:, s, c], hi(k), start=(k == 0), stop=False)
                    mm(o, WH[:, s, c], lo(k), start=False, stop=False)
                    last = mm(o, WL[:, s, c], hi(k), start=False, stop=(k == job.kts - 1))
                    if k % 8 == 7 or k == job.kts - 1:
                        last.then_inc(slab_used, 1)
                    yield

            def packed_job(name, operands):
                job = JOBS[name]
                sl = job.slabs[0]
                s = sl % SPLIT
                pe.wait_ge(lo_done, sl + 1)
                for a, (hi, lo) in enumerate(operands):
                    wait_empty(job.banks[a])
                    o = DB[job.banks[a] % 4][:, :]
                    for k in range(job.kts):
                        i = a * job.kts + k
                        c = slice(P * i, P * i + P)
                        mm(o, WH[:, s, c], hi(k), start=(k == 0), stop=False)
                        mm(o, WH[:, s, c], lo(k), start=False, stop=False)
                        last = mm(o, WL[:, s, c], hi(k), start=False, stop=(k == job.kts - 1))
                last.then_inc(slab_used, 1)

            def token_job(name, hi, lo, n, tiles=NT, xready=None):
                job = JOBS[name]
                per = job.kts // len(job.slabs)
                for j, sl in enumerate(job.slabs):
                    pe.wait_ge(lo_done, sl + 1)
                    s = sl % SPLIT
                    for kk in range(per):
                        k = j * per + kk
                        if xready is not None:
                            pe.wait_ge(xl_done, xready + k + 1)
                        for t in range(tiles):
                            if k == 0:
                                wait_empty(job.banks[t])
                            o = DB[job.banks[t] % 4][:, 0:n]
                            c, ts = slice(n * kk, n * kk + n), slice(P * t, P * t + P)
                            mm(o, hi(k)[:, ts], WH[:, s, c], start=(k == 0), stop=False)
                            mm(o, lo(k)[:, ts], WH[:, s, c], start=False, stop=False)
                            last = mm(o, hi(k)[:, ts], WL[:, s, c], start=False, stop=(k == job.kts - 1))
                    last.then_inc(slab_used, 1)

            def xh(k):
                return XH[:, k, :]

            def xl(k):
                return XL[:, k, :]

            def norm_sum(q, n=TOK):
                if q in (2, 4, 5, 6):
                    pe.wait_ge(sq_done, SUMS[q] + 1)
                    mm(SC[0][:, :], ONES, PB[:, 2, :], start=True, stop=True).then_inc(ss_done, 1)
                    return
                for k in range(KD):
                    pe.wait_ge(sq_done, SUMS[q] + k + 1)
                    mm(SC[0][:, 0:n], ONES, SQ[:, k % 2, 0:n], start=(k == 0), stop=(k == KD - 1)).then_inc(ss_done, 1)

            def attention(seg, tb_read=None):
                n = len(seg)
                for k in range(n + 3):
                    if k < n:
                        s = seg[k]
                        if s["g"] >= 2:
                            pe.wait_ge(bm_done, s["g"] - 1)
                        for a, (l, r) in enumerate(s["qk"]):
                            last = mm(SC[s["g"] % 2][:, 0:s["w"]], l, r, start=(a == 0), stop=(a == len(s["qk"]) - 1))
                        last.then_inc(qk_done, 1)
                    if 2 <= k < n + 2:
                        s = seg[k - 2]
                        if tb_read is not None and k == 2:
                            pe.wait_ge(*tb_read)
                        pe.wait_ge(nrm_done, s["g"] + 1)
                        if s["g"]:
                            pe.wait_ge(pt_done, s["g"])
                        for t in range(s["w"] // P):
                            last = nc.tensor.transpose(TB[:, P * t:P * t + P], PB[:, s["g"] % 3, P * t:P * t + P], IDENT)
                        last.then_inc(tr_done, 1)
                    if 3 <= k < n + 3:
                        s = seg[k - 3]
                        pe.wait_ge(pt_done, s["g"] + 1)
                        if s["first"] and s["group"]:
                            pe.wait_ge(o_out, s["group"])
                        nv = s["w"] // P
                        for t in range(nv):
                            last = mm(s["o"], s["v"][t], PT[:, s["g"] % 2, P * t:P * t + P], start=(t == 0), stop=(t == nv - 1))
                        last.then_inc(pv_done, 1)

            def rotate(r, mat, src, ready):
                pe.wait_ge(*ready)
                if r >= 2:
                    pe.wait_ge(roped, r - 1)
                mm(RB[r % 2][:, :], mat, src, start=True, stop=True).then_inc(rot_done, 1)

            def emptied(name):
                return act_emptied, EMPTIED[JOBS[name].banks[-1]][1]

            def head_sum(name, mats, n, rows=(slice(0, P), slice(0, P), slice(0, P))):
                q, idxs = HEADS[name]
                if q >= 2:
                    pe.wait_ge(hs_std, q - 1)
                for a, idx in enumerate(idxs):
                    pe.wait_ge(hs_sq, idx + 1)
                    mm(SC[q % 2][:, 0:n], mats[a][rows[a], :], SQ[rows[a], idx % 2, 0:n], start=(a == 0),
                       stop=(a == len(idxs) - 1)).then_inc(hs_ss, 1)

            pe.wait_ge(consts_in, 16 * 4)
            norm_sum(0)
            token_job("vbiw", xh, xl, 72, xready=0)
            for k in ("iq0", "iq1", "ik", "kb"):
                feature_job(k, xh, xl)
            pe.wait_ge(tabs_in, 16 * 4)
            rotate(0, ROTI, IQ[:, 0, :], emptied("iq0"))
            rotate(1, ROTI, IQ[:, 1, :], emptied("iq1"))
            feature_job("qa0", xh, xl)
            rotate(2, ROTI, IK[:, :], emptied("ik"))
            rotate(3, ROTB, KBT[:, :], emptied("kb"))
            feature_job("qa1", xh, xl)
            n = 0
            fill = ["qa2", "qa3", "ka0", "ka1", "ka2", "ka3"]
            pe.wait_ge(roped, 3)
            for i in range(1, NT):
                for h in range(IDXH):
                    if n >= 2:
                        pe.wait_ge(irelu_done, n - 1)
                    r = slice(IDXD * (h % 4), IDXD * (h % 4) + IDXD)
                    mm(SC[n % 2][:, 0:P * (i + 1)], IQ[r, h // 4, P * i:P * i + P], IK[r, 0:P * (i + 1)],
                       start=True, stop=True).then_inc(ilog_done, 1)
                    n += 1
                    if n % 4 == 0:
                        feature_job(fill[n // 4 - 1], xh, xl)
            token_job("va", xh, xl, 512)
            for g in ("qb", "ga", "gb"):
                for k in range(4):
                    feature_job(f"{g}{k}", xh, xl)
            for k in range(KD):
                feature_job(f"za{k}", xh, xl)
                if k >= 4:
                    rotate(k, ROTB, QB[:, k - 4, :], emptied(f"qb{k - 4}"))
            pe.wait_ge(roped, 8)
            pe.wait_ge(irelu_done, n)
            pe.wait_ge(*emptied("va"))
            attention(segments["ab"])
            pe.wait_ge(o_out, 8)
            for k in range(KD):
                feature_job(f"zb{k}", xh, xl)
                packed_job(f"pab{k}", [(lambda j: YAH[:, j, :], lambda j: YAL[:, j, :]),
                                       (lambda j: YBH[:, j, :], lambda j: YBL[:, j, :])])
            pe.drain().then_inc(arena_free, 1)
            pe.wait_ge(zb_used, KD)
            for k in range(KD):
                feature_job(f"o1_{k}", lambda j: MH[:, j, :], lambda j: ML[:, j, :])
                if k == 1:
                    norm_sum(1, MEM)
            pe.wait_ge(std_done, 2)
            norm_sum(2)
            for l in range(2):
                for k in range(2):
                    feature_job(f"mk{l}{k}", lambda j: XH[:, j, MEM * l:MEM * l + MEM],
                                lambda j: XL[:, j, MEM * l:MEM * l + MEM], n=MEM, xready=XLB[1] + KD * l)
                token_job(f"mv{l}", lambda j: XH[:, j, MEM * l:MEM * l + MEM],
                          lambda j: XL[:, j, MEM * l:MEM * l + MEM], MEM, tiles=2)
            pe.drain().then_inc(arena_free, 1)
            pe.wait_ge(std_done, 3)
            for l in range(2):
                for k in range(2):
                    head_sum(f"mk{l}{k}", [BONES], MEM)
            pe.wait_ge(hs_std, 4)
            norm_sum(3)
            for k in range(HG):
                feature_job(f"hf{k}", xh, xl, xready=XLB[3] if k == 0 else None)
            for k in range(HG):
                feature_job(f"hq{k}", xh, xl)
            for k in range(2):
                token_job(f"hv{k}", xh, xl, 384)
            fill = ["qm00", "qm01"] + [f"hg{k}" for k in range(HG)]
            n = 0

            def sum_to_tb(use, mat):
                if use:
                    pe.wait_ge(tb_copied, use)
                pe.wait_ge(hs_sq, HEADS["qm00"][1][0] + use + 1)
                mm(TB[:, :], mat, TMP[:, use % 2, :], start=True, stop=True).then_inc(hs_ss, 1)

            pe.wait_ge(*emptied("hv1"))
            for h in range(HG):
                for l in range(10):
                    if h == 1 and l in (0, 6):
                        sum_to_tb(l // 6, BONES)
                    elif h >= 2 and l == 2:
                        sum_to_tb(h, ONES)
                    if n >= 2:
                        pe.wait_ge(lv_cp, n - 1)
                    o = SC[n % 2]
                    pe.wait_ge(lv_w, n + 1)
                    for t in range(NT):
                        c = slice(P * t, P * t + P)
                        if l < 7:
                            last = mm(o[:, c], PB[:, n % 3, c], PB[:, n % 3, c], start=True, stop=True)
                        elif l == 7:
                            last = mm(o[:, c], HK[:, h, c], HQ[:, h, c], start=True, stop=True)
                    if l == 8:
                        for a, (j, i) in enumerate(((0, 1), (1, 2), (2, 3))):
                            mm(o[:, P * a:P * a + P], KX[:, P * j:P * j + P], QX[:, P * i:P * i + P], start=True, stop=True)
                        last = mm(o[:, 3 * P:4 * P], KX2[:, 0, :], QX[:, 2 * P:3 * P], start=True, stop=True)
                    if l == 9:
                        mm(o[:, 0:P], KX2[:, 1, :], QX[:, 3 * P:4 * P], start=True, stop=True)
                        last = mm(o[:, P:2 * P], KX2[:, 2, :], QX[:, 3 * P:4 * P], start=True, stop=True)
                    last.then_inc(lv_mm, 1)
                    n += 1
                    if l == 0:
                        beside = [feature_tiles(fill.pop(0), xh, xl) for _ in range(2 if h < 2 else 1)]
                    for job in beside if l < 8 else ():
                        next(job)
                        if l == 7:
                            next(job, None)
                pe.wait_ge(lv_cp, n)
                if h:
                    pe.wait_ge(ho_out, h)
                slot = {(0, 1): 0, (1, 2): 1, (2, 3): 2, (0, 2): 3, (1, 3): 4, (0, 3): 5}
                for i in range(NT):
                    for j in range(i + 1):
                        a = PT[:, h % 2, P * i:P * i + P] if j == i else AX[:, slot[j, i], :]
                        last = mm(OB[:, P * i:P * i + P], HV[:, j, P * h:P * h + P], a, start=(j == 0), stop=(j == i))
                last.then_inc(ho_mm, 1)
            assert not fill
            sum_to_tb(HG, ONES)
            sum_to_tb(HG + 1, ONES)
            pe.wait_ge(hs_done, HEADS["qm01"][0] + 1)
            attention(segments["m0"], (hs_std, HEADS["ho5"][0] + 1))
            pe.wait_ge(o_out, 10)
            pe.wait_ge(hs_done, HEADS["ho5"][0] + 1)

            def tail(l, hi, lo, ni):
                for k in range(KD):
                    feature_job(f"wo{l}{k}", hi, lo)
                pe.drain().then_inc(arena_free, 1)
                norm_sum(ni)
                ja = JOBS[f"ua{l}_0"]
                s0, u0 = ja.slabs[0], ja.banks[0]
                d0 = EMPTIED[u0 - 4][1]
                with pe.Fori(0, FF // 2) as it:
                    for j in range(4):
                        pe.wait_ge(dve_emptied, it * 4 + (d0 + j))
                        pe.wait_ge(lo_done, it * 4 + (s0 + j + 1))
                        s = (s0 + j) % SPLIT
                        for k in range(KD):
                            c = slice(P * k, P * k + P)
                            o = DB[(u0 + j) % 4][:, :]
                            if j == 0:
                                pe.wait_ge(xl_done, XLB[ni] + k + 1)
                            mm(o, WH[:, s, c], xh(k), start=(k == 0), stop=False)
                            mm(o, WH[:, s, c], xl(k), start=False, stop=False)
                            last = mm(o, WL[:, s, c], xh(k), start=False, stop=(k == KD - 1))
                        last.then_inc(slab_used, 1)
                jd = JOBS[f"dn{l}0"]
                s0, u0 = jd.slabs[0], jd.banks[0]
                d0 = EMPTIED[u0 - 4][1]
                with pe.Fori(0, KD // 4) as it:
                    for j in range(4):
                        pe.wait_ge(dve_emptied, it * 4 + (d0 + j))
                        o = DB[(u0 + j) % 4][:, :]
                        for k in range(FF):
                            sl = s0 + 3 * j + k // 8
                            s, c = sl % SPLIT, slice(P * (k % 8), P * (k % 8) + P)
                            if k % 8 == 0:
                                pe.wait_ge(lo_done, it * 12 + (sl + 1))
                            if j == 0:
                                pe.wait_ge(g_done, FF * l + k + 1)
                            mm(o, WH[:, s, c], GH[:, k, :], start=(k == 0), stop=False)
                            mm(o, WH[:, s, c], GL[:, k, :], start=False, stop=False)
                            last = mm(o, WL[:, s, c], GH[:, k, :], start=False, stop=(k == FF - 1))
                            if k % 8 == 7 or k == FF - 1:
                                last.then_inc(slab_used, 1)
                pe.drain().then_inc(arena_free, 1)

            tail(0, lambda j: YH[:, j, :], lambda j: YL[:, j, :], 4)
            norm_sum(5)
            for k in range(3):
                feature_job(f"cq{k}", xh, xl, xready=XLB[5] if k == 0 else None)
            for k in range(2):
                feature_job(f"ckv{k}", xh, xl)
            head_sum("cq", [ONES] * 3, TOK)
            feature_job("kpe", xh, xl)
            head_sum("ckv", [ONES] * 2, TOK)
            for k in range(2):
                feature_job(f"qm1{k}", xh, xl)
            for k in range(2):
                head_sum(f"qm1{k}", [BONES], TOK)
            rotate(8, ROTM, KPR[:, :], (gain_done, 1))
            pe.wait_ge(hs_done, HEADS["ckv"][0] + 1)
            cq, ckv = (lambda j: CQH[:, j, :], lambda j: CQL[:, j, :]), (lambda j: CKH[:, j, :], lambda j: CKL[:, j, :])
            for k in range(3):
                packed_job(f"uqn{k}", [cq] * 2)
            packed_job("uqr0", [cq] * 2)
            packed_job("uqr1", [cq])
            pe.drain().then_inc(arena_free, 1)
            for k in range(2):
                packed_job(f"ukn{k}", [ckv] * (4, 2)[k])
                for h in range(3 * k, 3 * k + 3):
                    head_sum(f"qn{h}", [ONES, ONES], TOK, (slice(0, P), HALF[h % 2]))
            for k in range(2):
                token_job(f"uv{k}", *ckv, 384)
            for h in range(MLH):
                head_sum(f"kn{h}", [ONES, ONES], TOK, (slice(0, P), HALF[0]))
            for k in range(3):
                rotate(9 + k, ROTM, QR[:, k, :], (gain_done, 2 + k))
            pe.wait_ge(roped, 12)
            pe.wait_ge(*emptied("uv1"))
            attention(segments["l"])
            attention(segments["m1"])
            pe.wait_ge(o_out, 18)
            tail(1, lambda j: YH1[:, j, :], lambda j: YL1[:, j, :], 6)

        @block.scalar
        def _(act):
            A = nc.scalar.activation

            split_next = [0]

            def high(n, turn=0, turns=0):
                if n >= SPLIT:
                    act.wait_ge(slab_used, turn * turns + (n - SPLIT + 1))
                act.wait_ge(raw_in[n % RING], turn * (16 * turns // RING) + 16 * (n // RING + 1))
                A(WH[:, n % SPLIT, :], RAW[:, n % RING, :], ACT.Copy).then_inc(hi_done, 1)

            def split_past(name):
                while split_next[0] < JOBS[name].done + SPLIT:
                    high(split_next[0])
                    split_next[0] += 1

            def job_ready(name):
                split_past(name)
                act.wait_ge(slab_used, JOBS[name].done)

            def evac(name, dst, func=ACT.Copy, t=0, width=TOK, **kw):
                job_ready(name)
                A(dst, DB[JOBS[name].banks[t] % 4][:, 0:width], func, **kw).then_inc(act_emptied, 1)

            def norm(ni, src, ready, n=TOK, halves=((0, 0),)):
                sums = 1 if src is None else KD
                for k in range(KD) if src is not None else ():
                    ready(k)
                    if k >= 2:
                        act.wait_ge(ss_done, SUMS[ni] + k - 1)
                    A(SQ[:, k % 2, 0:n], src(k), ACT.Square).then_inc(sq_done, 1)
                act.wait_ge(ss_done, SUMS[ni] + sums)
                if ni >= 3:
                    act.wait_ge(hs_done, {3: HEADS["mk11"], 4: HEADS["ho5"], 5: HEADS["ho5"], 6: HEADS["kn5"]}[ni][0] + 1)
                A(RS[:, 0:n], SC[0][:, 0:n], ACT.Sqrt, scale=1.0 / D, bias=col("eps")).then_inc(std_done, 1)
                for l, base in halves:
                    for k in range(KD):
                        if ni == 1 and k % 4 == 3:
                            split_past(f"o1_{2 + 2 * l + k // 4}")
                        act.wait_ge(xt_done, base + k + 1)
                        A(XH[:, k, n * l:n * l + n], TMP[:, k % 2, 0:n], ACT.Copy).then_inc(xh_done, 1)

            def head_square(idx, src, n=TOK, rows=slice(0, P)):
                if idx >= 2:
                    act.wait_ge(hs_ss, idx - 1)
                A(SQ[rows, idx % 2, 0:n], src, ACT.Square).then_inc(hs_sq, 1)

            def head_std(name, scale, eps, n=TOK):
                q, idxs = HEADS[name]
                act.wait_ge(hs_ss, idxs[-1] + 1)
                if q >= 2:
                    act.wait_ge(hs_done, q - 1)
                A(RH[q % 2][:, 0:n], SC[q % 2][:, 0:n], ACT.Sqrt, scale=scale, bias=col("eps", eps)).then_inc(hs_std, 1)

            def attention(seg, after=None):
                n = len(seg)
                for k in range(n + 2):
                    if k >= 2:
                        s = seg[k - 2]
                        g = s["g"]
                        act.wait_ge(tr_done, g + 1)
                        if g >= 2:
                            act.wait_ge(pv_done, g - 1)
                        A(PT[:, g % 2, 0:s["w"]], TB[:, 0:s["w"]], ACT.Copy).then_inc(pt_done, 1)
                    if k < n:
                        s = seg[k]
                        g = s["g"]
                        act.wait_ge(bm_done, g + 1)
                        if g >= 3:
                            act.wait_ge(tr_done, g - 2)
                        A(PB[:, g % 3, 0:s["w"]], SB[:, g % 2, 0:s["w"]], ACT.Exp, scale=-1.0,
                          bias=ST[:, g % 4:g % 4 + 1], accum_out=ST[:, 8 + g % 4:9 + g % 4]).then_inc(exp_done, 1)
                        if after is not None:
                            after(s)

            act.dma_start(PAR[:, :], pars).then_inc(consts_in, 16)
            act.dma_start(CONST[:, :, :], consts).then_inc(consts_in, 16)
            for k in range(KD):
                act.dma_start(X[:, k, :], xt_in[k]).then_inc(x_in, 16)
            act.dma_start(CZ[:, :], cz_in).then_inc(consts_in, 16)
            act.dma_start(CW[:, :, :, :], convp).then_inc(consts_in, 16)
            for i, t in enumerate((COSI, SINI, COSB, SINB)):
                act.dma_start(t[:, :], rope_tabs[i]).then_inc(tabs_in, 16)
            for n in range(SPLIT):
                high(n)
            split_next[0] = SPLIT
            act.wait_ge(lb_e, 1)
            A(LBC[:, 0:18], LBC[:, 0:18], ACT.Exp).then_inc(lb_e, 1)
            act.wait_ge(x_in, 16 * KD)
            act.wait_ge(consts_in, 16 * 4)
            norm(0, lambda k: X[:, k, :], lambda k: None)
            job_ready("vbiw")
            for t in range(NT):
                b = DB[JOBS["vbiw"].banks[t] % 4]
                A(VB[:, t, :], b[:, 0:DH], ACT.Copy)
                A(IW[:, t, :], b[:, DH:DH + IDXH], ACT.Copy, scale=float(IDXH ** -0.5 * IDXD ** -0.5)).then_inc(act_emptied, 1)
            evac("iq0", IQ[:, 0, :])
            evac("iq1", IQ[:, 1, :])
            evac("ik", IK[:, :])
            evac("kb", KBT[:, :])
            evac("qa0", QA[:, 0, :], scale=DH ** -0.5)
            evac("qa1", QA[:, 1, :], scale=DH ** -0.5)
            n = 0
            for i in range(1, NT):
                w = P * (i + 1)
                for h in range(IDXH):
                    act.wait_ge(ilog_done, n + 1)
                    if n >= 2:
                        act.wait_ge(iacc_done, n - 1)
                    A(SB[:, n % 2, 0:w], SC[n % 2][:, 0:w], ACT.Relu).then_inc(irelu_done, 1)
                    n += 1
                    if n in (4, 8):
                        evac(f"qa{n // 4 + 1}", QA[:, n // 4 + 1, :], scale=DH ** -0.5)
                    elif n % 4 == 0:
                        evac(f"ka{n // 4 - 3}", KA[:, n // 4 - 3, :])
            act.wait_ge(roped, 4)
            for p in range(2):
                act.dma_start(TP[:, p, :, :], toep[p]).then_inc(toep_in[p], 16)
            for t in range(NT):
                evac("va", VA[:, t, :], t=t)
            for k in range(4):
                evac(f"qb{k}", QB[:, k, :], scale=DH ** -0.5)
            for k in range(4):
                evac(f"ga{k}", GA[:, k, :], ACT.Silu)
            for k in range(4):
                evac(f"gb{k}", GB[:, k, :], ACT.Silu)
            for k in range(KD):
                evac(f"za{k}", ZA[:, k, :], ACT.Sigmoid, bias=col("bm0", k))

            def next_bias(s):
                if s["kind"] == "a" and s["last"] and s["grp"] < 2:
                    act.dma_start(TP[:, s["grp"], :, :], toep[s["grp"] + 2]).then_inc(toep_in[s["grp"]], 16)

            attention(segments["ab"], next_bias)
            for k in range(KD):
                if k >= 2:
                    act.wait_ge(zb_used, k - 1)
                evac(f"zb{k}", SQ[:, k % 2, :], ACT.Sigmoid, bias=col("bm1", k))
                split_past(f"pab{k}")
            act.wait_ge(arena_free, 1)
            act.dma_start(MRAW[:, :, :], memt_in).then_inc(mem_in, 16)
            act.wait_ge(zb_used, KD)
            act.dma_start(MSKI[:, :, :], masks8).then_inc(hg_in, 16)
            act.dma_start(RESET[:, :], resets).then_inc(hg_in, 16)
            act.wait_ge(mem_in, 16)
            split_past("o1_0")
            split_past("o1_1")
            norm(1, lambda k: MRAW[:, k, :], lambda k: None, MEM, ((0, XTB[1]), (1, XTB[1] + KD)))
            split_past(f"o1_{KD - 1}")
            norm(2, None, None, halves=())
            for l in range(2):
                for k in range(2):
                    evac(f"mk{l}{k}", MKT[l][:, k, :], width=MEM)
                for t in range(2):
                    evac(f"mv{l}", MVT[l][:, t, :], t=t, width=MEM)
            act.wait_ge(x_new, KD)
            for l in range(2):
                for k in range(2):
                    act.wait_ge(act_emptied, EMPTIED[JOBS[f"mk{l}{k}"].banks[0]][1])
                    head_square(HEADS[f"mk{l}{k}"][1][0], MKT[l][:, k, :], MEM)
                    head_std(f"mk{l}{k}", 1.0 / DH, 0, MEM)
            norm(3, lambda k: X[:, k, :], lambda k: act.wait_ge(x_new, k + 1), halves=((0, XTB[3]),))
            for k in range(HG):
                job_ready(f"hf{k}")
                b = DB[JOBS[f"hf{k}"].banks[0] % 4]
                A(HB[:, k, :], b[:, :], ACT.Sigmoid)
                A(HK[:, k, :], b[:, :], ACT.Sigmoid, scale=-1.0).then_inc(act_emptied, 1)
            for k in range(HG):
                evac(f"hq{k}", HQ[:, k, :], ACT.Silu)
            act.wait_ge(lb_done, 1)
            for k in range(HG):
                act.wait_ge(act_emptied, EMPTIED[JOBS[f"hf{k}"].banks[0]][1])
                A(HB[:, k, :], HB[:, k, :], ACT.Ln, scale=LBC[:, 30 + k:31 + k], bias=LBC[:, 24 + k:25 + k]).then_inc(hf_ln, 1)
            for k in range(2):
                for t in range(NT):
                    evac(f"hv{k}", HV[:, t, 384 * k:384 * k + 384], t=t, width=384)
            sq0 = HEADS["qm00"][1][0]

            def head_out(h):
                act.wait_ge(ho_mm, h + 1)
                A(HQ[:, h, :], OB[:, :], ACT.Copy).then_inc(ho_out, 1)
                act.wait_ge(ho_out, h + 1)
                square(h + 2, HQ[:, h, :])

            def square(use, src):
                if use >= 2:
                    act.wait_ge(hs_ss, sq0 + use - 1)
                A(TMP[:, use % 2, :], src, ACT.Square).then_inc(hs_sq, 1)

            def keep_sum(use, dst):
                act.wait_ge(hs_ss, sq0 + use + 1)
                A(dst, TB[:, :], ACT.Copy).then_inc(tb_copied, 1)

            for h in range(HG):
                for l in range(7):
                    act.wait_ge(lv_e, 8 * h + l + 1)
                    A(SB[:, l % 2, :], SB[:, l % 2, :], ACT.Exp).then_inc(lv_x, 1)
                    if h == 1 and l == 3:
                        keep_sum(0, RS[:, :])
                if h >= 2:
                    act.wait_ge(lv_w, 10 * (h - 1))
                act.wait_ge(lv_e, 8 * h + 8)
                A(SQ[:, h % 2, :], HB[:, h, :], ACT.Exp).then_inc(lv_x, 1)
                A(SB[:, 1, :], SB[:, 1, :], ACT.Exp).then_inc(lv_x, 1)
                if h == 0:
                    for k in range(2):
                        evac(f"qm0{k}", QM[:, k, :])
                    act.wait_ge(act_emptied, EMPTIED[JOBS["qm01"].banks[0]][1])
                    for k in range(2):
                        square(k, QM[:, k, :])
                else:
                    for k in ((0, 1), (2,), (3,), (4,), (5,))[h - 1]:
                        evac(f"hg{k}", HGT[:, k, :])
                if h:
                    keep_sum(h, RESET[:, :] if h == 1 else HB[:, h - 2, :])
                    head_out(h - 1)
                if h == 4:
                    act.wait_ge(act_emptied, EMPTIED[JOBS["hg4"].banks[0]][1])
                    A(HGT[:, 0:5, :], HGT[:, 0:5, :], ACT.Silu).then_inc(hg_silu, 1)
                    act.wait_ge(tb_copied, 2)
                    for r in (RS, RESET):
                        A(r[:, :], r[:, :], ACT.Sqrt, bias=col("eps", 1)).then_inc(hs_std, 1)
            keep_sum(HG, HB[:, HG - 2, :])
            head_out(HG - 1)
            act.wait_ge(act_emptied, EMPTIED[JOBS["hg5"].banks[0]][1])
            A(HGT[:, 5, :], HGT[:, 5, :], ACT.Silu).then_inc(hg_silu, 1)
            act.wait_ge(tb_copied, HG + 1)
            A(HB[:, 0:HG - 1, :], HB[:, 0:HG - 1, :], ACT.Sqrt, scale=1.0 / P, bias=col("eps", 0)).then_inc(hs_std, HG - 1)
            act.wait_ge(hs_ss, sq0 + HG + 2)
            A(HB[:, HG - 1, :], TB[:, :], ACT.Sqrt, scale=1.0 / P, bias=col("eps", 0)).then_inc(hs_std, 1)
            attention(segments["m0"])

            def tail(l, ni):
                split_past(f"wo{l}{KD - 1}")
                norm(ni, None, None, halves=((0, XTB[ni]),))
                ja = JOBS[f"ua{l}_0"]
                s0, u0, base = ja.slabs[0], ja.banks[0], FF * l
                with act.Fori(0, FF // 2) as it:
                    for jj in range(2):
                        act.wait_ge(cv_g, it * 2 + (base + 2 * l + jj + 1))
                        for e, dst in ((0, SB), (1, PB)):
                            j = 2 * jj + e
                            w = CW[:, l, bass.ds(it * 2 + jj, 1), :].rearrange("p o c -> p (o c)")
                            high(s0 + j + SPLIT, it, 4)
                            act.wait_ge(slab_used, it * 4 + (s0 + j + 1))
                            A(dst[:, jj, :], DB[(u0 + j) % 4][:, :], ACT.Identity, scale=w[:, 4 * e + 2:4 * e + 3],
                              bias=w[:, 4 * e + 3:4 * e + 4]).then_inc(cv_i, 1)
                        act.wait_ge(dve_emptied, it * 4 + (EMPTIED[u0 + 2 * jj][1]))
                        A(PT[:, jj, :], SB[:, jj, :], ACT.Silu).then_inc(cv_s, 1)
                s0 = JOBS[f"dn{l}0"].slabs[0]
                with act.Fori(0, KD // 4) as it:
                    for j in range(12):
                        high(s0 + j + SPLIT, it, 12)
                split_next[0] = s0 + 3 * KD + SPLIT

            tail(0, 4)
            act.wait_ge(arena_free, 4)
            act.dma_start(POSI[:, :], pos_in.partition_broadcast(P)).then_inc(pos_ready, 16)
            norm(5, None, None, halves=((0, XTB[5]),))
            for k in range(3):
                evac(f"cq{k}", CQ[:, k, :])
            for k in range(3):
                act.wait_ge(act_emptied, EMPTIED[JOBS[f"cq{k}"].banks[0]][1])
                head_square(HEADS["cq"][1][k], CQ[:, k, :]) if k < 2 else None
            for k in range(2):
                evac(f"ckv{k}", CKV[:, k, :])
            head_square(HEADS["cq"][1][2], CQ[:, 2, :])
            head_std("cq", 1.0 / 384, 0)
            act.wait_ge(act_emptied, EMPTIED[JOBS["ckv1"].banks[0]][1])
            evac("kpe", KPE[:, :])
            for k in range(2):
                head_square(HEADS["ckv"][1][k], CKV[:, k, :])
            head_std("ckv", 1.0 / 256, 0)
            for k in range(2):
                evac(f"qm1{k}", QM1[:, k, :])
            act.wait_ge(act_emptied, EMPTIED[JOBS["qm11"].banks[0]][1])
            for k in range(2):
                head_square(HEADS[f"qm1{k}"][1][0], QM1[:, k, :])
            for k in range(2):
                head_std(f"qm1{k}", 1.0, 1)
            for k, t in enumerate((SINM, COSM)):
                act.wait_ge(ang_done, k + 1)
                A(t[:, :], PB[:, 2 * k, :], ACT.Sin).then_inc(sin_done, 1)
            for k in range(MLH):
                evac(f"uqn{k // 2}", QN[:, k, :], t=k % 2)
            for k in range(3):
                evac(f"uqr{k // 2}", QR[:, k, :], t=k % 2)
            for k in range(MLH):
                if k % 3 == 0:
                    for h in ((0, 1, 2, 3), (4, 5))[k // 3]:
                        evac(f"ukn{k // 3}", KN[:, h, :], t=h % 4)
                q, idxs = HEADS[f"qn{k}"]
                act.wait_ge(act_emptied, EMPTIED[JOBS["uqr1"].banks[0]][1])
                head_square(idxs[0], QN[:, k, :])
                head_square(idxs[1], QR[HALF[k % 2], k // 2, :], rows=HALF[k % 2])
                head_std(f"qn{k}", 1.0, 2)
            for k in range(2):
                for t in range(NT):
                    evac(f"uv{k}", MV[:, t, 384 * k:384 * k + 384], t=t, width=384)
            for k in range(MLH):
                q, idxs = HEADS[f"kn{k}"]
                act.wait_ge(act_emptied, EMPTIED[JOBS["ukn1"].banks[1]][1])
                head_square(idxs[0], KN[:, k, :])
                head_square(idxs[1], KPE[HALF[0], :], rows=HALF[0])
                head_std(f"kn{k}", 1.0 / 192, 0)
            attention(segments["l"])
            attention(segments["m1"])
            tail(1, 6)

        @block.vector
        def _(dve):
            V = nc.vector
            chain = [0]

            def link(ins):
                chain[0] += 1
                ins.then_inc(dve_chain, 1)
                dve.wait_ge(dve_chain, chain[0])

            def norm(ni, srcs):
                dve.wait_ge(std_done, ni + 1)
                n = srcs[0][0].shape[-1]
                link(V.reciprocal(RS[:, 0:n], RS[:, 0:n]))
                base = XTB[ni]
                for a in range(len(srcs) + 1):
                    if a < len(srcs):
                        src, gain, _ = srcs[a]
                        if base + a >= 2:
                            dve.wait_ge(xl_done, base + a - 1)
                        V.scalar_tensor_tensor(TMP[:, a % 2, 0:n], src, gain, RS[:, 0:n], ALU.mult, ALU.mult).then_inc(xt_done, 1)
                    if a:
                        src, _, (k, c) = srcs[a - 1]
                        dve.wait_ge(xh_done, base + a)
                        V.tensor_tensor(XL[:, k, c], TMP[:, (a - 1) % 2, 0:n], XH[:, k, c].bitcast(F32),
                                        ALU.subtract).then_inc(xl_done, 1)

            def x_norm(ni, gain):
                norm(ni, [(X[:, k, :], col(gain, k), (k, slice(0, TOK))) for k in range(KD)])

            def split_out(hi, lo, src, signal=None):
                link(V.tensor_copy(hi, src))
                last = V.tensor_tensor(lo, src, hi.bitcast(F32), ALU.subtract)
                if signal is None:
                    link(last)
                else:
                    last.then_inc(signal, 1)

            def rope(r, x, cos, sin):
                dve.wait_ge(rot_done, r + 1)
                if r:
                    dve.wait_ge(roped, r)
                link(V.tensor_tensor(TMP[:, 0, :], RB[r % 2][:, :], sin, ALU.mult))
                link(V.tensor_tensor(x, x, cos, ALU.mult))
                V.tensor_tensor(x, x, TMP[:, 0, :], ALU.add).then_inc(roped, 1)

            def add_to_x(name, k):
                j = JOBS[name]
                dve.wait_ge(slab_used, j.done)
                V.tensor_tensor(X[:, k, :], X[:, k, :], DB[j.banks[0] % 4][:, :], ALU.add).then_inc(dve_emptied, 1)
                dve.wait_ge(dve_emptied, EMPTIED[j.banks[0]][1])
                sq = PB[:, 2, :] if k == 0 else PB[:, 1, :]
                link(V.tensor_tensor(sq, X[:, k, :], X[:, k, :], ALU.mult))
                if k:
                    last = V.tensor_tensor(PB[:, 2, :], PB[:, 2, :], sq, ALU.add)
                    link(last) if k < KD - 1 else last.then_inc(sq_done, 1)

            def head_root(name, n=TOK):
                q = HEADS[name][0]
                dve.wait_ge(hs_std, q + 1)
                link(V.reciprocal(RH[q % 2][:, 0:n], RH[q % 2][:, 0:n]))
                return RH[q % 2][:, 0:n]

            def group_out(s):
                dve.wait_ge(pv_done, s["g"] + 1)
                p = s["grp"]
                if s["kind"] in "ab":
                    gate, hi, lo = (GA, YAH, YAL) if s["kind"] == "a" else (GB, YBH, YBL)
                    link(V.tensor_tensor(TMP[:, 0, :], OB[:, :], gate[:, p, :], ALU.mult))
                    split_out(hi[:, p, :], lo[:, p, :], TMP[:, 0, :], o_out)
                else:
                    hi, lo, t = {"m0": (YH, YL, 6 + p), "m1": (YH1, YL1, 6 + p), "l": (YH1, YL1, p)}[s["kind"]]
                    split_out(hi[:, t, :], lo[:, t, :], OB[:, :], o_out)

            def attention(seg, beside=None):
                n = len(seg)
                for k in range(n + 4):
                    for _ in range(2 if beside is not None and k >= 2 else 0):
                        next(beside, None)
                    if k < n:
                        s = seg[k]
                        g = s["g"]
                        if s["kind"] == "a" and s["first"]:
                            dve.wait_ge(toep_in[s["grp"] % 2], 16 * (1 + s["grp"] // 2))
                        dve.wait_ge(qk_done, g + 1)
                        if g >= 2:
                            dve.wait_ge(exp_done, g - 1)
                        V.tensor_tensor_reduce(out=SB[:, g % 2, 0:s["w"]], in0=SC[g % 2][:, 0:s["w"]], in1=s["bias"],
                                               scale=-1.0, scalar=3.0e38, op0=ALU.add, op1=ALU.min,
                                               accum_out=ST[:, g % 4:g % 4 + 1]).then_inc(bm_done, 1)
                    if 1 <= k <= n:
                        s = seg[k - 1]
                        g = s["g"]
                        dve.wait_ge(exp_done, g + 1)
                        link(V.reciprocal(ST[:, 16 + g % 4:17 + g % 4], ST[:, 8 + g % 4:9 + g % 4]))
                        V.tensor_scalar(PB[:, g % 3, 0:s["w"]], PB[:, g % 3, 0:s["w"]], ST[:, 16 + g % 4:17 + g % 4],
                                        None, ALU.mult).then_inc(nrm_done, 1)
                    if k >= 4 and seg[k - 4]["last"]:
                        group_out(seg[k - 4])
                dve.wait_ge(tr_done, seg[-1]["g"] + 1)

            dve.wait_ge(consts_in, 16 * 4)
            c0 = COLS["lb"][0]
            lg = [PAR[:, c0 + HG * j:c0 + HG * j + HG] for j in range(3)]
            mx, lb, om = LBC[:, 18:24], LBC[:, 24:30], LBC[:, 30:36]
            link(V.tensor_tensor(mx, lg[0], lg[1], ALU.max))
            link(V.tensor_tensor(mx, mx, lg[2], ALU.max))
            for j in range(2):
                link(V.tensor_tensor(LBC[:, 6 * j:6 * j + 6], lg[j], mx, ALU.subtract))
            V.tensor_tensor(LBC[:, 12:18], lg[2], mx, ALU.subtract).then_inc(lb_e, 1)
            dve.wait_ge(lb_e, 2)
            link(V.tensor_tensor(mx, LBC[:, 0:6], LBC[:, 6:12], ALU.add))
            link(V.tensor_tensor(mx, mx, LBC[:, 12:18], ALU.add))
            link(V.reciprocal(mx, mx))
            link(V.tensor_tensor(lb, LBC[:, 0:6], mx, ALU.mult))
            link(V.tensor_scalar(om, lb, -1.0, 1.0, ALU.mult, ALU.add))
            V.tensor_scalar(mx, om, float(P ** -0.5), None, ALU.mult).then_inc(lb_done, 1)
            x_norm(0, "norm_gain")
            dve.wait_ge(tabs_in, 16 * 4)
            rope(0, IQ[:, 0, :], COSI[:, :], SINI[:, :])
            rope(1, IQ[:, 1, :], COSI[:, :], SINI[:, :])
            rope(2, IK[:, :], COSI[:, :], SINI[:, :])
            rope(3, KBT[:, :], COSB[:, :], SINB[:, :])
            n, off = 0, 0
            for i in range(1, NT):
                w = P * (i + 1)
                sc = MB[:, off:off + w]
                for h in range(IDXH):
                    dve.wait_ge(irelu_done, n + 1)
                    wt = IW[:, i, h:h + 1]
                    if h == 0:
                        V.tensor_scalar(sc, SB[:, n % 2, 0:w], wt, None, ALU.mult).then_inc(iacc_done, 1)
                    else:
                        dve.wait_ge(iacc_done, n)
                        V.scalar_tensor_tensor(sc, SB[:, n % 2, 0:w], wt, sc, ALU.mult, ALU.add).then_inc(iacc_done, 1)
                    n += 1
                off += w
            dve.wait_ge(iacc_done, n)
            off = 0
            for i in range(1, NT):
                w = P * (i + 1)
                sc = MB[:, off:off + w]
                link(V.memset(MB[0:CHUNK, off + w - CHUNK:off + w], BARRED))
                for _ in range(TOPK // 8):
                    link(V.max(MX8[:, :], sc))
                    link(V.match_replace(sc, MX8[:, :], sc, TAKEN))
                link(V.tensor_scalar(sc, sc, 0.5 * (TAKEN + BARRED), NEG, ALU.is_gt, ALU.mult))
                off += w
            for k in range(4):
                rope(4 + k, QB[:, k, :], COSB[:, :], SINB[:, :])
            attention(segments["ab"])
            dve.wait_ge(o_out, 8)
            for k in range(KD):
                j = JOBS[f"pab{k}"]
                dve.wait_ge(slab_used, j.done)
                V.tensor_tensor(TMP[:, 0, :], DB[j.banks[0] % 4][:, :], ZA[:, k, :], ALU.mult).then_inc(dve_emptied, 1)
                dve.wait_ge(act_emptied, EMPTIED[JOBS[f"zb{k}"].banks[0]][1])
                V.tensor_tensor(TMP[:, 1, :], DB[j.banks[1] % 4][:, :], SQ[:, k % 2, :], ALU.mult).then_inc(dve_emptied, 1)
                dve.wait_ge(dve_emptied, EMPTIED[j.banks[1]][1])
                link(V.tensor_tensor(TMP[:, 0, :], TMP[:, 0, :], TMP[:, 1, :], ALU.add))
                split_out(MH[:, k, :], ML[:, k, :], TMP[:, 0, :], zb_used)
                dve.wait_ge(zb_used, k + 1)
            add_to_x("o1_0", 0)
            add_to_x("o1_1", 1)
            norm(1, [(MRAW[:, k, :], col(f"mem{l}", k), (k, slice(MEM * l, MEM * l + MEM)))
                     for l in range(2) for k in range(KD)])
            for k in range(2, KD):
                add_to_x(f"o1_{k}", k)
            dve.wait_ge(std_done, 3)
            link(V.reciprocal(RS[:, :], RS[:, :]))
            for k in range(KD):
                V.scalar_tensor_tensor(X[:, k, :], X[:, k, :], col("final_gain", k), RS[:, :], ALU.mult, ALU.mult).then_inc(x_new, 1)
            dve.wait_ge(x_new, KD)
            for l in range(2):
                for k in range(2):
                    r = head_root(f"mk{l}{k}", MEM)
                    V.scalar_tensor_tensor(MKT[l][:, k, :], MKT[l][:, k, :], col(f"mk{l}"), r, ALU.mult, ALU.mult).then_inc(hs_done, 1)
            dve.wait_ge(arena_free, 2)
            x_norm(3, "mix0")
            dve.wait_ge(hg_in, 32)
            dve.wait_ge(lb_done, 1)
            for k in range(HG):
                dve.wait_ge(hf_ln, k + 1)
                link(V.tensor_scalar(HK[:, k, :], HK[:, k, :], LBC[:, 18 + k:19 + k], None, ALU.mult))
                link(V.tensor_tensor_scan(HB[:, k, :], RESET[:, :], HB[:, k, :], 0.0, ALU.mult, ALU.add))
            V.drain().then_inc(decays_ready, 1)
            link(V.memset(PT[:, :, :], 0.0))
            link(V.tensor_copy(MSK[:, :, :], MSKI[:, :, :]))
            dve.wait_ge(act_emptied, EMPTIED[JOBS["hq5"].banks[0]][1])
            def query_norm(k, root):
                dve.wait_ge(hs_std, HEADS[f"qm0{k}"][0] + 1)
                link(V.reciprocal(root[:, :], root[:, :]))
                V.scalar_tensor_tensor(QM[:, k, :], QM[:, k, :], col("mq0"), root[:, :], ALU.mult, ALU.mult).then_inc(hs_done, 1)

            for h in range(HG):
                if h == HG - 1:
                    query_norm(0, RS)
                    query_norm(1, RESET)
                b, q_, k_ = HB[:, h, :], HQ[:, h, :], HK[:, h, :]

                def weigh(l):
                    n = 10 * h + l
                    e = SB[:, l % 2, :]
                    if l < 7:
                        dve.wait_ge(lv_x, 9 * h + l + 1)
                        if n >= 3:
                            dve.wait_ge(lv_mm, n - 2)
                        m = LEVELS[l]

                        def v(a):
                            return a.rearrange("p (n s m) -> p n s m", s=2, m=m)

                        o = v(PB[:, n % 3, :])
                        V.tensor_tensor(o[:, :, 1, :], v(q_)[:, :, 1, :], v(e)[:, :, 1, :], ALU.mult)
                        V.tensor_tensor(o[:, :, 0, :], v(k_)[:, :, 0, :], v(e)[:, :, 0, :], ALU.mult).then_inc(lv_w, 1)
                    else:
                        dve.wait_ge(lv_x, 9 * h + 9)
                        if h:
                            dve.wait_ge(lv_mm, 10 * h)
                        eb = SQ[:, h % 2, :]
                        V.tensor_tensor(QX[:, :], q_, eb, ALU.mult).then_inc(lv_w, 1)
                        link(V.tensor_tensor(KX[:, :], k_, e, ALU.mult))
                        link(V.tensor_scalar(KX2[:, 1, :], KX[:, P:2 * P], eb[:, 3 * P - 1:3 * P], None, ALU.mult))
                        V.tensor_scalar(KX2[:, 0, :], KX[:, 0:P], eb[:, 2 * P - 1:2 * P], None, ALU.mult).then_inc(lv_w, 1)
                        dve.wait_ge(lv_w, 10 * h + 9)
                        V.tensor_scalar(KX2[:, 2, :], KX2[:, 0, :], eb[:, 3 * P - 1:3 * P], None, ALU.mult).then_inc(lv_w, 1)

                def place(l):
                    n = 10 * h + l
                    dve.wait_ge(lv_mm, n + 1)
                    if n:
                        dve.wait_ge(lv_cp, n)
                    if l == 0 and h >= 2:
                        dve.wait_ge(ho_mm, h - 1)
                    if l == 8 and h:
                        dve.wait_ge(ho_mm, h)
                    s = SC[n % 2]
                    if l < 8:
                        V.copy_predicated(PT[:, h % 2, :].rearrange("p (t n) -> p t n", t=NT),
                                          MSK[:, l:l + 1, :].broadcast_to([P, NT, P]),
                                          s[:, :].rearrange("p (t n) -> p t n", t=NT)).then_inc(lv_cp, 1)
                    else:
                        a, b_ = (0, 4) if l == 8 else (4, 6)
                        V.tensor_copy(AX[:, a:b_, :].rearrange("p t n -> p (t n)"), s[:, 0:P * (b_ - a)]).then_inc(lv_cp, 1)

                for t in range(10):
                    if 1 <= t <= 8:
                        weigh(t - 1)
                    if t >= 2:
                        place(t - 2)
                place(8)
                place(9)
            def head_outputs():
                for h in range(HG):
                    r = HB[:, h, :]
                    if h == 0:
                        dve.wait_ge(hg_silu, 2)
                        dve.wait_ge(hs_std, HEADS["ho5"][0] + 1)
                    link(V.reciprocal(r, r))
                    yield
                    link(V.scalar_tensor_tensor(TMP[:, 0, :], HQ[:, h, :], col("onorm"), r, ALU.mult, ALU.mult))
                    yield
                    link(V.tensor_tensor(TMP[:, 1, :], TMP[:, 0, :], HGT[:, h, :], ALU.mult))
                    yield
                    link(V.tensor_copy(YH[:, h, :], TMP[:, 1, :]))
                    yield
                    V.tensor_tensor(YL[:, h, :], TMP[:, 1, :], YH[:, h, :].bitcast(F32), ALU.subtract).then_inc(hs_done, 1)
                    dve.wait_ge(hs_done, HEADS[f"ho{h}"][0] + 1)
                    yield

            attention(segments["m0"], head_outputs())

            def tail(l, ni, gain):
                for k in range(KD):
                    add_to_x(f"wo{l}{k}", k)
                dve.wait_ge(arena_free, {0: 3, 1: 6}[l])
                x_norm(ni, gain)
                ja = JOBS[f"ua{l}_0"]
                u0, base, c0 = ja.banks[0], FF * l, chain[0]
                d0 = EMPTIED[u0][1]
                V.drain().then_inc(cv_g, 2)
                with dve.Fori(0, FF // 2) as it:
                    for jj in range(2):
                        pair = it * 2 + (base + jj)
                        for e, dst in ((0, SB), (1, PB)):
                            j = 2 * jj + e
                            y, u = dst[:, jj, :], DB[(u0 + j) % 4]
                            w = CW[:, l, bass.ds(it * 2 + jj, 1), :].rearrange("p o c -> p (o c)")
                            dve.wait_ge(cv_i, it * 4 + (2 * base + j + 1))
                            V.scalar_tensor_tensor(y[:, 1:TOK], u[:, 0:TOK - 1], w[:, 4 * e + 1:4 * e + 2], y[:, 1:TOK],
                                                   ALU.mult, ALU.add).then_inc(dve_chain, 1)
                            dve.wait_ge(dve_chain, it * 6 + (c0 + 3 * jj + e + 1))
                            V.scalar_tensor_tensor(y[:, 2:TOK], u[:, 0:TOK - 2], w[:, 4 * e:4 * e + 1], y[:, 2:TOK],
                                                   ALU.mult, ALU.add).then_inc(dve_emptied, 1)
                        dve.wait_ge(dve_emptied, it * 4 + (d0 + 2 * jj + 1))
                        dve.wait_ge(cv_s, pair + 1)
                        V.tensor_tensor(TMP[:, jj, :], PT[:, jj, :], PB[:, jj, :], ALU.mult).then_inc(cv_g, 1)
                        dve.wait_ge(cv_g, pair + (2 * l + 3))
                        gh = GH[:, bass.ds(it * 2 + jj, 1), :].rearrange("p o n -> p (o n)")
                        gl = GL[:, bass.ds(it * 2 + jj, 1), :].rearrange("p o n -> p (o n)")
                        V.tensor_copy(gh, TMP[:, jj, :]).then_inc(dve_chain, 1)
                        dve.wait_ge(dve_chain, it * 6 + (c0 + 3 * jj + 3))
                        V.tensor_tensor(gl, TMP[:, jj, :], gh.bitcast(F32), ALU.subtract).then_inc(g_done, 1)
                chain[0] = c0 + 6 * (FF // 2)
                jd = JOBS[f"dn{l}0"]
                s0, u0, c1 = jd.slabs[0], jd.banks[0], chain[0] + 1
                link(V.memset(PB[:, 2, :], 0.0))
                with dve.Fori(0, KD // 4) as it:
                    for j in range(4):
                        dve.wait_ge(slab_used, it * 12 + (s0 + 3 * j + 3))
                        x = X[:, bass.ds(it * 4 + j, 1), :].rearrange("p o n -> p (o n)")
                        V.tensor_tensor(x, x, DB[(u0 + j) % 4][:, :], ALU.add).then_inc(dve_emptied, 1)
                        if l == 0:
                            dve.wait_ge(dve_emptied, it * 4 + EMPTIED[u0 + j][1])
                            V.tensor_tensor(PB[:, 1, :], x, x, ALU.mult).then_inc(dve_chain, 1)
                            dve.wait_ge(dve_chain, it * 8 + (c1 + 2 * j + 1))
                            V.tensor_tensor(PB[:, 2, :], PB[:, 2, :], PB[:, 1, :], ALU.add).then_inc(dve_chain, 1)
                            dve.wait_ge(dve_chain, it * 8 + (c1 + 2 * j + 2))
                if l == 0:
                    chain[0] += 2 * KD
                    V.drain().then_inc(sq_done, 1)

            tail(0, 4, "ffn0")
            x_norm(5, "mix1")
            ang, turns, arg = PB[:, 0, :], PB[:, 1, :], PB[:, 2, :]
            dve.wait_ge(pos_ready, 16)
            link(V.tensor_copy(PT[:, 0, :], POSI[:, :]))
            link(V.tensor_scalar(PT[:, 1, :], PT[:, 0, :], col("inv"), None, ALU.mult))
            ang = PT[:, 1, :]
            for i, (dst, quarter) in enumerate(((PB[:, 0, :], 0.0), (PB[:, 2, :], 0.25))):
                link(V.tensor_scalar(turns, ang, float(1 / (2 * np.pi)), quarter, ALU.mult, ALU.add))
                link(V.tensor_scalar(turns, turns, ROUND, ROUND, ALU.add, ALU.subtract))
                link(V.scalar_tensor_tensor(dst, turns, -TURN[0], ang, ALU.mult, ALU.add))
                link(V.scalar_tensor_tensor(dst, turns, -TURN[1], dst, ALU.mult, ALU.add))
                link(V.scalar_tensor_tensor(dst, turns, -TURN[2], dst, ALU.mult, ALU.add))
                link(V.tensor_scalar(dst, dst, float(2 * np.pi * quarter), HALFTURN, ALU.add, ALU.min))
                V.tensor_scalar(dst, dst, -HALFTURN, None, ALU.max).then_inc(ang_done, 1)
            r = head_root("cq")
            for k in range(3):
                link(V.scalar_tensor_tensor(TMP[:, 0, :], CQ[:, k, :], col("qa", k), r, ALU.mult, ALU.mult))
                split_out(CQH[:, k, :], CQL[:, k, :], TMP[:, 0, :], hs_done if k == 2 else None)
            dve.wait_ge(hs_done, HEADS["cq"][0] + 1)
            r = head_root("ckv")
            for k in range(2):
                link(V.scalar_tensor_tensor(TMP[:, 0, :], CKV[:, k, :], col("kva", k), r, ALU.mult, ALU.mult))
                split_out(CKH[:, k, :], CKL[:, k, :], TMP[:, 0, :], hs_done if k == 1 else None)
            dve.wait_ge(hs_done, HEADS["ckv"][0] + 1)
            dve.wait_ge(act_emptied, EMPTIED[JOBS["kpe"].banks[0]][1])
            V.tensor_scalar(KPR[:, :], KPE[:, :], col("kn", 1), None, ALU.mult).then_inc(gain_done, 1)
            for k in range(2):
                r = head_root(f"qm1{k}")
                V.scalar_tensor_tensor(QM1[:, k, :], QM1[:, k, :], col("mq1"), r, ALU.mult, ALU.mult).then_inc(hs_done, 1)
            dve.wait_ge(sin_done, 2)
            rope(8, KPR[:, :], COSM[:, :], SINM[:, :])
            dve.wait_ge(roped, 9)
            for h in range(MLH):
                r, half = head_root(f"qn{h}"), HALF[h % 2]
                link(V.scalar_tensor_tensor(QN[:, h, :], QN[:, h, :], col("qn"), r, ALU.mult, ALU.mult))
                V.tensor_tensor(QR[half, h // 2, :], QR[half, h // 2, :], r[half], ALU.mult).then_inc(hs_done, 1)
            for h in range(MLH):
                r, half = head_root(f"kn{h}"), HALF[h % 2]
                link(V.scalar_tensor_tensor(KN[:, h, :], KN[:, h, :], col("kn"), r, ALU.mult, ALU.mult))
                V.tensor_tensor(KR[half, h // 2, :], KPR[half, :], r[half], ALU.mult).then_inc(hs_done, 1)
            for k in range(3):
                V.tensor_scalar(QR[:, k, :], QR[:, k, :], col("qn", 1), None, ALU.mult).then_inc(gain_done, 1)
            for k in range(3):
                rope(9 + k, QR[:, k, :], COSM[:, :], SINM[:, :])
            attention(segments["l"])
            attention(segments["m1"])
            tail(1, 6, "ffn1")


def host_layout(inputs):
    f = {k: np.asarray(v) for k, v in inputs.items()}
    w_in, hgw, mlw = f["w_in"][0], f["hg_w_in_2"][0], f["mla_w_in_2"][0]
    sizes = (512, 512, 512, 512, 512, 64, 64, 512, 256, 32, 8, 1024, 1024)
    o = np.concatenate([[0], np.cumsum(sizes)])
    qa, ka, va, ga, qb, kb, vb, gb, iq, ik, iw, za, zb = (w_in[:, o[i]:o[i + 1]] for i in range(13))
    stream = np.zeros((NSLAB, P, SLAB), np.float32)

    def tiles(w):
        return w.reshape(-1, P, w.shape[1]).transpose(1, 0, 2)

    def feature(name, w):
        t = tiles(w)
        for a, n in enumerate(JOBS[name].slabs):
            part = t[:, 8 * a:8 * a + 8, :]
            stream[n, :, :part.shape[1] * P] = part.reshape(P, -1)

    def packed(name, ws):
        stream[JOBS[name].slabs[0], :, :P * JOBS[name].kts * len(ws)] = np.concatenate(
            [tiles(w) for w in ws], 1).reshape(P, -1)

    def token(name, w):
        t, slabs = tiles(w), JOBS[name].slabs
        per = t.shape[1] // len(slabs)
        for a, n in enumerate(slabs):
            part = t[:, per * a:per * a + per, :]
            stream[n, :, :per * w.shape[1]] = part.reshape(P, -1)

    def c(w, k):
        return w[:, P * k:P * k + P]

    token("vbiw", np.concatenate([vb, iw], 1))
    feature("iq0", c(iq, 0))
    feature("iq1", c(iq, 1))
    feature("ik", np.concatenate([ik] * 4, 1))
    feature("kb", np.concatenate([kb] * 2, 1))
    for name, w in (("qa", qa), ("ka", ka), ("qb", qb), ("ga", ga), ("gb", gb)):
        for k in range(4):
            feature(f"{name}{k}", c(w, k))
    token("va", va)
    for k in range(KD):
        feature(f"za{k}", c(za, k))
        feature(f"zb{k}", c(zb, k))
        packed(f"pab{k}", [c(f["w_branch_a"][0], k), c(f["w_branch_b"][0], k)])
        feature(f"o1_{k}", c(f["w_out"][0], k))
        for l in range(2):
            feature(f"wo{l}{k}", c(f["w_out_2"][l], k))
            feature(f"dn{l}{k}", c(f["w_down_2"][l], k))
    for l in range(2):
        kv = f["w_mem_kv_2"][l]
        for k in range(2):
            feature(f"mk{l}{k}", c(kv, k))
        token(f"mv{l}", kv[:, 256:])
        for k in range(FF):
            feature(f"ua{l}_{k}", c(f["w_up_2"][l], k))
            feature(f"ub{l}_{k}", c(f["w_up_2"][l], FF + k))
    for k in range(HG):
        feature(f"hq{k}", c(hgw, k))
        feature(f"hf{k}", c(hgw, HG + k))
        feature(f"hg{k}", c(hgw, 3 * HG + k))
    for k in range(2):
        token(f"hv{k}", hgw[:, 1536 + 384 * k:1920 + 384 * k])
        feature(f"qm0{k}", hgw[:, 3072 + P * k:3200 + P * k])
        feature(f"qm1{k}", mlw[:, 704 + P * k:832 + P * k])
        feature(f"ckv{k}", mlw[:, 384 + P * k:512 + P * k])
    for k in range(3):
        feature(f"cq{k}", c(mlw, k))
    feature("kpe", np.concatenate([mlw[:, 640:704]] * 2, 1))
    uq = f["mla_w_uq_2"][0].reshape(384, MLH, 192)
    ukv = f["mla_w_ukv_2"][0].reshape(256, MLH, 256)
    uqr = [uq[:, 2 * k:2 * k + 2, P:].reshape(384, P) for k in range(3)]
    for k in range(3):
        packed(f"uqn{k}", [uq[:, h, :P] for h in (2 * k, 2 * k + 1)])
    packed("uqr0", uqr[:2])
    packed("uqr1", uqr[2:])
    packed("ukn0", [ukv[:, h, :P] for h in range(4)])
    packed("ukn1", [ukv[:, h, :P] for h in range(4, MLH)])
    for k in range(2):
        token(f"uv{k}", ukv[:, 3 * k:3 * k + 3, P:].reshape(256, 384))

    def cols(v):
        return v.reshape(-1, P).T

    inv_m = (np.float32(10000.0) ** (-np.arange(32, dtype=np.float32) / np.float32(32))).astype(np.float32)
    pars = np.zeros((P, NCOL), np.float32)
    qn, kn = f["mla_q_norm_g_2"][0], f["mla_k_norm_g_2"][0]
    for name, v in (("norm_gain", cols(f["norm_gain"][0])), ("final_gain", cols(f["final_norm_gain"])),
                    ("mix0", cols(f["mix_norm_g_2"][0])), ("mix1", cols(f["mix_norm_g_2"][1])),
                    ("ffn0", cols(f["ffn_norm_g_2"][0])), ("ffn1", cols(f["ffn_norm_g_2"][1])),
                    ("mem0", cols(f["mem_norm_g_2"][0])), ("mem1", cols(f["mem_norm_g_2"][1])),
                    ("bm0", cols(f["b_merge"][0, 0])), ("bm1", cols(f["b_merge"][0, 1])),
                    ("mq0", cols(np.tile(f["mem_q_norm_g_2"][0], 2))), ("mq1", cols(np.tile(f["mem_q_norm_g_2"][1], 2))),
                    ("mk0", cols(np.tile(f["mem_k_norm_g_2"][0], 2))), ("mk1", cols(np.tile(f["mem_k_norm_g_2"][1], 2))),
                    ("lb", cols(f["hg_lb_logits_2"])), ("onorm", cols(f["hg_out_norm_g_2"][0])),
                    ("qa", cols(f["mla_qa_norm_g_2"][0])), ("kva", cols(f["mla_kva_norm_g_2"][0])),
                    ("qn", cols(np.concatenate([qn[:P], qn[P:], qn[P:]]))),
                    ("kn", cols(np.concatenate([kn[:P], kn[P:], kn[P:]]))),
                    ("inv", cols(np.tile(inv_m, 4))),
                    ("eps", np.tile(np.array([EPS, DH * EPS, 192 * EPS], np.float32), (P, 1)))):
        pars[:, COLS[name][0]:COLS[name][0] + COLS[name][1]] = v
    convp = np.zeros((P, 2, FF, 8), np.float32)
    for l in range(2):
        for half in range(2):
            for tap in range(3):
                convp[:, l, :, 4 * half + tap] = cols(f["conv_w_2"][l, tap, 2816 * half:2816 * half + 2816])
            convp[:, l, :, 4 * half + 3] = cols(f["conv_b_2"][l, 2816 * half:2816 * half + 2816])

    def rotation(head, rot):
        m, half = np.zeros((P, P), np.float32), rot // 2
        for b in range(0, P, head):
            for j in range(half):
                m[b + half + j, b + j] = -1.0
                m[b + j, b + half + j] = 1.0
        return m

    part, free = np.arange(P)[:, None], np.arange(P)[None, :]
    chb = np.where((part < CHUNK) & (free >= CHUNK), np.float32(NEG), np.float32(0))
    consts = np.stack([np.eye(P, dtype=np.float32), np.ones((P, P), np.float32),
                       (part // DH == free // DH).astype(np.float32), rotation(DH, 16), rotation(IDXD, 8),
                       rotation(DH, 64), chb], 1).astype(np.float32)

    def rope_table(head, rot):
        half = rot // 2
        inv = (np.float32(500000.0) ** (-np.arange(half, dtype=np.float32) / np.float32(half))).astype(np.float32)
        ang = (np.arange(TOK, dtype=np.float32)[None, :] * inv[:, None]).astype(np.float64)
        c_, s_ = np.ones((P, TOK), np.float32), np.zeros((P, TOK), np.float32)
        for b in range(0, P, head):
            for a in range(2):
                c_[b + half * a:b + half * a + half] = np.cos(ang)
                s_[b + half * a:b + half * a + half] = np.sin(ang)
        return c_, s_

    rope_tabs = np.stack([*rope_table(IDXD, 8), *rope_table(DH, 16)])
    c_ = np.arange(TOK)[None, :]
    at_ = 256 + np.minimum(part - c_ + TOK - P, 256)
    toep = f["rel_bias"][0][:, at_].reshape(4, 2, P, TOK).transpose(0, 2, 1, 3).copy()
    toep[:, :CHUNK, :, TOK - CHUNK:] = NEG
    s_, t_ = part, free
    levels = [(s_ // (2 * m) == t_ // (2 * m)) & (s_ // m % 2 == 0) & (t_ // m % 2 == 1) for m in LEVELS]
    masks8 = np.stack(levels + [s_ == t_], 1).astype(np.int32)
    resets = np.tile((np.arange(TOK) % P != 0).astype(np.float32), (P, 1))
    cz = np.where(c_ - (TOK - P) <= part, np.float32(0), np.float32(NEG)).astype(np.float32)
    xt = np.ascontiguousarray(f["x"][0].T).reshape(KD, P, TOK)
    memt = np.ascontiguousarray(f["mem_2"][0].T.reshape(KD, P, MEM).transpose(1, 0, 2))
    return dict(stream=stream, xt=xt, memt=memt, pars=pars, convp=convp, consts=consts, rope=rope_tabs,
                toep=toep, masks8=masks8, resets=resets, cz=cz, pos=f["positions_2"][0].astype(np.int32))


def kernel(**inputs):
    import concourse.bacc as _bacc
    from concourse.bass_utils import run_bass_kernel_spmd as _run

    nc = _bacc.Bacc("TRN2", target_bir_lowering=False, num_devices=1)
    arrays, args = {}, []
    for name, a in host_layout(inputs).items():
        a = np.ascontiguousarray(a)
        arrays[f"in_{name}_dram"] = a
        args.append(nc.dram_tensor(f"in_{name}_dram", a.shape, mybir.dt.from_np(a.dtype), kind="ExternalInput").ap())
    out = nc.dram_tensor("out_dram", (KD, P, TOK), F32, kind="ExternalOutput").ap()
    build(nc, *args, out)
    r = _run(nc, [arrays], core_ids=[0])
    got = r.results[0]["out_dram"]
    return got.reshape(1, D, TOK).transpose(0, 2, 1)
```

```python
from contextlib import ExitStack

import numpy as np

import concourse.bass as bass
from concourse import mybir

F32 = mybir.dt.float32
F32R = mybir.dt.float32r
I32 = mybir.dt.int32
I8 = mybir.dt.int8
ALU = mybir.AluOpType
ACT = mybir.ActivationFunctionType

P = 128
TOK = 512
NT = TOK // P
D = 1024
KD = D // P
CHUNK = 64
EPS = 1e-6
NEG = -1e30
TAKEN = -3e38
BARRED = -1e38
TOPK = 128
DH = 64
NHEAD = 8
IDXH = 8
IDXD = 32
MEM = 256
HG = 6
LEVELS = [64, 32, 16, 8, 4, 2, 1]
MLH = 6
FF = 22
RING = 4
SPLIT = 2
SLAB = 1024

COLS = {}


def _col(name, n):
    COLS[name] = (sum(c for _, c in COLS.values()), n)


for _name, _n in (("norm_gain", KD), ("final_gain", KD), ("mix0", KD), ("mix1", KD), ("ffn0", KD),
                  ("ffn1", KD), ("mem0", KD), ("mem1", KD), ("bm0", KD), ("bm1", KD), ("mq0", 1),
                  ("mq1", 1), ("mk0", 1), ("mk1", 1), ("lb", 3 * HG), ("onorm", 1), ("qa", 3),
                  ("kva", 2), ("qn", 2), ("kn", 2), ("inv", 1), ("eps", 3)):
    _col(_name, _n)
NCOL = sum(c for _, c in COLS.values())


class Job:

    def __init__(self, slabs, banks, kts, empties):
        self.slabs, self.banks, self.kts, self.empties = slabs, banks, kts, empties
        self.done = slabs[-1] + 1


def plan_stream():
    jobs, emptied, n, u = {}, [], 0, 0
    count = {"act": 0, "dve": 0}

    def add(name, nslab, nbank, kts, who):
        nonlocal n, u
        jobs[name] = Job(list(range(n, n + nslab)), list(range(u, u + nbank)), kts, who)
        n += nslab
        u += nbank
        for _ in range(nbank):
            count[who] += 1
            emptied.append((who, count[who]))

    for k in ("vbiw", "iq0", "iq1", "ik", "kb"):
        add(k, 1, 1, KD, "act")
    for k in range(4):
        add(f"qa{k}", 1, 1, KD, "act")
    for k in range(4):
        add(f"ka{k}", 1, 1, KD, "act")
    add("va", 4, NT, KD, "act")
    for g in ("qb", "ga", "gb"):
        for k in range(4):
            add(f"{g}{k}", 1, 1, KD, "act")
    for k in range(KD):
        add(f"za{k}", 1, 1, KD, "act")
    for k in range(KD):
        add(f"zb{k}", 1, 1, KD, "act")
        add(f"pab{k}", 1, 2, 4, "dve")
    for k in range(KD):
        add(f"o1_{k}", 1, 1, KD, "dve")
    for l in range(2):
        for k in range(2):
            add(f"mk{l}{k}", 1, 1, KD, "act")
        add(f"mv{l}", 2, 2, KD, "act")
    for k in range(HG):
        add(f"hf{k}", 1, 1, KD, "act")
    for k in range(HG):
        add(f"hq{k}", 1, 1, KD, "act")
    for k in range(2):
        add(f"hv{k}", 4, NT, KD, "act")
    for k in range(2):
        add(f"qm0{k}", 1, 1, KD, "act")
    for k in range(HG):
        add(f"hg{k}", 1, 1, KD, "act")

    def ffn(l):
        for k in range(KD):
            add(f"wo{l}{k}", 1, 1, KD, "dve")
        for k in range(FF):
            add(f"ua{l}_{k}", 1, 1, KD, "dve")
            add(f"ub{l}_{k}", 1, 1, KD, "dve")
        for k in range(KD):
            add(f"dn{l}{k}", 3, 1, FF, "dve")

    ffn(0)
    for k in range(3):
        add(f"cq{k}", 1, 1, KD, "act")
    for k in range(2):
        add(f"ckv{k}", 1, 1, KD, "act")
    add("kpe", 1, 1, KD, "act")
    for k in range(2):
        add(f"qm1{k}", 1, 1, KD, "act")
    for k in range(3):
        add(f"uqn{k}", 1, 2, 3, "act")
    add("uqr0", 1, 2, 3, "act")
    add("uqr1", 1, 1, 3, "act")
    add("ukn0", 1, 4, 2, "act")
    add("ukn1", 1, 2, 2, "act")
    for k in range(2):
        add(f"uv{k}", 1, NT, 2, "act")
    ffn(1)
    return jobs, emptied, n


JOBS, EMPTIED, NSLAB = plan_stream()
NSLAB = -(-(NSLAB + SPLIT) // RING) * RING

SQB = {0: 0, 1: KD, 3: 2 * KD}
ACC = {0: 0, 1: KD - 1, 2: 2 * (KD - 1), 3: 2 * KD - 1, 4: 3 * KD - 2, 5: 3 * KD - 1, 6: 3 * KD}
XLB = {0: 0, 1: KD, 3: 3 * KD, 4: 4 * KD, 5: 5 * KD, 6: 6 * KD}


def plan_heads():
    plan, idx, groups = {}, 0, {}
    for group, names, parts, m, nt in (("mk", [f"mk{l}{k}" for l in range(2) for k in range(2)], 1, 2, MEM // P),
                                       ("qm0", ["qm00", "qm01"], 1, 2, NT), ("ho", [f"ho{h}" for h in range(HG)], 1, 1, NT),
                                       ("cq", ["cq"], 3, 1, NT), ("ckv", ["ckv"], 2, 1, NT),
                                       ("qm1", ["qm10", "qm11"], 1, 2, NT), ("qn", [f"qn{h}" for h in range(MLH)], 2, 1, NT),
                                       ("kn", [f"kn{h}" for h in range(MLH)], 1, 1, NT)):
        groups[group] = (len(groups), names, m, nt)
        for a, name in enumerate(names):
            if group == "qn":
                plan[name] = (len(plan), [idx + a, idx + MLH + a // 2])
            else:
                plan[name] = (len(plan), list(range(idx + parts * a, idx + parts * a + parts)))
        idx = plan[names[-1]][1][-1] + 1
    return plan, groups


HEADS, GROUPS = plan_heads()
XTB = XLB

_t1 = 6.28125
_t2 = float(np.round((2 * np.pi - _t1) * 2 ** 20) / 2 ** 20)
TURN = (_t1, _t2, float(2 * np.pi - _t1 - _t2))
HALFTURN = 3.1415925
ROUND = 12582912.0


def build(nc, stream, xt_in, memt_in, pars, convp, consts, rope_tabs, toep, masks8, resets, cz_in, pos_in, out):
    with ExitStack() as ctx:
        BASE = 16512
        KB = 1024

        def at(name, shape, kb, dt=F32):
            return nc.alloc_sbuf_tensor_at(name, shape, dt, offset=BASE + int(kb * KB))

        def bank(name):
            return ctx.enter_context(nc.psum_tensor(name, [P, TOK], F32))

        def sem(name):
            return ctx.enter_context(nc.semaphore(name))

        X = at("X", [P, KD, TOK], 0)
        XH = at("XH", [P, KD, TOK], 16, F32R)
        XL = at("XL", [P, KD, TOK], 32, F32R)
        RAW = at("RAW", [P, RING, SLAB], 48)
        WH = at("WH", [P, SPLIT, SLAB], 64, F32R)
        WL = at("WL", [P, SPLIT, SLAB], 72, F32R)
        CONST = at("CONST", [P, 7, P], 80)
        IDENT, ONES, BONES, ROTB, ROTI, ROTM, CHB = (CONST[:, i, :] for i in range(7))
        CZ = at("CZ", [P, TOK], 84)
        PAR = at("PAR", [P, NCOL], 86)
        LBC = at("LBC", [P, 6 * HG], 87)
        CW = at("CW", [P, 2, FF, 8], 88)
        SB = at("SB", [P, 2, TOK], 90)
        PB = at("PB", [P, 3, TOK], 94)
        PT = at("PT", [P, 2, TOK], 100)
        SQ = at("SQ", [P, 2, TOK], 104)
        RS = at("RS", [P, TOK], 108)
        TMP = at("TMP", [P, 2, TOK], 110)
        ST = at("ST", [P, 32], 114)
        NR = at("NR", [P, NT, 1], 114.25)
        HR = at("HR", [P, 2, 24, 1], 114.375)
        KS = at("KS", [P, 1, NT], 114.625)
        MX8 = at("MX8", [P, 8], 114.75)
        A0 = 115
        QA = at("QA", [P, 4, TOK], A0 + 0)
        KA = at("KA", [P, 4, TOK], A0 + 8)
        VA = at("VA", [P, NT, 512], A0 + 16)
        QB = at("QB", [P, 4, TOK], A0 + 24)
        GA = at("GA", [P, 4, TOK], A0 + 32)
        GB = at("GB", [P, 4, TOK], A0 + 40)
        TP = at("TP", [P, 2, 2, TOK], A0 + 48)
        IQ = at("IQ", [P, 2, TOK], A0 + 48)
        IK = at("IK", [P, TOK], A0 + 52)
        COSI = at("COSI", [P, TOK], A0 + 54)
        SINI = at("SINI", [P, TOK], A0 + 56)
        KBT = at("KBT", [P, TOK], A0 + 58)
        COSB = at("COSB", [P, TOK], A0 + 60)
        SINB = at("SINB", [P, TOK], A0 + 62)
        VB = at("VB", [P, NT, DH], A0 + 64)
        IW = at("IW", [P, NT, IDXH], A0 + 65)
        MB = at("MB", [P, 1152], A0 + 66)
        ZA = at("ZA", [P, KD, TOK], A0 + 71)
        YAH = at("YAH", [P, 4, TOK], A0 + 0, F32R)
        YAL = at("YAL", [P, 4, TOK], A0 + 8, F32R)
        YBL = at("YBL", [P, 4, TOK], A0 + 16, F32R)
        YBH = at("YBH", [P, 4, TOK], A0 + 24, F32R)
        MH = at("MH", [P, KD, TOK], A0 + 32, F32R)
        ML = at("ML", [P, KD, TOK], A0 + 48, F32R)
        MRAW = at("MRAW", [P, KD, MEM], A0 + 0)
        MKT = [at(f"MKT{l}", [P, 2, MEM], A0 + 84 + 4 * l) for l in range(2)]
        MVT = [at(f"MVT{l}", [P, 2, MEM], A0 + 86 + 4 * l) for l in range(2)]
        YH = at("YH", [P, KD, TOK], A0 + 0, F32R)
        YL = at("YL", [P, KD, TOK], A0 + 16, F32R)
        HK = at("HK", [P, HG, TOK], A0 + 0)
        HB = at("HB", [P, HG, TOK], A0 + 16)
        HQ = at("HQ", [P, HG, TOK], A0 + 32)
        HV = at("HV", [P, NT, HG * P], A0 + 44)
        HGT = at("HGT", [P, HG, TOK], A0 + 56)
        QM = at("QM", [P, 2, TOK], A0 + 68)
        MSK = at("MSK", [P, 8, P], A0 + 72, I8)
        MSKI = at("MSKI", [P, 8, P], A0 + 76, I32)
        AX = at("AX", [P, 6, P], A0 + 73)
        QX = at("QX", [P, TOK], A0 + 76)
        KX = at("KX", [P, TOK], A0 + 78)
        KX2 = at("KX2", [P, 3, P], A0 + 80)
        RESET = at("RESET", [P, TOK], A0 + 82)
        GH = at("GH", [P, FF, TOK], A0 + 0, F32R)
        GL = at("GL", [P, FF, TOK], A0 + 44, F32R)
        YH1 = at("YH1", [P, KD, TOK], A0 + 0, F32R)
        YL1 = at("YL1", [P, KD, TOK], A0 + 16, F32R)
        QN = at("QN", [P, MLH, TOK], A0 + 0)
        KN = at("KN", [P, MLH, TOK], A0 + 16)
        QR = at("QR", [P, 3, TOK], A0 + 32)
        KR = at("KR", [P, 3, TOK], A0 + 38)
        MV = at("MV", [P, NT, MLH * P], A0 + 44)
        CQH = at("CQH", [P, 3, TOK], A0 + 44, F32R)
        CQL = at("CQL", [P, 3, TOK], A0 + 50, F32R)
        QM1 = at("QM1", [P, 2, TOK], A0 + 56)
        CQ = at("CQ", [P, 3, TOK], A0 + 60)
        CKV = at("CKV", [P, 2, TOK], A0 + 66)
        KPE = at("KPE", [P, TOK], A0 + 70)
        CKH = at("CKH", [P, 2, TOK], A0 + 72, F32R)
        CKL = at("CKL", [P, 2, TOK], A0 + 76, F32R)
        COSM = at("COSM", [P, TOK], A0 + 80)
        SINM = at("SINM", [P, TOK], A0 + 82)
        POSI = at("POSI", [P, TOK], A0 + 84, I32)

        KPR = at("KPR", [P, TOK], A0 + 60)
        HALF = [slice(0, DH), slice(DH, P)]
        DB = [bank(f"DB{i}") for i in range(4)]
        SC = [bank(f"SC{i}") for i in range(2)]
        TB = bank("TB")
        OB = bank("OB")
        RB = [TB, OB]
        RH = [RS, SB[:, 1, :]]
        SUMS_AT = {"mk": (SC[0], 0), "qm0": (TB, 0), "ho": (TB, 16), "cq": (SC[0], 0), "ckv": (SC[0], 4),
                   "qm1": (SC[0], 8), "qn": (SC[0], 24), "kn": (SC[0], 48)}
        QN0 = HEADS["qn0"][1][0]

        def square_at(idx):
            if idx < QN0:
                return SQ[:, idx % 2, :]
            return (SQ[:, 0, :], SQ[:, 1, :], PB[:, 0, :], PB[:, 1, :])[(idx - QN0) % 4]

        def col(name, i=0):
            c = COLS[name][0] + i
            return PAR[:, c:c + 1]

        raw_in = [sem(f"raw_in{i}") for i in range(RING)]
        hi_done = sem("hi_done")
        lo_done = sem("lo_done")
        slab_used = sem("slab_used")
        act_emptied = sem("act_emptied")
        dve_emptied = sem("dve_emptied")
        consts_in = sem("consts_in")
        tabs_in = sem("tabs_in")
        x_in = [sem(f"x_in{k}") for k in range(KD)]
        mem_in = sem("mem_in")
        toep_in = [sem(f"toep_in{i}") for i in range(2)]
        hg_in = sem("hg_in")
        pos_ready = sem("pos_ready")
        sq_done = sem("sq_done")
        ss_done = sem("ss_done")
        std_done = sem("std_done")
        rs_ready = sem("rs_ready")
        rs_spread = sem("rs_spread")
        hs_bc = sem("hs_bc")
        hs_rb = sem("hs_rb")
        kpe_sq = sem("kpe_sq")
        kpe_ss = sem("kpe_ss")
        kn_sum = sem("kn_sum")
        vb_turned = sem("vb_turned")
        acc_done = sem("acc_done")
        xt_done = sem("xt_done")
        xh_done = sem("xh_done")
        xl_done = sem("xl_done")
        x_new = sem("x_new")
        rot_done = sem("rot_done")
        roped = sem("roped")
        ilog_done = sem("ilog_done")
        irelu_done = sem("irelu_done")
        iacc_done = sem("iacc_done")
        qk_done = sem("qk_done")
        bm_done = sem("bm_done")
        exp_done = sem("exp_done")
        nrm_done = sem("nrm_done")
        tr_done = sem("tr_done")
        pt_done = sem("pt_done")
        pv_done = sem("pv_done")
        o_out = sem("o_out")
        zb_used = sem("zb_used")
        hs_sq = sem("hs_sq")
        hs_ss = sem("hs_ss")
        hs_std = sem("hs_std")
        hs_done = sem("hs_done")
        lb_e = sem("lb_e")
        lb_done = sem("lb_done")
        hf_ln = sem("hf_ln")
        lv_e = sem("lv_e")
        lv_x = sem("lv_x")
        lv_w = sem("lv_w")
        lv_mm = sem("lv_mm")
        lv_cp = sem("lv_cp")
        decays_ready = sem("decays_ready")
        ho_mm = sem("ho_mm")
        ho_out = sem("ho_out")
        cv_i = sem("cv_i")
        cv_c = sem("cv_c")
        cv_s = sem("cv_s")
        g_done = sem("g_done")
        ang_done = sem("ang_done")
        sin_done = sem("sin_done")
        sin_neg = sem("sin_neg")
        dve_chain = sem("dve_chain")
        act_chain = sem("act_chain")
        arena_free = sem("arena_free")
        gain_done = sem("gain_done")
        cv_g = sem("cv_g")
        hg_silu = sem("hg_silu")
        reset_ready = sem("reset_ready")
        out_done = sem("out_done")

        OUT2 = (OB, DB[3])

        def steps_a():
            for p in range(4):
                for i in range(NT):
                    for e in range(2):
                        r = slice(DH * e, DH * e + DH)
                        w = P * (i + 1)
                        h = 2 * p + e
                        yield dict(qk=[(QA[r, p, P * i:P * i + P], KA[r, p, 0:w])], w=w,
                                   bias=TP[:, p % 2, e, TOK - w:TOK],
                                   v=[VA[:, s, DH * h:DH * h + DH] for s in range(i + 1)],
                                   bank=OUT2[p % 2], o=OUT2[p % 2][r, P * i:P * i + P], first=(i == 0 and e == 0), last=(i == NT - 1 and e == 1),
                                   kind="a", grp=p)

        def steps_b():
            for p in range(4):
                for i in range(NT):
                    for e in range(2):
                        r = slice(DH * e, DH * e + DH)
                        w = P * (i + 1)
                        off = {1: 0, 2: 256, 3: 640}.get(i, 0)
                        yield dict(qk=[(QB[r, p, P * i:P * i + P], KBT[r, 0:w])], w=w,
                                   bias=CHB if i == 0 else MB[:, off:off + w],
                                   v=[VB[:, s, :] for s in range(i + 1)],
                                   bank=OUT2[p % 2], o=OUT2[p % 2][r, P * i:P * i + P], first=(i == 0 and e == 0), last=(i == NT - 1 and e == 1),
                                   kind="b", grp=p)

        def steps_m(l):
            q = QM if l == 0 else QM1
            for p in range(2):
                for i in range(NT):
                    for e in range(2):
                        r = slice(DH * e, DH * e + DH)
                        h = 2 * p + e
                        yield dict(qk=[(q[r, p, P * i:P * i + P], MKT[l][r, p, :])], w=MEM,
                                   bias=CZ[:, 0:MEM],
                                   v=[MVT[l][:, s, DH * h:DH * h + DH] for s in range(2)],
                                   bank=OB, o=OB[r, P * i:P * i + P], first=(i == 0 and e == 0), last=(i == NT - 1 and e == 1),
                                   kind=f"m{l}", grp=p)

        def steps_l():
            for h in range(MLH):
                r = slice(DH * (h % 2), DH * (h % 2) + DH)
                for i in range(NT):
                    w = P * (i + 1)
                    yield dict(qk=[(QN[:, h, P * i:P * i + P], KN[:, h, 0:w]),
                                   (QR[r, h // 2, P * i:P * i + P], KR[r, h // 2, 0:w])], w=w,
                               bias=CZ[:, TOK - w:TOK],
                               v=[MV[:, s, P * h:P * h + P] for s in range(i + 1)],
                               bank=OUT2[h % 2], o=OUT2[h % 2][:, P * i:P * i + P], first=(i == 0), last=(i == NT - 1),
                               kind="l", grp=h)

        segments, g, grp = {}, 0, 0
        for name, it in (("ab", list(steps_a()) + list(steps_b())), ("m0", list(steps_m(0))),
                         ("l", list(steps_l())), ("m1", list(steps_m(1)))):
            for s in it:
                s["g"], s["group"] = g, grp
                g += 1
                grp += s["last"]
            two, first_group = name in ("ab", "l"), it[0]["group"]
            for s in it:
                s["left"] = s["group"] - (two and s["group"] > first_group)
            segments[name] = it

        block = ctx.enter_context(nc.Block())

        @block.sync
        def _(sp):
            for k in range(0, KD, 2):
                sp.dma_start(X[:, k, :], xt_in[k]).then_inc(x_in[k], 16)
            for j in range(RING):
                sp.dma_start(RAW[:, j, :], stream[j]).then_inc(raw_in[j], 16)
            for i, t in enumerate((COSI, SINI, COSB, SINB)):
                sp.dma_start(t[:, :], rope_tabs[i]).then_inc(tabs_in, 16)
            sp.dma_start(CZ[:, :], cz_in).then_inc(tabs_in, 16)
            sp.dma_start(CW[:, :, :, :], convp).then_inc(tabs_in, 16)
            with sp.Fori(1, NSLAB // RING) as it:
                for j in range(RING):
                    sp.wait_ge(lo_done, it * RING + (j - RING + 1))
                    sp.dma_start(RAW[:, j, :], stream[bass.ds(it * RING + j, 1)].rearrange("o p n -> (o p) n")
                                 ).then_inc(raw_in[j], 16)
            for m in range(KD):
                sp.wait_ge(dve_emptied, EMPTIED[JOBS[f"dn1{m}"].banks[0]][1])
                sp.dma_start(out[m], X[:, m, :]).then_inc(out_done, 16)
            sp.wait_ge(out_done, 16 * KD)

        @block.gpsimd
        def _(pool):
            def low(j, n):
                s = j % SPLIT
                pool.wait_ge(hi_done, n + 1)
                nc.gpsimd.tensor_tensor(WL[:, s, :], RAW[:, j, :], WH[:, s, :].bitcast(F32),
                                        ALU.subtract).then_inc(lo_done, 1)

            def lows(first, end):
                a, b = -(-first // RING), end // RING
                for n in range(first, a * RING):
                    low(n % RING, n)
                with pool.Fori(a, b) as it:
                    for j in range(RING):
                        low(j, it * RING + j)
                for n in range(b * RING, end):
                    low(n % RING, n)

            s0 = JOBS["qm00"].slabs[0]
            lows(0, s0 + 2)
            slabs = [[], [2, 3], [4, 5], [6], [7], [8]]
            pool.wait_ge(decays_ready, 1)
            for h in range(HG):
                b = HB[:, h, :]
                for l in range(8):
                    e = SB[:, l % 2, :]
                    if l >= 2:
                        pool.wait_ge(lv_w, 10 * h + l - 1)
                    elif h:
                        pool.wait_ge(lv_w, 10 * h - 3 * (l == 0))
                    if l < 7:
                        m = LEVELS[l]
                        bv = b.rearrange("p (n s m) -> p n s m", s=2, m=m)
                        ev = e.rearrange("p (n s m) -> p n s m", s=2, m=m)
                        ref = bv[:, :, 0, m - 1:m].broadcast_to([P, TOK // (2 * m), m])
                        nc.gpsimd.tensor_tensor(ev[:, :, 1, :], bv[:, :, 1, :], ref, ALU.subtract)
                        nc.gpsimd.tensor_tensor(ev[:, :, 0, :], ref, bv[:, :, 0, :], ALU.subtract).then_inc(lv_e, 1)
                    else:
                        bv = b.rearrange("p (n m) -> p n m", m=P)
                        nc.gpsimd.tensor_tensor(e.rearrange("p (n m) -> p n m", m=P),
                                                bv[:, :, P - 1:P].broadcast_to([P, NT, P]), bv, ALU.subtract).then_inc(lv_e, 1)
                    if l == 1:
                        for n in slabs[h]:
                            low((s0 + n) % RING, s0 + n)
            lows(s0 + 9, NSLAB)

        @block.tensor
        def _(pe):
            mm = nc.tensor.matmul

            def wait_empty(u):
                if u >= 4:
                    who, c = EMPTIED[u - 4]
                    pe.wait_ge(act_emptied if who == "act" else dve_emptied, c)

            def feature_job(*args, **kw):
                for _ in feature_tiles(*args, **kw):
                    pass

            def feature_tiles(name, hi, lo, n=TOK, xready=None, inputs=None):
                job = JOBS[name]
                u = job.banks[0]
                wait_empty(u)
                o = DB[u % 4][:, 0:n]
                for k in range(job.kts):
                    sl = job.slabs[k // 8]
                    s, c = sl % SPLIT, slice(P * (k % 8), P * (k % 8) + P)
                    if k % 8 == 0:
                        pe.wait_ge(lo_done, sl + 1)
                    if xready is not None:
                        pe.wait_ge(xl_done, xready + k + 1)
                    if inputs is not None:
                        pe.wait_ge(*inputs(k))
                    mm(o, WH[:, s, c], hi(k), start=(k == 0), stop=False)
                    mm(o, WH[:, s, c], lo(k), start=False, stop=False)
                    last = mm(o, WL[:, s, c], hi(k), start=False, stop=(k == job.kts - 1))
                    if k % 8 == 7 or k == job.kts - 1:
                        last.then_inc(slab_used, 1)
                    yield

            def packed_job(name, operands):
                for _ in packed_tiles(name, operands):
                    pass

            def packed_tiles(name, operands):
                job = JOBS[name]
                sl = job.slabs[0]
                s = sl % SPLIT
                pe.wait_ge(lo_done, sl + 1)
                for a, (hi, lo) in enumerate(operands):
                    wait_empty(job.banks[a])
                    o = DB[job.banks[a] % 4][:, :]
                    for k in range(job.kts):
                        i = a * job.kts + k
                        c = slice(P * i, P * i + P)
                        mm(o, WH[:, s, c], hi(k), start=(k == 0), stop=False)
                        mm(o, WH[:, s, c], lo(k), start=False, stop=False)
                        last = mm(o, WL[:, s, c], hi(k), start=False, stop=(k == job.kts - 1))
                    if a == len(operands) - 1:
                        last.then_inc(slab_used, 1)
                    yield

            def token_job(*args, **kw):
                for _ in token_tiles(*args, **kw):
                    pass

            def token_tiles(name, hi, lo, n, tiles=NT, xready=None):
                job = JOBS[name]
                per = job.kts // len(job.slabs)
                for j, sl in enumerate(job.slabs):
                    pe.wait_ge(lo_done, sl + 1)
                    s = sl % SPLIT
                    for kk in range(per):
                        k = j * per + kk
                        if xready is not None:
                            pe.wait_ge(xl_done, xready + k + 1)
                        for t in range(tiles):
                            if k == 0:
                                wait_empty(job.banks[t])
                            o = DB[job.banks[t] % 4][:, 0:n]
                            c, ts = slice(n * kk, n * kk + n), slice(P * t, P * t + P)
                            mm(o, hi(k)[:, ts], WH[:, s, c], start=(k == 0), stop=False)
                            mm(o, lo(k)[:, ts], WH[:, s, c], start=False, stop=False)
                            last = mm(o, hi(k)[:, ts], WL[:, s, c], start=False, stop=(k == job.kts - 1))
                        if kk == per - 1:
                            last.then_inc(slab_used, 1)
                        yield

            def xh(k):
                return XH[:, k, :]

            def xl(k):
                return XL[:, k, :]

            def sum_cols(o, sq, mat, start=True, stop=True, step=None):
                m, nt = mat.shape[-1], sq.shape[-1] // P
                for t in range(nt):
                    c = t * (step or m)
                    last = mm(o[:, c:c + m], sq[:, P * t:P * t + P], mat, start=start and t == 0,
                              stop=stop and t == nt - 1)
                return last

            def spread(o, src):
                for t in range(src.shape[-1] // P):
                    last = mm(o[:, P * t:P * t + P], src[:, P * t:P * t + P], IDENT, start=True, stop=True)
                return last

            def norm_sum(q, n=TOK):
                pe.wait_ge(acc_done, ACC[q] + (KD - 1 if q in SQB else 1))
                sum_cols(SC[0], PB[:, 0 if q in SQB else 2, 0:n], ONES[:, 0:1]).then_inc(ss_done, 1)

            def norm_spread(q, n=TOK):
                pe.wait_ge(rs_ready, q + 1)
                spread(SC[1], RS[:, 0:n]).then_inc(rs_spread, 1)

            def attention(seg, tb_read=None, beside=None, bank_free=None):
                n = len(seg)
                for k in range(n + 3):
                    if beside is not None and k >= 3 and k % 2 == 1:
                        next(beside, None)
                    if k < n:
                        s = seg[k]
                        if s["g"] >= 2:
                            pe.wait_ge(bm_done, s["g"] - 1)
                        for a, (l, r) in enumerate(s["qk"]):
                            last = mm(SC[s["g"] % 2][:, 0:s["w"]], l, r, start=(a == 0), stop=(a == len(s["qk"]) - 1))
                        last.then_inc(qk_done, 1)
                    if 2 <= k < n + 2:
                        s = seg[k - 2]
                        if tb_read is not None and k == 2:
                            pe.wait_ge(*tb_read)
                        pe.wait_ge(nrm_done, s["g"] + 1)
                        if s["g"]:
                            pe.wait_ge(pt_done, s["g"])
                        for t in range(s["w"] // P):
                            last = nc.tensor.transpose(TB[:, P * t:P * t + P], PB[:, s["g"] % 3, P * t:P * t + P], IDENT)
                        last.then_inc(tr_done, 1)
                    if 3 <= k < n + 3:
                        s = seg[k - 3]
                        pe.wait_ge(pt_done, s["g"] + 1)
                        if s["first"] and s["left"]:
                            pe.wait_ge(o_out, s["left"])
                        if s["first"] and k < 40 and bank_free is not None:
                            pe.wait_ge(*bank_free)
                        nv = s["w"] // P
                        for t in range(nv):
                            last = mm(s["o"], s["v"][t], PT[:, s["g"] % 2, P * t:P * t + P], start=(t == 0), stop=(t == nv - 1))
                        last.then_inc(pv_done, 1)

            def rotate(r, mat, src, ready):
                pe.wait_ge(*ready)
                if r >= 2:
                    pe.wait_ge(roped, r - 1 if r < 8 else r)
                mm(RB[r % 2 if r < 8 else 0][:, :], mat, src, start=True, stop=True).then_inc(rot_done, 1)

            def emptied(name):
                return act_emptied, EMPTIED[JOBS[name].banks[-1]][1]

            def head_sum(group, a, part=0):
                q0, names, m, nt = GROUPS[group]
                bank_, c0 = SUMS_AT[group]
                idxs = HEADS[names[a]][1]
                c = c0 + m * nt * a
                o, idx = bank_[:, c:c + m * nt], idxs[part]
                mat = BONES[:, 0:P:DH] if m == 2 else ONES[:, 0:1]
                sq = (TMP[:, a % 2, :] if group in ("qm0", "ho") else square_at(idx))[:, 0:P * nt]
                pe.wait_ge(hs_sq, idx + 1)
                if group == "qn":
                    o = bank_[:, c0 + 8 * (a // 2) + (a % 2) * (part == 0):c0 + 8 * (a // 2) + 8]
                    mat = BONES[:, 0:P:DH] if part else mat
                    sum_cols(o, sq, mat, part == 0 and a == 0, part == 1 and a == MLH - 2, 2).then_inc(hs_ss, 1)
                else:
                    sum_cols(o, sq, mat, part == 0, part == len(idxs) - 1).then_inc(hs_ss, 1)

            def head_spread(name, bank_=None):
                q = HEADS[name][0]
                pe.wait_ge(hs_bc, q + 1)
                if q >= 2 and name[:2] != "ho":
                    pe.wait_ge(hs_done, q - 1)
                group = name[:2] if name[:2] in GROUPS else name[:3] if name[:3] in GROUPS else name
                n = P * GROUPS[group][3]
                src = HB[:, int(name[2]), :] if group == "ho" else (RS, RESET)[q % 2] if group == "qm0" else RH[q % 2]
                spread(bank_ if bank_ is not None else (SC[1], OB)[q % 2], src[:, 0:n]).then_inc(hs_rb, 1)

            pe.wait_ge(consts_in, 16 * 2)
            norm_sum(0)
            norm_spread(0)
            feature_job("vbiw", xh, xl, xready=0)
            feature_job("iq0", xh, xl)
            pe.wait_ge(*emptied("vbiw"))
            for t in range(NT):
                last = nc.tensor.transpose(TB[:, 128 * t:128 * t + 72], SQ[0:72, 1, P * t:P * t + P], IDENT[0:72, 0:72])
            last.then_inc(vb_turned, 1)
            for k in ("iq1", "ik", "kb"):
                feature_job(k, xh, xl)
            pe.wait_ge(tabs_in, 16 * 6)
            pe.wait_ge(vb_turned, 2)
            rotate(0, ROTI, IQ[:, 0, :], emptied("iq0"))
            rotate(1, ROTI, IQ[:, 1, :], emptied("iq1"))
            feature_job("qa0", xh, xl)
            rotate(2, ROTI, IK[:, :], emptied("ik"))
            rotate(3, ROTB, KBT[:, :], emptied("kb"))
            feature_job("qa1", xh, xl)
            n = 0
            fill = ["qa2", "qa3", "ka0", "ka1", "ka2", "ka3"]
            pe.wait_ge(roped, 3)
            for i in range(1, NT):
                for h in range(IDXH):
                    if n >= 2:
                        pe.wait_ge(irelu_done, n - 1)
                    r = slice(IDXD * (h % 4), IDXD * (h % 4) + IDXD)
                    mm(SC[n % 2][:, 0:P * (i + 1)], IQ[r, h // 4, P * i:P * i + P], IK[r, 0:P * (i + 1)],
                       start=True, stop=True).then_inc(ilog_done, 1)
                    n += 1
                    if n % 4 == 0:
                        feature_job(fill[n // 4 - 1], xh, xl)
            token_job("va", xh, xl, 512)
            for g in ("qb", "ga", "gb"):
                for k in range(4):
                    feature_job(f"{g}{k}", xh, xl)
            for k in range(KD):
                feature_job(f"za{k}", xh, xl)
                if k >= 4:
                    rotate(k, ROTB, QB[:, k - 4, :], emptied(f"qb{k - 4}"))
            pe.wait_ge(roped, 8)
            pe.wait_ge(irelu_done, n)
            pe.wait_ge(*emptied("va"))
            attention(segments["ab"], bank_free=emptied("za7"))
            assert JOBS["zb0"].banks[0] % 4 != 3
            for k in range(KD):
                feature_job(f"zb{k}", xh, xl)
                if k == 0:
                    pe.wait_ge(o_out, 8)
                packed_job(f"pab{k}", [(lambda j: YAH[:, j, :], lambda j: YAL[:, j, :]),
                                       (lambda j: YBH[:, j, :], lambda j: YBL[:, j, :])])
            pe.drain().then_inc(arena_free, 1)
            for k in range(KD):
                feature_job(f"o1_{k}", lambda j: MH[:, j, :], lambda j: ML[:, j, :],
                            inputs=(lambda j: (zb_used, j + 1)) if k == 0 else None)
                if k == 2:
                    norm_sum(1, MEM)
                if k == 3:
                    norm_spread(1, MEM)
            norm_sum(2)
            pe.wait_ge(xt_done, XTB[3])
            norm_spread(2)
            def memory_halves(l):
                return lambda j: XH[:, j, MEM * l:MEM * l + MEM], lambda j: XL[:, j, MEM * l:MEM * l + MEM]

            for k in range(2):
                feature_job(f"mk0{k}", *memory_halves(0), n=MEM, xready=XLB[1])
            token_job("mv0", *memory_halves(0), MEM, tiles=2)
            feature_job("mk10", *memory_halves(1), n=MEM, xready=XLB[1] + KD)
            feature_job("mk11", *memory_halves(1), n=MEM)
            norm_sum(3)
            token_job("mv1", *memory_halves(1), MEM, tiles=2)
            pe.drain().then_inc(arena_free, 1)
            pe.wait_ge(x_new, KD)
            norm_spread(3)
            for k in range(HG):
                feature_job(f"hf{k}", xh, xl, xready=XLB[3] if k == 0 else None)
                if k == 1:
                    for a in range(4):
                        head_sum("mk", a)
                if k == 2:
                    for a in range(4):
                        head_spread(f"mk{a // 2}{a % 2}")
            for k in range(HG):
                feature_job(f"hq{k}", xh, xl)
            for k in range(2):
                token_job(f"hv{k}", xh, xl, 384)
            fill = ["qm00", "qm01"] + [f"hg{k}" for k in range(HG)]
            n = 0

            pe.wait_ge(*emptied("hv1"))
            for h in range(HG):
                for l in range(10):
                    if h == 1 and l in (0, 1):
                        head_sum("qm0", l)
                    elif h >= 2 and l == 2:
                        head_sum("ho", h - 2)
                    if h == HG - 1 and l in (4, 5):
                        pe.wait_ge(*emptied("hg4"))
                        head_spread(f"qm0{l - 4}", DB[(JOBS["hg5"].banks[0] + l - 3) % 4])
                    if n >= 2:
                        pe.wait_ge(lv_cp, n - 1)
                    o = SC[n % 2]
                    pe.wait_ge(lv_w, n + 1)
                    for t in range(NT):
                        c = slice(P * t, P * t + P)
                        if l < 7:
                            last = mm(o[:, c], PB[:, n % 3, c], PB[:, n % 3, c], start=True, stop=True)
                        elif l == 7:
                            last = mm(o[:, c], HK[:, h, c], HQ[:, h, c], start=True, stop=True)
                    if l == 8:
                        for a, (j, i) in enumerate(((0, 1), (1, 2), (2, 3))):
                            mm(o[:, P * a:P * a + P], KX[:, P * j:P * j + P], QX[:, P * i:P * i + P], start=True, stop=True)
                        last = mm(o[:, 3 * P:4 * P], KX2[:, 0, :], QX[:, 2 * P:3 * P], start=True, stop=True)
                    if l == 9:
                        mm(o[:, 0:P], KX2[:, 1, :], QX[:, 3 * P:4 * P], start=True, stop=True)
                        last = mm(o[:, P:2 * P], KX2[:, 2, :], QX[:, 3 * P:4 * P], start=True, stop=True)
                    last.then_inc(lv_mm, 1)
                    n += 1
                    if l == 0:
                        beside = [feature_tiles(fill.pop(0), xh, xl) for _ in range(2 if h < 2 else 1)]
                    for job in beside if l < 8 else ():
                        next(job)
                        if l == 7:
                            next(job, None)
                pe.wait_ge(lv_cp, n)
                if h:
                    pe.wait_ge(ho_out, h)
                slot = {(0, 1): 0, (1, 2): 1, (2, 3): 2, (0, 2): 3, (1, 3): 4, (0, 3): 5}
                for i in range(NT):
                    for j in range(i + 1):
                        a = PT[:, h % 2, P * i:P * i + P] if j == i else AX[:, slot[j, i], :]
                        last = mm(OB[:, P * i:P * i + P], HV[:, j, P * h:P * h + P], a, start=(j == 0), stop=(j == i))
                last.then_inc(ho_mm, 1)
            assert not fill

            def head_spreads():
                pe.wait_ge(*emptied("hg5"))
                for h in range(HG):
                    if h >= 4:
                        pe.wait_ge(hs_done, HEADS[f"ho{h - 4}"][0] + 1)
                    head_spread(f"ho{h}", DB[h % 4])
                    yield

            head_sum("ho", HG - 2)
            head_sum("ho", HG - 1)
            pe.wait_ge(hs_done, HEADS["qm01"][0] + 1)
            attention(segments["m0"], (hs_std, HEADS["ho5"][0] + 1), head_spreads())

            def tail(l, hi, lo, ni, inputs):
                for k in range(KD):
                    feature_job(f"wo{l}{k}", hi, lo, inputs=inputs if k == 0 else None)
                pe.drain().then_inc(arena_free, 1)
                norm_sum(ni)
                norm_spread(ni)
                ja = JOBS[f"ua{l}_0"]
                s0, u0 = ja.slabs[0], ja.banks[0]
                d0 = EMPTIED[u0 - 4][1]
                with pe.Fori(0, FF // 2) as it:
                    for j in range(4):
                        pe.wait_ge(dve_emptied, it * 4 + (d0 + j))
                        pe.wait_ge(lo_done, it * 4 + (s0 + j + 1))
                        s = (s0 + j) % SPLIT
                        for k in range(KD):
                            c = slice(P * k, P * k + P)
                            o = DB[(u0 + j) % 4][:, :]
                            if j == 0:
                                pe.wait_ge(xl_done, XLB[ni] + k + 1)
                            mm(o, WH[:, s, c], xh(k), start=(k == 0), stop=False)
                            mm(o, WH[:, s, c], xl(k), start=False, stop=False)
                            last = mm(o, WL[:, s, c], xh(k), start=False, stop=(k == KD - 1))
                        last.then_inc(slab_used, 1)
                jd = JOBS[f"dn{l}0"]
                s0, u0 = jd.slabs[0], jd.banks[0]
                d0 = EMPTIED[u0 - 4][1]
                with pe.Fori(0, KD // 4) as it:
                    for j in range(4):
                        pe.wait_ge(dve_emptied, it * 4 + (d0 + j))
                        o = DB[(u0 + j) % 4][:, :]
                        for k in range(FF):
                            sl = s0 + 3 * j + k // 8
                            s, c = sl % SPLIT, slice(P * (k % 8), P * (k % 8) + P)
                            if k % 8 == 0:
                                pe.wait_ge(lo_done, it * 12 + (sl + 1))
                            if j == 0:
                                pe.wait_ge(g_done, FF * l + k + 1)
                            mm(o, WH[:, s, c], GH[:, k, :], start=(k == 0), stop=False)
                            mm(o, WH[:, s, c], GL[:, k, :], start=False, stop=False)
                            last = mm(o, WL[:, s, c], GH[:, k, :], start=False, stop=(k == FF - 1))
                            if k % 8 == 7 or k == FF - 1:
                                last.then_inc(slab_used, 1)
                pe.drain().then_inc(arena_free, 1)

            tail(0, lambda j: YH[:, j, :], lambda j: YL[:, j, :], 4,
                 lambda j: (hs_done, HEADS["ho5"][0] + 1) if j < HG else (o_out, j + 3))
            norm_sum(5)
            norm_spread(5)
            for k in range(3):
                feature_job(f"cq{k}", xh, xl, xready=XLB[5] if k == 0 else None)
            for k in range(2):
                feature_job(f"ckv{k}", xh, xl)
            feature_job("kpe", xh, xl)
            for k in range(3):
                head_sum("cq", 0, k)
            feature_job("qm10", xh, xl)
            head_spread("cq")
            for k in range(2):
                head_sum("ckv", 0, k)
            feature_job("qm11", xh, xl)
            head_spread("ckv")
            cq, ckv = (lambda j: CQH[:, j, :], lambda j: CQL[:, j, :]), (lambda j: CKH[:, j, :], lambda j: CKL[:, j, :])
            pe.wait_ge(hs_done, HEADS["cq"][0] + 1)
            packed_job("uqn0", [cq] * 2)
            for k in range(2):
                head_sum("qm1", k)
            packed_job("uqn1", [cq] * 2)
            for k in range(2):
                head_sum("qn", k)
            packed_job("uqn2", [cq] * 2)
            for k in range(2, 4):
                head_sum("qn", k)
            head_spread("qm10")
            head_spread("qm11")
            rotate(8, ROTM, KPR[:, :], (gain_done, 1))
            packed_job("uqr0", [cq] * 2)
            for k in range(4, 6):
                head_sum("qn", k)
            packed_job("uqr1", [cq])
            pe.drain().then_inc(arena_free, 1)
            for k in range(2):
                head_sum("qn", 2 * k, 1)
            pe.wait_ge(hs_done, HEADS["ckv"][0] + 1)
            ukn0, ukn1 = packed_tiles("ukn0", [ckv] * 4), packed_tiles("ukn1", [ckv] * 2)
            uv0, uv1 = token_tiles("uv0", *ckv, 384), token_tiles("uv1", *ckv, 384)

            def turn(k):
                rotate(9 + k, ROTM, QR[:, k, :], (hs_done, HEADS[f"qn{2 * k + 1}"][0] + 1))

            def key_sums(*heads):
                for h in heads:
                    head_sum("kn", h)

            next(ukn0)
            head_sum("qn", 4, 1)
            for _ in ukn0:
                pass
            pe.wait_ge(hs_std, HEADS["qn5"][0] + 1)
            pe.wait_ge(kpe_sq, 1)
            sum_cols(SC[0][:, 72:76], PB[:, 2, :], BONES[:, 0:1]).then_inc(kpe_ss, 1)
            next(ukn1)
            head_spread("qn0")
            next(ukn1)
            head_spread("qn1")
            key_sums(0, 1)
            next(uv0)
            head_spread("qn2")
            key_sums(2)
            next(uv0)
            head_spread("qn3")
            turn(0)
            key_sums(3)
            next(uv1)
            head_spread("qn4")
            key_sums(4, 5)
            turn(1)
            next(uv1)
            head_spread("qn5")
            turn(2)
            for h in range(MLH):
                head_spread(f"kn{h}")
            for job in (ukn1, uv0, uv1):
                next(job, None)
            pe.wait_ge(roped, 12)
            pe.wait_ge(hs_done, HEADS["kn5"][0] + 1)
            pe.wait_ge(*emptied("uv1"))
            attention(segments["l"])
            attention(segments["m1"])
            tail(1, lambda j: YH1[:, j, :], lambda j: YL1[:, j, :], 6, lambda j: (o_out, j + 11))

        @block.scalar
        def _(act):
            A = nc.scalar.activation

            split_next = [0]

            def high(n, turn=0, turns=0):
                if n >= SPLIT:
                    act.wait_ge(slab_used, turn * turns + (n - SPLIT + 1))
                act.wait_ge(raw_in[n % RING], turn * (16 * turns // RING) + 16 * (n // RING + 1))
                A(WH[:, n % SPLIT, :], RAW[:, n % RING, :], ACT.Copy).then_inc(hi_done, 1)

            def split_past(name):
                while split_next[0] < JOBS[name].done + SPLIT:
                    high(split_next[0])
                    split_next[0] += 1

            def job_ready(name):
                split_past(name)
                act.wait_ge(slab_used, JOBS[name].done)

            def evac(name, dst, func=ACT.Copy, t=0, width=TOK, **kw):
                job_ready(name)
                A(dst, DB[JOBS[name].banks[t] % 4][:, 0:width], func, **kw).then_inc(act_emptied, 1)

            def norm_squares(ni, src, ready, n=TOK, tiles=range(KD)):
                for k in tiles:
                    ready(k)
                    if k >= 3:
                        act.wait_ge(acc_done, ACC[ni] + k - 2)
                    A(SQ[:, k % 2, 0:n] if k else PB[:, 0, 0:n], src(k), ACT.Square).then_inc(sq_done, 1)

            def norm_std(ni, n=TOK):
                act.wait_ge(ss_done, ni + 1)
                if ni:
                    act.wait_ge(rs_ready, ni)
                A(NR[:, 0:n // P, 0], SC[0][:, 0:n // P], ACT.Sqrt, scale=1.0 / D, bias=col("eps")).then_inc(std_done, 1)

            def norm_high(ni, n=TOK, halves=None):
                for l, base in halves or ((0, XTB[ni]),):
                    for k in range(KD):
                        if ni == 1 and k % 4 == 3:
                            split_past(f"o1_{4 + 2 * l + k // 4}")
                        act.wait_ge(xt_done, base + k + 1)
                        A(XH[:, k, n * l:n * l + n], TMP[:, k % 2, 0:n], ACT.Copy).then_inc(xh_done, 1)

            def norm_rest(ni):
                norm_std(ni)
                norm_high(ni)

            def head_square(idx, src, n=TOK):
                if idx >= QN0 + 4:
                    act.wait_ge(hs_ss, idx - 3)
                elif idx >= QN0:
                    act.wait_ge(hs_ss, QN0)
                elif idx >= 2:
                    act.wait_ge(hs_ss, idx - 1)
                A(square_at(idx)[:, 0:n], src, ACT.Square).then_inc(hs_sq, 1)

            def group_std(group, scale, eps):
                g, names, m, nt = GROUPS[group]
                act.wait_ge(hs_ss, HEADS[names[-1]][1][-1] + 1)
                if group == "kn":
                    act.wait_ge(kn_sum, 1)
                if g >= 2:
                    act.wait_ge(hs_bc, HEADS[list(GROUPS.values())[g - 1][1][0]][0])
                bank_, c = SUMS_AT[group]
                n = m * nt * len(names)
                A(HR[:, g % 2, 0:n, 0], HR[:, g % 2, 0:n, 0] if group == "kn" else bank_[:, c:c + n], ACT.Sqrt, scale=scale,
                  bias=col("eps", eps)).then_inc(hs_std, len(names))

            def attention(seg, after=None):
                n = len(seg)
                for k in range(n + 2):
                    if k >= 2:
                        s = seg[k - 2]
                        g = s["g"]
                        act.wait_ge(tr_done, g + 1)
                        if g >= 2:
                            act.wait_ge(pv_done, g - 1)
                        A(PT[:, g % 2, 0:s["w"]], TB[:, 0:s["w"]], ACT.Copy).then_inc(pt_done, 1)
                    if k < n:
                        s = seg[k]
                        g = s["g"]
                        act.wait_ge(bm_done, g + 1)
                        if g >= 3:
                            act.wait_ge(tr_done, g - 2)
                        A(PB[:, g % 3, 0:s["w"]], SB[:, g % 2, 0:s["w"]], ACT.Exp, scale=-1.0,
                          bias=ST[:, g % 4:g % 4 + 1], accum_out=ST[:, 8 + g % 4:9 + g % 4]).then_inc(exp_done, 1)
                        if after is not None:
                            after(s)

            for k in range(1, KD, 2):
                act.dma_start(X[:, k, :], xt_in[k]).then_inc(x_in[k], 16)
            act.dma_start(PAR[:, :], pars).then_inc(consts_in, 16)
            act.dma_start(CONST[:, :, :], consts).then_inc(consts_in, 16)
            norm_squares(0, lambda k: X[:, k, :], lambda k: act.wait_ge(x_in[k], 16))
            for n in range(SPLIT):
                high(n)
            split_next[0] = SPLIT
            act.wait_ge(consts_in, 16 * 2)
            norm_rest(0)
            act.wait_ge(lb_e, 1)
            A(LBC[:, 0:18], LBC[:, 0:18], ACT.Exp).then_inc(lb_e, 1)
            job_ready("vbiw")
            A(SQ[0:72, 1, :], DB[JOBS["vbiw"].banks[0] % 4][0:72, :], ACT.Copy).then_inc(act_emptied, 1)
            evac("iq0", IQ[:, 0, :])
            act.wait_ge(vb_turned, 1)
            turned = TB[:, :].rearrange("p (t n) -> p t n", n=P)
            A(IW[:, :, :], turned[:, :, DH:DH + IDXH], ACT.Copy, scale=float(IDXH ** -0.5 * IDXD ** -0.5))
            A(VB[:, :, :], turned[:, :, 0:DH], ACT.Copy).then_inc(vb_turned, 1)
            evac("iq1", IQ[:, 1, :])
            evac("ik", IK[:, :])
            evac("kb", KBT[:, :])
            evac("qa0", QA[:, 0, :], scale=DH ** -0.5)
            evac("qa1", QA[:, 1, :], scale=DH ** -0.5)
            n = 0
            for i in range(1, NT):
                w = P * (i + 1)
                for h in range(IDXH):
                    act.wait_ge(ilog_done, n + 1)
                    if n >= 2:
                        act.wait_ge(iacc_done, n - 1)
                    A(SB[:, n % 2, 0:w], SC[n % 2][:, 0:w], ACT.Relu).then_inc(irelu_done, 1)
                    n += 1
                    if n in (4, 8):
                        evac(f"qa{n // 4 + 1}", QA[:, n // 4 + 1, :], scale=DH ** -0.5)
                    elif n % 4 == 0:
                        evac(f"ka{n // 4 - 3}", KA[:, n // 4 - 3, :])
            act.wait_ge(roped, 4)
            for p in range(2):
                act.dma_start(TP[:, p, :, :], toep[p]).then_inc(toep_in[p], 16)
            for t in range(NT):
                evac("va", VA[:, t, :], t=t)
            for k in range(4):
                evac(f"qb{k}", QB[:, k, :], scale=DH ** -0.5)
            for k in range(4):
                evac(f"ga{k}", GA[:, k, :], ACT.Silu)
            for k in range(4):
                evac(f"gb{k}", GB[:, k, :], ACT.Silu)
            for k in range(KD):
                evac(f"za{k}", ZA[:, k, :], ACT.Sigmoid, bias=col("bm0", k))

            def next_bias(s):
                if s["kind"] == "a" and s["last"] and s["grp"] < 2:
                    act.dma_start(TP[:, s["grp"], :, :], toep[s["grp"] + 2]).then_inc(toep_in[s["grp"]], 16)

            attention(segments["ab"], next_bias)
            for k in range(KD):
                if k >= 2:
                    act.wait_ge(zb_used, k - 1)
                evac(f"zb{k}", SQ[:, k % 2, :], ACT.Sigmoid, bias=col("bm1", k))
                split_past(f"pab{k}")
            act.wait_ge(arena_free, 1)
            act.dma_start(MRAW[:, :, :], memt_in).then_inc(mem_in, 16)
            act.wait_ge(zb_used, KD)
            act.dma_start(MSKI[:, :, :], masks8).then_inc(hg_in, 16)
            act.dma_start(RESET[:, :], resets).then_inc(hg_in, 16)
            act.wait_ge(mem_in, 16)
            split_past("o1_0")
            split_past("o1_1")
            norm_squares(1, lambda k: MRAW[:, k, :], lambda k: None, MEM)
            split_past("o1_2")
            norm_std(1, MEM)
            split_past("o1_3")
            norm_high(1, MEM, ((0, XTB[1]), (1, XTB[1] + KD)))
            split_past(f"o1_{KD - 1}")
            norm_std(2)

            def mixer_squares(*tiles):
                norm_squares(3, lambda k: X[:, k, :], lambda k: act.wait_ge(x_new, k + 1), tiles=tiles)

            def memory_values(l):
                for t in range(2):
                    evac(f"mv{l}", MVT[l][:, t, :], t=t, width=MEM)

            mixer_squares(0, 1)
            evac("mk00", MKT[0][:, 0, :], width=MEM)
            mixer_squares(2, 3)
            evac("mk01", MKT[0][:, 1, :], width=MEM)
            mixer_squares(4, 5)
            memory_values(0)
            mixer_squares(6, 7)
            evac("mk10", MKT[1][:, 0, :], width=MEM)
            split_past("mk11")
            norm_std(3)
            evac("mk11", MKT[1][:, 1, :], width=MEM)
            memory_values(1)
            norm_high(3)
            for k in range(HG):
                if k == 1:
                    for a in range(4):
                        act.wait_ge(act_emptied, EMPTIED[JOBS["mv1"].banks[1]][1])
                        head_square(HEADS[f"mk{a // 2}{a % 2}"][1][0], MKT[a // 2][:, a % 2, :], MEM)
                    group_std("mk", 1.0 / DH, 0)
                job_ready(f"hf{k}")
                b = DB[JOBS[f"hf{k}"].banks[0] % 4]
                A(HB[:, k, :], b[:, :], ACT.Sigmoid)
                A(HK[:, k, :], b[:, :], ACT.Sigmoid, scale=-1.0).then_inc(act_emptied, 1)
            act.wait_ge(lb_done, 1)
            for k in range(HG):
                act.wait_ge(act_emptied, EMPTIED[JOBS[f"hf{k}"].banks[0]][1])
                A(HB[:, k, :], HB[:, k, :], ACT.Ln, scale=LBC[:, 30 + k:31 + k], bias=LBC[:, 24 + k:25 + k]).then_inc(hf_ln, 1)
            for k in range(HG):
                evac(f"hq{k}", HQ[:, k, :], ACT.Silu)
            for k in range(2):
                for t in range(NT):
                    evac(f"hv{k}", HV[:, t, 384 * k:384 * k + 384], t=t, width=384)
            sq0 = HEADS["qm00"][1][0]

            def head_out(h):
                act.wait_ge(ho_mm, h + 1)
                A(HQ[:, h, :], OB[:, :], ACT.Copy).then_inc(ho_out, 1)
                act.wait_ge(ho_out, h + 1)
                square(h + 2, HQ[:, h, :])

            def square(use, src):
                if use >= 2:
                    act.wait_ge(hs_ss, sq0 + use - 1)
                A(TMP[:, use % 2, :], src, ACT.Square).then_inc(hs_sq, 1)

            for h in range(HG):
                for l in range(7):
                    act.wait_ge(lv_e, 8 * h + l + 1)
                    A(SB[:, l % 2, :], SB[:, l % 2, :], ACT.Exp).then_inc(lv_x, 1)
                if h >= 2:
                    act.wait_ge(lv_w, 10 * (h - 1))
                act.wait_ge(lv_e, 8 * h + 8)
                A(SQ[:, h % 2, :], HB[:, h, :], ACT.Exp).then_inc(lv_x, 1)
                A(SB[:, 1, :], SB[:, 1, :], ACT.Exp).then_inc(lv_x, 1)
                if h == 0:
                    for k in range(2):
                        evac(f"qm0{k}", QM[:, k, :])
                    act.wait_ge(act_emptied, EMPTIED[JOBS["qm01"].banks[0]][1])
                    for k in range(2):
                        square(k, QM[:, k, :])
                else:
                    for k in ((0, 1), (2,), (3,), (4,), (5,))[h - 1]:
                        evac(f"hg{k}", HGT[:, k, :])
                if h:
                    head_out(h - 1)
                if h == 4:
                    act.wait_ge(act_emptied, EMPTIED[JOBS["hg4"].banks[0]][1])
                    A(HGT[:, 0:5, :], HGT[:, 0:5, :], ACT.Silu).then_inc(hg_silu, 1)
                    group_std("qm0", 1.0, 1)
            head_out(HG - 1)
            act.wait_ge(act_emptied, EMPTIED[JOBS["hg5"].banks[0]][1])
            A(HGT[:, 5, :], HGT[:, 5, :], ACT.Silu).then_inc(hg_silu, 1)
            group_std("ho", 1.0 / P, 0)
            attention(segments["m0"])

            def tail(l, ni):
                split_past(f"wo{l}{KD - 1}")
                norm_rest(ni)
                ja = JOBS[f"ua{l}_0"]
                s0, u0, base = ja.slabs[0], ja.banks[0], FF * l
                with act.Fori(0, FF // 2) as it:
                    for jj in range(2):
                        act.wait_ge(cv_g, it * 2 + (base + 2 * l + jj + 1))
                        for e, dst in ((0, SB), (1, PB)):
                            j = 2 * jj + e
                            w = CW[:, l, bass.ds(it * 2 + jj, 1), :].rearrange("p o c -> p (o c)")
                            high(s0 + j + SPLIT, it, 4)
                            act.wait_ge(slab_used, it * 4 + (s0 + j + 1))
                            A(dst[:, jj, :], DB[(u0 + j) % 4][:, :], ACT.Identity, scale=w[:, 4 * e + 2:4 * e + 3],
                              bias=w[:, 4 * e + 3:4 * e + 4]).then_inc(cv_i, 1)
                        act.wait_ge(dve_emptied, it * 4 + (EMPTIED[u0 + 2 * jj][1]))
                        A(PT[:, jj, :], SB[:, jj, :], ACT.Silu).then_inc(cv_s, 1)
                s0 = JOBS[f"dn{l}0"].slabs[0]
                with act.Fori(0, KD // 4) as it:
                    for j in range(12):
                        high(s0 + j + SPLIT, it, 12)
                split_next[0] = s0 + 3 * KD + SPLIT

            tail(0, 4)
            act.wait_ge(arena_free, 4)
            act.dma_start(POSI[:, :], pos_in.partition_broadcast(P)).then_inc(pos_ready, 16)
            norm_rest(5)
            for k in range(3):
                evac(f"cq{k}", CQ[:, k, :])
            for k in range(2):
                evac(f"ckv{k}", CKV[:, k, :])
            act.wait_ge(act_emptied, EMPTIED[JOBS["ckv1"].banks[0]][1])
            for k in range(3):
                head_square(HEADS["cq"][1][k], CQ[:, k, :])
            group_std("cq", 1.0 / 384, 0)
            evac("kpe", KPE[:, :])
            for k in range(2):
                head_square(HEADS["ckv"][1][k], CKV[:, k, :])
            evac("qm10", QM1[:, 0, :])
            group_std("ckv", 1.0 / 256, 0)
            evac("qm11", QM1[:, 1, :])
            act.wait_ge(act_emptied, EMPTIED[JOBS["qm11"].banks[0]][1])
            for k in range(2):
                head_square(HEADS[f"qm1{k}"][1][0], QM1[:, k, :])
            group_std("qm1", 1.0, 1)
            for k, t in enumerate((SINM, COSM)):
                act.wait_ge(ang_done, k + 1)
                A(t[:, :], PB[:, 2 * k, :], ACT.Sin).then_inc(sin_done, 1)
            act.wait_ge(sin_done, 2)

            def evacuated(name, t=0):
                act.wait_ge(act_emptied, EMPTIED[JOBS[name].banks[t]][1])

            for k in range(3):
                for t in range(2):
                    evac(f"uqn{k}", QN[:, 2 * k + t, :], t=t)
                evacuated(f"uqn{k}", 1)
                for h in (2 * k, 2 * k + 1):
                    head_square(HEADS[f"qn{h}"][1][0], QN[:, h, :])
            for k in range(3):
                evac(f"uqr{k // 2}", QR[:, k, :], t=k % 2)
                evacuated(f"uqr{k // 2}", k % 2)
                head_square(HEADS[f"qn{2 * k}"][1][1], QR[:, k, :])
            A(PB[:, 2, :], KPE[:, :], ACT.Square).then_inc(kpe_sq, 1)
            group_std("qn", 1.0, 2)
            for h in range(4):
                evac("ukn0", KN[:, h, :], t=h)
            evacuated("ukn0", 3)
            for h in range(2):
                head_square(HEADS[f"kn{h}"][1][0], KN[:, h, :])
            for h in range(4, 6):
                evac("ukn1", KN[:, h, :], t=h - 4)
            evacuated("ukn1", 1)
            for h in range(2, 6):
                head_square(HEADS[f"kn{h}"][1][0], KN[:, h, :])
            for k in range(2):
                for t in range(NT):
                    evac(f"uv{k}", MV[:, t, 384 * k:384 * k + 384], t=t, width=384)
            group_std("kn", 1.0 / 192, 0)
            attention(segments["l"])
            attention(segments["m1"])
            tail(1, 6)

        @block.vector
        def _(dve):
            V = nc.vector
            chain = [0]

            def link(ins):
                chain[0] += 1
                ins.then_inc(dve_chain, 1)
                dve.wait_ge(dve_chain, chain[0])

            def add_square(ni, k, n=TOK):
                dve.wait_ge(sq_done, SQB[ni] + k + 1)
                if k > 1:
                    dve.wait_ge(acc_done, ACC[ni] + k - 1)
                V.tensor_tensor(PB[:, 0, 0:n], PB[:, 0, 0:n], SQ[:, k % 2, 0:n], ALU.add).then_inc(acc_done, 1)

            def norm_root(ni, n=TOK):
                nt = n // P
                link(V.reciprocal(NR[:, 0:nt, :], NR[:, 0:nt, :]))
                V.tensor_copy(RS[:, 0:n].rearrange("p (t n) -> p t n", n=P), NR[:, 0:nt, :].broadcast_to([P, nt, P])
                              ).then_inc(rs_ready, 1)
                dve.wait_ge(rs_spread, ni + 1)

            def norm(ni, srcs, halfway=None):
                n = srcs[0][0].shape[-1]
                if ni in (0, 1):
                    for k in range(1, KD):
                        add_square(ni, k, n)
                    dve.wait_ge(consts_in, 16 * 2)
                dve.wait_ge(std_done, ni + 1)
                norm_root(ni, n)
                base = XTB[ni]
                for a in range(len(srcs) + 1):
                    if a == KD and halfway is not None:
                        halfway()
                    if a < len(srcs):
                        src, gain, _ = srcs[a]
                        if base + a >= 2:
                            dve.wait_ge(xl_done, base + a - 1)
                        V.scalar_tensor_tensor(TMP[:, a % 2, 0:n], src, gain, SC[1][:, 0:n], ALU.mult, ALU.mult).then_inc(xt_done, 1)
                    if a:
                        src, _, (k, c) = srcs[a - 1]
                        dve.wait_ge(xh_done, base + a)
                        V.tensor_tensor(XL[:, k, c], TMP[:, (a - 1) % 2, 0:n], XH[:, k, c].bitcast(F32),
                                        ALU.subtract).then_inc(xl_done, 1)

            def x_norm(ni, gain):
                norm(ni, [(X[:, k, :], col(gain, k), (k, slice(0, TOK))) for k in range(KD)])

            def split_out(hi, lo, src, signal=None):
                link(V.tensor_copy(hi, src))
                last = V.tensor_tensor(lo, src, hi.bitcast(F32), ALU.subtract)
                if signal is None:
                    link(last)
                else:
                    last.then_inc(signal, 1)

            def rope(r, x, cos, sin):
                dve.wait_ge(rot_done, r + 1)
                if r:
                    dve.wait_ge(roped, r)
                link(V.tensor_tensor(TMP[:, 0, :], RB[r % 2 if r < 8 else 0][:, :], sin, ALU.mult))
                link(V.tensor_tensor(x, x, cos, ALU.mult))
                V.tensor_tensor(x, x, TMP[:, 0, :], ALU.add).then_inc(roped, 1)

            def add_to_x(name, k):
                j = JOBS[name]
                dve.wait_ge(slab_used, j.done)
                V.tensor_tensor(X[:, k, :], X[:, k, :], DB[j.banks[0] % 4][:, :], ALU.add).then_inc(dve_emptied, 1)
                dve.wait_ge(dve_emptied, EMPTIED[j.banks[0]][1])
                sq = PB[:, 2, :] if k == 0 else PB[:, 1, :]
                link(V.tensor_tensor(sq, X[:, k, :], X[:, k, :], ALU.mult))
                if k:
                    last = V.tensor_tensor(PB[:, 2, :], PB[:, 2, :], sq, ALU.add)
                    link(last) if k < KD - 1 else last.then_inc(acc_done, 1)

            def group_roots(group):
                g, names, m, nt = GROUPS[group]
                dve.wait_ge(hs_std, HEADS[names[-1]][0] + 1)
                n = m * nt * len(names)
                link(V.reciprocal(HR[:, g % 2, 0:n, 0], HR[:, g % 2, 0:n, 0]))

            def head_copy(group, a, dst=None):
                g, names, m, nt = GROUPS[group]
                q = HEADS[names[a]][0]
                if dst is None:
                    dst = RH[q % 2]
                    if q >= 2:
                        dve.wait_ge(hs_rb, q - 1)
                w = m * nt
                c = slice(w * a, w * a + w)
                if group == "qn":
                    c = slice(8 * (a // 2) + a % 2, 8 * (a // 2) + 8, 2)
                V.tensor_copy(dst[:, 0:P * nt].rearrange("p (t n) -> p t n", n=P // m),
                              HR[:, g % 2, c, :].broadcast_to([P, w, P // m])).then_inc(hs_bc, 1)

            def head_root(name, n=TOK):
                q = HEADS[name][0]
                dve.wait_ge(hs_rb, q + 1)
                return (SC[1], OB)[q % 2][:, 0:n]

            def group_out(s):
                dve.wait_ge(pv_done, s["g"] + 1)
                p, src = s["grp"], s["bank"][:, :]
                if s["kind"] in "ab":
                    gate, hi, lo = (GA, YAH, YAL) if s["kind"] == "a" else (GB, YBH, YBL)
                    t = p
                    link(V.tensor_tensor(TMP[:, 0, :], src, gate[:, p, :], ALU.mult))
                    src = TMP[:, 0, :]
                    yield
                else:
                    hi, lo, t = {"m0": (YH, YL, 6 + p), "m1": (YH1, YL1, 6 + p), "l": (YH1, YL1, p)}[s["kind"]]
                link(V.tensor_copy(hi[:, t, :], src))
                yield
                V.tensor_tensor(lo[:, t, :], src, hi[:, t, :].bitcast(F32), ALU.subtract).then_inc(o_out, 1)
                if src is not s["bank"]:
                    dve.wait_ge(o_out, s["group"] + 1)

            def attention(seg, beside=None):
                n, leaving = len(seg), []
                for k in range(n + 4):
                    for _ in range(2 if beside is not None and k >= 2 else 0):
                        next(beside, None)
                    if k < n:
                        s = seg[k]
                        g = s["g"]
                        if s["kind"] == "a" and s["first"]:
                            dve.wait_ge(toep_in[s["grp"] % 2], 16 * (1 + s["grp"] // 2))
                        dve.wait_ge(qk_done, g + 1)
                        if g >= 2:
                            dve.wait_ge(exp_done, g - 1)
                        V.tensor_tensor_reduce(out=SB[:, g % 2, 0:s["w"]], in0=SC[g % 2][:, 0:s["w"]], in1=s["bias"],
                                               scale=-1.0, scalar=3.0e38, op0=ALU.add, op1=ALU.min,
                                               accum_out=ST[:, g % 4:g % 4 + 1]).then_inc(bm_done, 1)
                    if 1 <= k <= n:
                        s = seg[k - 1]
                        g = s["g"]
                        dve.wait_ge(exp_done, g + 1)
                        link(V.reciprocal(ST[:, 16 + g % 4:17 + g % 4], ST[:, 8 + g % 4:9 + g % 4]))
                        V.tensor_scalar(PB[:, g % 3, 0:s["w"]], PB[:, g % 3, 0:s["w"]], ST[:, 16 + g % 4:17 + g % 4],
                                        None, ALU.mult).then_inc(nrm_done, 1)
                    if k >= 4 and seg[k - 4]["last"]:
                        leaving.append(group_out(seg[k - 4]))
                    while leaving and seg[0]["kind"][0] == "m" and next(leaving[0], "left") != "left":
                        pass
                    if leaving and next(leaving[0], "left") == "left":
                        leaving.pop(0)
                for group in leaving:
                    for _ in group:
                        pass
                dve.wait_ge(tr_done, seg[-1]["g"] + 1)

            x_norm(0, "norm_gain")
            c0 = COLS["lb"][0]
            lg = [PAR[:, c0 + HG * j:c0 + HG * j + HG] for j in range(3)]
            mx, lb, om = LBC[:, 18:24], LBC[:, 24:30], LBC[:, 30:36]
            link(V.tensor_tensor(mx, lg[0], lg[1], ALU.max))
            link(V.tensor_tensor(mx, mx, lg[2], ALU.max))
            for j in range(2):
                link(V.tensor_tensor(LBC[:, 6 * j:6 * j + 6], lg[j], mx, ALU.subtract))
            V.tensor_tensor(LBC[:, 12:18], lg[2], mx, ALU.subtract).then_inc(lb_e, 1)
            dve.wait_ge(lb_e, 2)
            link(V.tensor_tensor(mx, LBC[:, 0:6], LBC[:, 6:12], ALU.add))
            link(V.tensor_tensor(mx, mx, LBC[:, 12:18], ALU.add))
            link(V.reciprocal(mx, mx))
            link(V.tensor_tensor(lb, LBC[:, 0:6], mx, ALU.mult))
            link(V.tensor_scalar(om, lb, -1.0, 1.0, ALU.mult, ALU.add))
            V.tensor_scalar(mx, om, float(P ** -0.5), None, ALU.mult).then_inc(lb_done, 1)
            dve.wait_ge(tabs_in, 16 * 6)
            rope(0, IQ[:, 0, :], COSI[:, :], SINI[:, :])
            rope(1, IQ[:, 1, :], COSI[:, :], SINI[:, :])
            rope(2, IK[:, :], COSI[:, :], SINI[:, :])
            rope(3, KBT[:, :], COSB[:, :], SINB[:, :])
            n, off = 0, 0
            for i in range(1, NT):
                w = P * (i + 1)
                sc = MB[:, off:off + w]
                for h in range(IDXH):
                    dve.wait_ge(irelu_done, n + 1)
                    wt = IW[:, i, h:h + 1]
                    if h == 0:
                        V.tensor_scalar(sc, SB[:, n % 2, 0:w], wt, None, ALU.mult).then_inc(iacc_done, 1)
                    else:
                        dve.wait_ge(iacc_done, n)
                        V.scalar_tensor_tensor(sc, SB[:, n % 2, 0:w], wt, sc, ALU.mult, ALU.add).then_inc(iacc_done, 1)
                    n += 1
                off += w
            dve.wait_ge(iacc_done, n)
            off = 0
            for i in range(1, NT):
                w = P * (i + 1)
                sc = MB[:, off:off + w]
                link(V.memset(MB[0:CHUNK, off + w - CHUNK:off + w], BARRED))
                for _ in range(TOPK // 8):
                    link(V.max(MX8[:, :], sc))
                    link(V.match_replace(sc, MX8[:, :], sc, TAKEN))
                link(V.tensor_scalar(sc, sc, 0.5 * (TAKEN + BARRED), NEG, ALU.is_gt, ALU.mult))
                off += w
            for k in range(4):
                rope(4 + k, QB[:, k, :], COSB[:, :], SINB[:, :])
            attention(segments["ab"])
            dve.wait_ge(o_out, 8)
            for k in range(KD):
                j = JOBS[f"pab{k}"]
                dve.wait_ge(slab_used, j.done)
                V.tensor_tensor(TMP[:, 0, :], DB[j.banks[0] % 4][:, :], ZA[:, k, :], ALU.mult).then_inc(dve_emptied, 1)
                dve.wait_ge(act_emptied, EMPTIED[JOBS[f"zb{k}"].banks[0]][1])
                V.tensor_tensor(TMP[:, 1, :], DB[j.banks[1] % 4][:, :], SQ[:, k % 2, :], ALU.mult).then_inc(dve_emptied, 1)
                dve.wait_ge(dve_emptied, EMPTIED[j.banks[1]][1])
                link(V.tensor_tensor(TMP[:, 0, :], TMP[:, 0, :], TMP[:, 1, :], ALU.add))
                split_out(MH[:, k, :], ML[:, k, :], TMP[:, 0, :], zb_used)
                dve.wait_ge(zb_used, k + 1)
            add_to_x("o1_0", 0)
            add_to_x("o1_1", 1)
            norm(1, [(MRAW[:, k, :], col(f"mem{l}", k), (k, slice(MEM * l, MEM * l + MEM)))
                     for l in range(2) for k in range(KD)], lambda: [add_to_x(f"o1_{k}", k) for k in (2, 3)])
            for k in range(4, KD):
                add_to_x(f"o1_{k}", k)
            dve.wait_ge(std_done, 3)
            norm_root(2)
            for k in range(KD):
                V.scalar_tensor_tensor(X[:, k, :], X[:, k, :], col("final_gain", k), SC[1][:, :], ALU.mult, ALU.mult).then_inc(x_new, 1)
                if k >= 2:
                    add_square(3, k - 1)
            add_square(3, KD - 1)
            dve.wait_ge(arena_free, 2)
            x_norm(3, "mix0")
            group_roots("mk")
            head_copy("mk", 0)
            for l in range(2):
                for k in range(2):
                    if 2 * l + k < 3:
                        head_copy("mk", 2 * l + k + 1)
                    r = head_root(f"mk{l}{k}", MEM)
                    V.scalar_tensor_tensor(MKT[l][:, k, :], MKT[l][:, k, :], col(f"mk{l}"), r, ALU.mult, ALU.mult).then_inc(hs_done, 1)
            dve.wait_ge(hg_in, 32)
            dve.wait_ge(lb_done, 1)
            for k in range(HG):
                dve.wait_ge(hf_ln, k + 1)
                link(V.tensor_scalar(HK[:, k, :], HK[:, k, :], LBC[:, 18 + k:19 + k], None, ALU.mult))
                link(V.tensor_tensor_scan(HB[:, k, :], RESET[:, :], HB[:, k, :], 0.0, ALU.mult, ALU.add))
            V.drain().then_inc(decays_ready, 1)
            link(V.memset(PT[:, :, :], 0.0))
            link(V.tensor_copy(MSK[:, :, :], MSKI[:, :, :]))
            dve.wait_ge(act_emptied, EMPTIED[JOBS["hq5"].banks[0]][1])
            def query_norm(k):
                r = DB[(JOBS["hg5"].banks[0] + k + 1) % 4][:, :]
                dve.wait_ge(hs_rb, HEADS[f"qm0{k}"][0] + 1)
                V.scalar_tensor_tensor(QM[:, k, :], QM[:, k, :], col("mq0"), r, ALU.mult, ALU.mult).then_inc(hs_done, 1)

            for h in range(HG):
                if h == HG - 1:
                    group_roots("qm0")
                    for k in range(2):
                        head_copy("qm0", k, (RS, RESET)[HEADS[f"qm0{k}"][0] % 2])
                b, q_, k_ = HB[:, h, :], HQ[:, h, :], HK[:, h, :]

                def weigh(l):
                    n = 10 * h + l
                    e = SB[:, l % 2, :]
                    if l < 7:
                        dve.wait_ge(lv_x, 9 * h + l + 1)
                        if n >= 3:
                            dve.wait_ge(lv_mm, n - 2)
                        m = LEVELS[l]

                        def v(a):
                            return a.rearrange("p (n s m) -> p n s m", s=2, m=m)

                        o = v(PB[:, n % 3, :])
                        V.tensor_tensor(o[:, :, 1, :], v(q_)[:, :, 1, :], v(e)[:, :, 1, :], ALU.mult)
                        V.tensor_tensor(o[:, :, 0, :], v(k_)[:, :, 0, :], v(e)[:, :, 0, :], ALU.mult).then_inc(lv_w, 1)
                    else:
                        dve.wait_ge(lv_x, 9 * h + 9)
                        if h:
                            dve.wait_ge(lv_mm, 10 * h)
                        eb = SQ[:, h % 2, :]
                        V.tensor_tensor(QX[:, :], q_, eb, ALU.mult).then_inc(lv_w, 1)
                        link(V.tensor_tensor(KX[:, :], k_, e, ALU.mult))
                        link(V.tensor_scalar(KX2[:, 1, :], KX[:, P:2 * P], eb[:, 3 * P - 1:3 * P], None, ALU.mult))
                        V.tensor_scalar(KX2[:, 0, :], KX[:, 0:P], eb[:, 2 * P - 1:2 * P], None, ALU.mult).then_inc(lv_w, 1)
                        dve.wait_ge(lv_w, 10 * h + 9)
                        V.tensor_scalar(KX2[:, 2, :], KX2[:, 0, :], eb[:, 3 * P - 1:3 * P], None, ALU.mult).then_inc(lv_w, 1)

                def place(l):
                    n = 10 * h + l
                    dve.wait_ge(lv_mm, n + 1)
                    if n:
                        dve.wait_ge(lv_cp, n)
                    if l == 0 and h >= 2:
                        dve.wait_ge(ho_mm, h - 1)
                    if l == 8 and h:
                        dve.wait_ge(ho_mm, h)
                    s = SC[n % 2]
                    if l < 8:
                        V.copy_predicated(PT[:, h % 2, :].rearrange("p (t n) -> p t n", t=NT),
                                          MSK[:, l:l + 1, :].broadcast_to([P, NT, P]),
                                          s[:, :].rearrange("p (t n) -> p t n", t=NT)).then_inc(lv_cp, 1)
                    else:
                        a, b_ = (0, 4) if l == 8 else (4, 6)
                        V.tensor_copy(AX[:, a:b_, :].rearrange("p t n -> p (t n)"), s[:, 0:P * (b_ - a)]).then_inc(lv_cp, 1)

                for t in range(10):
                    if 1 <= t <= 8:
                        weigh(t - 1)
                    if t >= 2:
                        place(t - 2)
                place(8)
                place(9)

            def head_outputs():
                dve.wait_ge(hg_silu, 2)
                group_roots("ho")
                for h in range(HG):
                    head_copy("ho", h, HB[:, h, :])
                    yield
                for h in range(HG):
                    dve.wait_ge(hs_rb, HEADS[f"ho{h}"][0] + 1)
                    r = DB[h % 4][:, :]
                    link(V.scalar_tensor_tensor(TMP[:, 0, :], HQ[:, h, :], col("onorm"), r, ALU.mult, ALU.mult))
                    yield
                    link(V.tensor_tensor(TMP[:, 1, :], TMP[:, 0, :], HGT[:, h, :], ALU.mult))
                    yield
                    link(V.tensor_copy(YH[:, h, :], TMP[:, 1, :]))
                    yield
                    V.tensor_tensor(YL[:, h, :], TMP[:, 1, :], YH[:, h, :].bitcast(F32), ALU.subtract).then_inc(hs_done, 1)
                    dve.wait_ge(hs_done, HEADS[f"ho{h}"][0] + 1)
                    yield

            for k in range(2):
                query_norm(k)
            attention(segments["m0"], head_outputs())

            def tail(l, ni, gain):
                for k in range(KD):
                    add_to_x(f"wo{l}{k}", k)
                dve.wait_ge(arena_free, {0: 3, 1: 6}[l])
                x_norm(ni, gain)
                ja = JOBS[f"ua{l}_0"]
                u0, base, c0 = ja.banks[0], FF * l, chain[0]
                d0 = EMPTIED[u0][1]
                V.drain().then_inc(cv_g, 2)
                with dve.Fori(0, FF // 2) as it:
                    for jj in range(2):
                        pair = it * 2 + (base + jj)
                        for e, dst in ((0, SB), (1, PB)):
                            j = 2 * jj + e
                            y, u = dst[:, jj, :], DB[(u0 + j) % 4]
                            w = CW[:, l, bass.ds(it * 2 + jj, 1), :].rearrange("p o c -> p (o c)")
                            dve.wait_ge(cv_i, it * 4 + (2 * base + j + 1))
                            V.scalar_tensor_tensor(y[:, 1:TOK], u[:, 0:TOK - 1], w[:, 4 * e + 1:4 * e + 2], y[:, 1:TOK],
                                                   ALU.mult, ALU.add).then_inc(dve_chain, 1)
                            dve.wait_ge(dve_chain, it * 6 + (c0 + 3 * jj + e + 1))
                            V.scalar_tensor_tensor(y[:, 2:TOK], u[:, 0:TOK - 2], w[:, 4 * e:4 * e + 1], y[:, 2:TOK],
                                                   ALU.mult, ALU.add).then_inc(dve_emptied, 1)
                        dve.wait_ge(dve_emptied, it * 4 + (d0 + 2 * jj + 1))
                        dve.wait_ge(cv_s, pair + 1)
                        V.tensor_tensor(TMP[:, jj, :], PT[:, jj, :], PB[:, jj, :], ALU.mult).then_inc(cv_g, 1)
                        dve.wait_ge(cv_g, pair + (2 * l + 3))
                        gh = GH[:, bass.ds(it * 2 + jj, 1), :].rearrange("p o n -> p (o n)")
                        gl = GL[:, bass.ds(it * 2 + jj, 1), :].rearrange("p o n -> p (o n)")
                        V.tensor_copy(gh, TMP[:, jj, :]).then_inc(dve_chain, 1)
                        dve.wait_ge(dve_chain, it * 6 + (c0 + 3 * jj + 3))
                        V.tensor_tensor(gl, TMP[:, jj, :], gh.bitcast(F32), ALU.subtract).then_inc(g_done, 1)
                chain[0] = c0 + 6 * (FF // 2)
                jd = JOBS[f"dn{l}0"]
                s0, u0, c1 = jd.slabs[0], jd.banks[0], chain[0] + 1
                link(V.memset(PB[:, 2, :], 0.0))
                with dve.Fori(0, KD // 4) as it:
                    for j in range(4):
                        dve.wait_ge(slab_used, it * 12 + (s0 + 3 * j + 3))
                        x = X[:, bass.ds(it * 4 + j, 1), :].rearrange("p o n -> p (o n)")
                        V.tensor_tensor(x, x, DB[(u0 + j) % 4][:, :], ALU.add).then_inc(dve_emptied, 1)
                        if l == 0:
                            dve.wait_ge(dve_emptied, it * 4 + EMPTIED[u0 + j][1])
                            V.tensor_tensor(PB[:, 1, :], x, x, ALU.mult).then_inc(dve_chain, 1)
                            dve.wait_ge(dve_chain, it * 8 + (c1 + 2 * j + 1))
                            V.tensor_tensor(PB[:, 2, :], PB[:, 2, :], PB[:, 1, :], ALU.add).then_inc(dve_chain, 1)
                            dve.wait_ge(dve_chain, it * 8 + (c1 + 2 * j + 2))
                if l == 0:
                    chain[0] += 2 * KD
                    V.drain().then_inc(acc_done, 1)

            tail(0, 4, "ffn0")
            x_norm(5, "mix1")
            ang, turns, arg = PB[:, 0, :], PB[:, 1, :], PB[:, 2, :]
            dve.wait_ge(pos_ready, 16)
            link(V.tensor_copy(PT[:, 0, :], POSI[:, :]))
            link(V.tensor_scalar(PT[:, 1, :], PT[:, 0, :], col("inv"), None, ALU.mult))
            ang = PT[:, 1, :]
            for i, (dst, quarter) in enumerate(((PB[:, 0, :], 0.0), (PB[:, 2, :], 0.25))):
                link(V.tensor_scalar(turns, ang, float(1 / (2 * np.pi)), quarter, ALU.mult, ALU.add))
                link(V.tensor_scalar(turns, turns, ROUND, ROUND, ALU.add, ALU.subtract))
                link(V.scalar_tensor_tensor(dst, turns, -TURN[0], ang, ALU.mult, ALU.add))
                link(V.scalar_tensor_tensor(dst, turns, -TURN[1], dst, ALU.mult, ALU.add))
                link(V.scalar_tensor_tensor(dst, turns, -TURN[2], dst, ALU.mult, ALU.add))
                link(V.tensor_scalar(dst, dst, float(2 * np.pi * quarter), HALFTURN, ALU.add, ALU.min))
                V.tensor_scalar(dst, dst, -HALFTURN, None, ALU.max).then_inc(ang_done, 1)
            group_roots("cq")
            head_copy("cq", 0)
            r = head_root("cq")
            for k in range(3):
                link(V.scalar_tensor_tensor(TMP[:, 0, :], CQ[:, k, :], col("qa", k), r, ALU.mult, ALU.mult))
                split_out(CQH[:, k, :], CQL[:, k, :], TMP[:, 0, :], hs_done if k == 2 else None)
            dve.wait_ge(hs_done, HEADS["cq"][0] + 1)
            group_roots("ckv")
            head_copy("ckv", 0)
            r = head_root("ckv")
            for k in range(2):
                link(V.scalar_tensor_tensor(TMP[:, 0, :], CKV[:, k, :], col("kva", k), r, ALU.mult, ALU.mult))
                split_out(CKH[:, k, :], CKL[:, k, :], TMP[:, 0, :], hs_done if k == 1 else None)
            dve.wait_ge(hs_done, HEADS["ckv"][0] + 1)
            dve.wait_ge(act_emptied, EMPTIED[JOBS["kpe"].banks[0]][1])
            V.tensor_scalar(KPR[:, :], KPE[:, :], col("kn", 1), None, ALU.mult).then_inc(gain_done, 1)
            group_roots("qm1")
            for k in range(2):
                head_copy("qm1", k)
            for k in range(2):
                r = head_root(f"qm1{k}")
                V.scalar_tensor_tensor(QM1[:, k, :], QM1[:, k, :], col("mq1"), r, ALU.mult, ALU.mult).then_inc(hs_done, 1)
            dve.wait_ge(sin_done, 2)
            rope(8, KPR[:, :], COSM[:, :], SINM[:, :])
            dve.wait_ge(roped, 9)
            group_roots("qn")
            head_copy("qn", 0)
            for h in range(MLH):
                if h < MLH - 1:
                    head_copy("qn", h + 1)
                r, half = head_root(f"qn{h}"), HALF[h % 2]
                link(V.scalar_tensor_tensor(QN[:, h, :], QN[:, h, :], col("qn"), r, ALU.mult, ALU.mult))
                V.scalar_tensor_tensor(QR[half, h // 2, :], QR[half, h // 2, :], col("qn", 1)[half], r[half], ALU.mult,
                                       ALU.mult).then_inc(hs_done, 1)
                if h == 4:
                    dve.wait_ge(kpe_ss, 1)
                    dve.wait_ge(hs_ss, HEADS["kn5"][1][0] + 1)
                    g, c = GROUPS["kn"][0], SUMS_AT["kn"][1]
                    link(V.tensor_copy(KS[:, 0, :], SC[0][:, 72:76]))
                    V.tensor_tensor(HR[:, g % 2, 0:24, 0].rearrange("p (h t) -> p h t", t=NT),
                                    SC[0][:, c:c + 24].rearrange("p (h t) -> p h t", t=NT),
                                    KS[:, :, :].broadcast_to([P, MLH, NT]), ALU.add).then_inc(kn_sum, 1)
                if h >= 3:
                    k = h - 3
                    rope(9 + k, QR[:, k, :], COSM[:, :], SINM[:, :])
            group_roots("kn")
            head_copy("kn", 0)
            for h in range(MLH):
                if h < MLH - 1:
                    head_copy("kn", h + 1)
                r, half = head_root(f"kn{h}"), HALF[h % 2]
                link(V.scalar_tensor_tensor(KN[:, h, :], KN[:, h, :], col("kn"), r, ALU.mult, ALU.mult))
                V.tensor_tensor(KR[half, h // 2, :], KPR[half, :], r[half], ALU.mult).then_inc(hs_done, 1)
            attention(segments["l"])
            attention(segments["m1"])
            tail(1, 6, "ffn1")


def host_layout(inputs):
    f = {k: np.asarray(v) for k, v in inputs.items()}
    w_in, hgw, mlw = f["w_in"][0], f["hg_w_in_2"][0], f["mla_w_in_2"][0]
    sizes = (512, 512, 512, 512, 512, 64, 64, 512, 256, 32, 8, 1024, 1024)
    o = np.concatenate([[0], np.cumsum(sizes)])
    qa, ka, va, ga, qb, kb, vb, gb, iq, ik, iw, za, zb = (w_in[:, o[i]:o[i + 1]] for i in range(13))
    stream = np.zeros((NSLAB, P, SLAB), np.float32)

    def tiles(w):
        return w.reshape(-1, P, w.shape[1]).transpose(1, 0, 2)

    def feature(name, w):
        t = tiles(w)
        for a, n in enumerate(JOBS[name].slabs):
            part = t[:, 8 * a:8 * a + 8, :]
            stream[n, :, :part.shape[1] * P] = part.reshape(P, -1)

    def packed(name, ws):
        stream[JOBS[name].slabs[0], :, :P * JOBS[name].kts * len(ws)] = np.concatenate(
            [tiles(w) for w in ws], 1).reshape(P, -1)

    def token(name, w):
        t, slabs = tiles(w), JOBS[name].slabs
        per = t.shape[1] // len(slabs)
        for a, n in enumerate(slabs):
            part = t[:, per * a:per * a + per, :]
            stream[n, :, :per * w.shape[1]] = part.reshape(P, -1)

    def c(w, k):
        return w[:, P * k:P * k + P]

    feature("vbiw", np.concatenate([vb, iw, np.zeros((D, P - DH - IDXH), np.float32)], 1))
    feature("iq0", c(iq, 0))
    feature("iq1", c(iq, 1))
    feature("ik", np.concatenate([ik] * 4, 1))
    feature("kb", np.concatenate([kb] * 2, 1))
    for name, w in (("qa", qa), ("ka", ka), ("qb", qb), ("ga", ga), ("gb", gb)):
        for k in range(4):
            feature(f"{name}{k}", c(w, k))
    token("va", va)
    for k in range(KD):
        feature(f"za{k}", c(za, k))
        feature(f"zb{k}", c(zb, k))
        packed(f"pab{k}", [c(f["w_branch_a"][0], k), c(f["w_branch_b"][0], k)])
        feature(f"o1_{k}", c(f["w_out"][0], k))
        for l in range(2):
            feature(f"wo{l}{k}", c(f["w_out_2"][l], k))
            feature(f"dn{l}{k}", c(f["w_down_2"][l], k))
    for l in range(2):
        kv = f["w_mem_kv_2"][l]
        for k in range(2):
            feature(f"mk{l}{k}", c(kv, k))
        token(f"mv{l}", kv[:, 256:])
        for k in range(FF):
            feature(f"ua{l}_{k}", c(f["w_up_2"][l], k))
            feature(f"ub{l}_{k}", c(f["w_up_2"][l], FF + k))
    for k in range(HG):
        feature(f"hq{k}", c(hgw, k))
        feature(f"hf{k}", c(hgw, HG + k))
        feature(f"hg{k}", c(hgw, 3 * HG + k))
    for k in range(2):
        token(f"hv{k}", hgw[:, 1536 + 384 * k:1920 + 384 * k])
        feature(f"qm0{k}", hgw[:, 3072 + P * k:3200 + P * k])
        feature(f"qm1{k}", mlw[:, 704 + P * k:832 + P * k])
        feature(f"ckv{k}", mlw[:, 384 + P * k:512 + P * k])
    for k in range(3):
        feature(f"cq{k}", c(mlw, k))
    feature("kpe", np.concatenate([mlw[:, 640:704]] * 2, 1))
    uq = f["mla_w_uq_2"][0].reshape(384, MLH, 192)
    ukv = f["mla_w_ukv_2"][0].reshape(256, MLH, 256)
    uqr = [uq[:, 2 * k:2 * k + 2, P:].reshape(384, P) for k in range(3)]
    for k in range(3):
        packed(f"uqn{k}", [uq[:, h, :P] for h in (2 * k, 2 * k + 1)])
    packed("uqr0", uqr[:2])
    packed("uqr1", uqr[2:])
    packed("ukn0", [ukv[:, h, :P] for h in range(4)])
    packed("ukn1", [ukv[:, h, :P] for h in range(4, MLH)])
    for k in range(2):
        token(f"uv{k}", ukv[:, 3 * k:3 * k + 3, P:].reshape(256, 384))

    def cols(v):
        return v.reshape(-1, P).T

    inv_m = (np.float32(10000.0) ** (-np.arange(32, dtype=np.float32) / np.float32(32))).astype(np.float32)
    pars = np.zeros((P, NCOL), np.float32)
    qn, kn = f["mla_q_norm_g_2"][0], f["mla_k_norm_g_2"][0]
    for name, v in (("norm_gain", cols(f["norm_gain"][0])), ("final_gain", cols(f["final_norm_gain"])),
                    ("mix0", cols(f["mix_norm_g_2"][0])), ("mix1", cols(f["mix_norm_g_2"][1])),
                    ("ffn0", cols(f["ffn_norm_g_2"][0])), ("ffn1", cols(f["ffn_norm_g_2"][1])),
                    ("mem0", cols(f["mem_norm_g_2"][0])), ("mem1", cols(f["mem_norm_g_2"][1])),
                    ("bm0", cols(f["b_merge"][0, 0])), ("bm1", cols(f["b_merge"][0, 1])),
                    ("mq0", cols(np.tile(f["mem_q_norm_g_2"][0], 2))), ("mq1", cols(np.tile(f["mem_q_norm_g_2"][1], 2))),
                    ("mk0", cols(np.tile(f["mem_k_norm_g_2"][0], 2))), ("mk1", cols(np.tile(f["mem_k_norm_g_2"][1], 2))),
                    ("lb", cols(f["hg_lb_logits_2"])), ("onorm", cols(f["hg_out_norm_g_2"][0])),
                    ("qa", cols(f["mla_qa_norm_g_2"][0])), ("kva", cols(f["mla_kva_norm_g_2"][0])),
                    ("qn", cols(np.concatenate([qn[:P], qn[P:], qn[P:]]))),
                    ("kn", cols(np.concatenate([kn[:P], kn[P:], kn[P:]]))),
                    ("inv", cols(np.tile(inv_m, 4))),
                    ("eps", np.tile(np.array([EPS, DH * EPS, 192 * EPS], np.float32), (P, 1)))):
        pars[:, COLS[name][0]:COLS[name][0] + COLS[name][1]] = v
    convp = np.zeros((P, 2, FF, 8), np.float32)
    for l in range(2):
        for half in range(2):
            for tap in range(3):
                convp[:, l, :, 4 * half + tap] = cols(f["conv_w_2"][l, tap, 2816 * half:2816 * half + 2816])
            convp[:, l, :, 4 * half + 3] = cols(f["conv_b_2"][l, 2816 * half:2816 * half + 2816])

    def rotation(head, rot):
        m, half = np.zeros((P, P), np.float32), rot // 2
        for b in range(0, P, head):
            for j in range(half):
                m[b + half + j, b + j] = -1.0
                m[b + j, b + half + j] = 1.0
        return m

    part, free = np.arange(P)[:, None], np.arange(P)[None, :]
    chb = np.where((part < CHUNK) & (free >= CHUNK), np.float32(NEG), np.float32(0))
    consts = np.stack([np.eye(P, dtype=np.float32), np.ones((P, P), np.float32),
                       (part // DH == free // DH).astype(np.float32), rotation(DH, 16), rotation(IDXD, 8),
                       rotation(DH, 64), chb], 1).astype(np.float32)

    def rope_table(head, rot):
        half = rot // 2
        inv = (np.float32(500000.0) ** (-np.arange(half, dtype=np.float32) / np.float32(half))).astype(np.float32)
        ang = (np.arange(TOK, dtype=np.float32)[None, :] * inv[:, None]).astype(np.float64)
        c_, s_ = np.ones((P, TOK), np.float32), np.zeros((P, TOK), np.float32)
        for b in range(0, P, head):
            for a in range(2):
                c_[b + half * a:b + half * a + half] = np.cos(ang)
                s_[b + half * a:b + half * a + half] = np.sin(ang)
        return c_, s_

    rope_tabs = np.stack([*rope_table(IDXD, 8), *rope_table(DH, 16)])
    c_ = np.arange(TOK)[None, :]
    at_ = 256 + np.minimum(part - c_ + TOK - P, 256)
    toep = f["rel_bias"][0][:, at_].reshape(4, 2, P, TOK).transpose(0, 2, 1, 3).copy()
    toep[:, :CHUNK, :, TOK - CHUNK:] = NEG
    s_, t_ = part, free
    levels = [(s_ // (2 * m) == t_ // (2 * m)) & (s_ // m % 2 == 0) & (t_ // m % 2 == 1) for m in LEVELS]
    masks8 = np.stack(levels + [s_ == t_], 1).astype(np.int32)
    resets = np.tile((np.arange(TOK) % P != 0).astype(np.float32), (P, 1))
    cz = np.where(c_ - (TOK - P) <= part, np.float32(0), np.float32(NEG)).astype(np.float32)
    xt = np.ascontiguousarray(f["x"][0].T).reshape(KD, P, TOK)
    memt = np.ascontiguousarray(f["mem_2"][0].T.reshape(KD, P, MEM).transpose(1, 0, 2))
    return dict(stream=stream, xt=xt, memt=memt, pars=pars, convp=convp, consts=consts, rope=rope_tabs,
                toep=toep, masks8=masks8, resets=resets, cz=cz, pos=f["positions_2"][0].astype(np.int32))


def kernel(**inputs):
    import concourse.bacc as _bacc
    from concourse.bass_utils import run_bass_kernel_spmd as _run

    nc = _bacc.Bacc("TRN2", target_bir_lowering=False, num_devices=1)
    arrays, args = {}, []
    for name, a in host_layout(inputs).items():
        a = np.ascontiguousarray(a)
        arrays[f"in_{name}_dram"] = a
        args.append(nc.dram_tensor(f"in_{name}_dram", a.shape, mybir.dt.from_np(a.dtype), kind="ExternalInput").ap())
    out = nc.dram_tensor("out_dram", (KD, P, TOK), F32, kind="ExternalOutput").ap()
    build(nc, *args, out)
    r = _run(nc, [arrays], core_ids=[0])
    got = r.results[0]["out_dram"]
    return got.reshape(1, D, TOK).transpose(0, 2, 1)
```
